# Optimizing a Trainium2 kernel written in Bass

```python
import math
import jax, jax.numpy as jnp
from jax import lax
import numpy as np

D_MODEL = 1024
BATCH = 1
SEQ = 512
DEPTH = 1

D_MIX = D_MODEL
D_LRU = D_MIX // 2
LRU_HEADS = 8
LRU_HEAD_DIM = D_LRU // LRU_HEADS
CONV_WIDTH = 4
LRU_C = 8.0
D_FOURIER = D_MIX - D_LRU
FOURIER_GROUPS = 4
FOURIER_GROUP_DIM = D_FOURIER // FOURIER_GROUPS
D_IN_PROJ = 2 * D_LRU + D_FOURIER
N_EXPERTS = 16
CAPACITY_FACTOR = 2
D_FF_EXPERT = 2 * D_MODEL
EPS = 1e-6


def rmsnorm(x, g):
    xf = x.astype(jnp.float32)
    y = xf * lax.rsqrt(jnp.mean(xf * xf, axis=-1, keepdims=True) + EPS)
    return (y * g.astype(jnp.float32)).astype(x.dtype)

def centred_depthwise_conv(u, w, b):
    s = u.shape[1]
    left = CONV_WIDTH // 2
    right = CONV_WIDTH - 1 - left
    up = jnp.pad(u, ((0, 0), (left, right), (0, 0)))
    out = b
    for k in range(CONV_WIDTH):
        out = out + w[k] * up[:, k:k + s, :]
    return out

def _linear_recurrence_combine(left, right):
    a1, b1 = left
    a2, b2 = right
    return a1 * a2, a2 * b1 + b2

def rglru(u, w_a, b_a, w_x, b_x, lam, reverse):
    bsz, s, _ = u.shape
    uf = u.astype(jnp.float32)
    uh = uf.reshape(bsz, s, LRU_HEADS, LRU_HEAD_DIM)
    r = jax.nn.sigmoid(jnp.einsum('bshi,hij->bshj', uh, w_a.astype(jnp.float32)).reshape(bsz, s, D_LRU) + b_a)
    i = jax.nn.sigmoid(jnp.einsum('bshi,hij->bshj', uh, w_x.astype(jnp.float32)).reshape(bsz, s, D_LRU) + b_x)
    log_a = LRU_C * r * jax.nn.log_sigmoid(lam.astype(jnp.float32))
    a = jnp.exp(log_a)
    mult = jnp.sqrt(-jnp.expm1(2.0 * log_a))
    bterm = mult * (i * uf)
    _, h = lax.associative_scan(_linear_recurrence_combine, (a, bterm), axis=1, reverse=reverse)
    return h

def fourier_mix(u):
    bsz, s, _ = u.shape
    f = u.astype(jnp.float32).reshape(bsz, s, FOURIER_GROUPS, FOURIER_GROUP_DIM)
    y = jnp.fft.fft2(f, axes=(1, 3), norm='ortho').real
    return y.reshape(bsz, s, D_FOURIER)

def expert_choice_moe(h, w_router, w_gate, w_up, w_down):
    bsz, s, d = h.shape
    cap = CAPACITY_FACTOR * s // N_EXPERTS
    logits = jnp.einsum('bsd,de->bse', h.astype(jnp.float32), w_router.astype(jnp.float32))
    aff = jax.nn.softmax(logits, axis=-1)
    scores = jnp.transpose(aff, (0, 2, 1))
    gate, idx = lax.top_k(scores, cap)
    bidx = jnp.arange(bsz)[:, None, None]
    xin = h[bidx, idx]
    g = jnp.einsum('becd,edf->becf', xin, w_gate)
    u = jnp.einsum('becd,edf->becf', xin, w_up)
    eo = jnp.einsum('becf,efd->becd', jax.nn.silu(g) * u, w_down)
    contrib = gate.astype(eo.dtype)[..., None] * eo
    out = jnp.zeros((bsz, s, d), dtype=eo.dtype).at[bidx, idx].add(contrib)
    return out

def first_inputs(seed: int = 0) -> dict:
    key = jax.random.key(seed)
    ks = jax.random.split(key, 24)
    f32 = jnp.float32
    nrm = lambda k, shape, scale: jax.random.normal(k, shape, f32) * scale

    def lam_init(k):
        u = jax.random.uniform(k, (D_LRU,), f32, 0.9, 0.999)
        return jnp.log(u) - jnp.log1p(-u)

    return {
        "x": nrm(ks[0], (BATCH, SEQ, D_MODEL), 1.0),
        "norm1_g": 1.0 + nrm(ks[1], (D_MODEL,), 0.02),
        "w_in": nrm(ks[2], (D_MODEL, D_IN_PROJ), D_MODEL ** -0.5),
        "conv_w": nrm(ks[3], (CONV_WIDTH, D_LRU), CONV_WIDTH ** -0.5),
        "conv_b": nrm(ks[4], (D_LRU,), 0.01),
        "lru_wa_f": nrm(ks[5], (LRU_HEADS, LRU_HEAD_DIM, LRU_HEAD_DIM), LRU_HEAD_DIM ** -0.5),
        "lru_ba_f": nrm(ks[6], (D_LRU,), 0.01),
        "lru_wx_f": nrm(ks[7], (LRU_HEADS, LRU_HEAD_DIM, LRU_HEAD_DIM), LRU_HEAD_DIM ** -0.5),
        "lru_bx_f": nrm(ks[8], (D_LRU,), 0.01),
        "lru_lam_f": lam_init(ks[9]),
        "lru_wa_b": nrm(ks[10], (LRU_HEADS, LRU_HEAD_DIM, LRU_HEAD_DIM), LRU_HEAD_DIM ** -0.5),
        "lru_ba_b": nrm(ks[11], (D_LRU,), 0.01),
        "lru_wx_b": nrm(ks[12], (LRU_HEADS, LRU_HEAD_DIM, LRU_HEAD_DIM), LRU_HEAD_DIM ** -0.5),
        "lru_bx_b": nrm(ks[13], (D_LRU,), 0.01),
        "lru_lam_b": lam_init(ks[14]),
        "w_out": nrm(ks[15], (D_MIX, D_MODEL), D_MIX ** -0.5),
        "norm2_g": 1.0 + nrm(ks[16], (D_MODEL,), 0.02),
        "w_router": nrm(ks[17], (D_MODEL, N_EXPERTS), D_MODEL ** -0.5),
        "w_gate": nrm(ks[18], (N_EXPERTS, D_MODEL, D_FF_EXPERT), D_MODEL ** -0.5),
        "w_up": nrm(ks[19], (N_EXPERTS, D_MODEL, D_FF_EXPERT), D_MODEL ** -0.5),
        "w_down": nrm(ks[20], (N_EXPERTS, D_FF_EXPERT, D_MODEL), D_FF_EXPERT ** -0.5),
        "normf_g": 1.0 + nrm(ks[21], (D_MODEL,), 0.02),
    }

def first_block(x, norm1_g, w_in, conv_w, conv_b,
              lru_wa_f, lru_ba_f, lru_wx_f, lru_bx_f, lru_lam_f,
              lru_wa_b, lru_ba_b, lru_wx_b, lru_bx_b, lru_lam_b,
              w_out, norm2_g, w_router, w_gate, w_up, w_down, normf_g):
    for _ in range(DEPTH):
        h = rmsnorm(x, norm1_g)
        p = jnp.einsum('bsd,dn->bsn', h, w_in)
        lru_x = p[..., :D_LRU]
        lru_gate = p[..., D_LRU:2 * D_LRU]
        four_in = p[..., 2 * D_LRU:]
        c = centred_depthwise_conv(lru_x, conv_w, conv_b)
        h_f = rglru(c, lru_wa_f, lru_ba_f, lru_wx_f, lru_bx_f, lru_lam_f, reverse=False)
        h_b = rglru(c, lru_wa_b, lru_ba_b, lru_wx_b, lru_bx_b, lru_lam_b, reverse=True)
        y_lru = (jax.nn.gelu(lru_gate.astype(jnp.float32)) * (h_f + h_b)).astype(x.dtype)
        y_four = fourier_mix(four_in).astype(x.dtype)
        mixed = jnp.concatenate([y_lru, y_four], axis=-1)
        x = x + jnp.einsum('bsm,md->bsd', mixed, w_out)
        h2 = rmsnorm(x, norm2_g)
        x = x + expert_choice_moe(h2, w_router, w_gate, w_up, w_down).astype(x.dtype)
    return rmsnorm(x, normf_g)


CHUNK = 64
LEFT_CHUNKS = 8
BAND_CHUNKS = LEFT_CHUNKS + 1
BAND = BAND_CHUNKS * CHUNK

N_HEADS = 8
HEAD_DIM = 64
ATTN_WIDTH = N_HEADS * HEAD_DIM
MAX_REL = 128
N_REL = CHUNK + MAX_REL
ATTN_SCALE = 1.0 / math.sqrt(HEAD_DIM)
NEG_INF = -1e30

SSM_WIDTH = 512
SSM_GROUP = 16
SSM_GROUPS = SSM_WIDTH // SSM_GROUP
SSM_STATE = 64
DT_MIN = 0.001
DT_MAX = 0.1

NORM_EPS = 1e-6
IN_COLS = 4 * ATTN_WIDTH + 2 * SSM_WIDTH + 2 * D_MODEL
SPLITS = list(np.cumsum([ATTN_WIDTH, ATTN_WIDTH, ATTN_WIDTH, ATTN_WIDTH, SSM_WIDTH, SSM_WIDTH, D_MODEL])[:])


def rms_norm(x, gain):
    xf = x.astype(jnp.float32)
    inv = lax.rsqrt(jnp.mean(xf * xf, axis=-1, keepdims=True) + NORM_EPS)
    return (xf * inv * gain.astype(jnp.float32)).astype(x.dtype)

def band_attention(q, k, v, rel_bias):
    b, l, h, dh = q.shape
    nc = l // CHUNK
    qc = q.reshape(b, nc, CHUNK, h, dh)
    kc = k.reshape(b, nc, CHUNK, h, dh)
    vc = v.reshape(b, nc, CHUNK, h, dh)
    pad = ((0, 0), (LEFT_CHUNKS, 0), (0, 0), (0, 0), (0, 0))
    kp = jnp.pad(kc, pad)
    vp = jnp.pad(vc, pad)
    k_band = jnp.stack([kp[:, j:j + nc] for j in range(BAND_CHUNKS)], axis=2).reshape(b, nc, BAND, h, dh)
    v_band = jnp.stack([vp[:, j:j + nc] for j in range(BAND_CHUNKS)], axis=2).reshape(b, nc, BAND, h, dh)
    scores = jnp.einsum("bnqhd,bnkhd->bnhqk", qc, k_band,
                        preferred_element_type=jnp.float32) * ATTN_SCALE
    qi = jnp.arange(CHUNK)[:, None] + LEFT_CHUNKS * CHUNK
    kp_idx = jnp.arange(BAND)[None, :]
    rel = jnp.clip(qi - kp_idx, -(CHUNK - 1), MAX_REL) + (CHUNK - 1)
    bias = rel_bias.astype(jnp.float32)[:, rel]
    key_chunk = jnp.arange(nc)[:, None] - LEFT_CHUNKS + (jnp.arange(BAND) // CHUNK)[None, :]
    valid = (key_chunk >= 0)[None, :, None, None, :]
    scores = jnp.where(valid, scores + bias[None, None], NEG_INF)
    probs = jax.nn.softmax(scores, axis=-1).astype(v.dtype)
    out = jnp.einsum("bnhqk,bnkhd->bnqhd", probs, v_band)
    return out.reshape(b, l, h * dh)

def _complex_linear_combine(e1, e2):
    a1r, a1i, b1r, b1i = e1
    a2r, a2i, b2r, b2i = e2
    ar = a2r * a1r - a2i * a1i
    ai = a2r * a1i + a2i * a1r
    br = a2r * b1r - a2i * b1i + b2r
    bi = a2r * b1i + a2i * b1r + b2i
    return ar, ai, br, bi

def s5_ssm(u, a_re, a_im, log_dt, b_re, b_im, c_re, c_im, d_skip):
    bsz, l, _ = u.shape
    f32 = jnp.float32
    uf = u.astype(f32).reshape(bsz, l, SSM_GROUPS, SSM_GROUP)
    lam_re = a_re.astype(f32)
    lam_im = a_im.astype(f32)
    dt = jnp.exp(log_dt.astype(f32))[:, None]
    mag = jnp.exp(lam_re * dt)
    ab_re = mag * jnp.cos(lam_im * dt)
    ab_im = mag * jnp.sin(lam_im * dt)
    n_re = ab_re - 1.0
    n_im = ab_im
    den = lam_re * lam_re + lam_im * lam_im
    f_re = ((n_re * lam_re + n_im * lam_im) / den)[..., None]
    f_im = ((n_im * lam_re - n_re * lam_im) / den)[..., None]
    br_ = b_re.astype(f32)
    bi_ = b_im.astype(f32)
    bb_re = f_re * br_ - f_im * bi_
    bb_im = f_re * bi_ + f_im * br_
    bu_re = jnp.einsum("blgc,gpc->blgp", uf, bb_re)
    bu_im = jnp.einsum("blgc,gpc->blgp", uf, bb_im)
    a_r = jnp.broadcast_to(ab_re, bu_re.shape)
    a_i = jnp.broadcast_to(ab_im, bu_im.shape)
    _, _, h_re, h_im = lax.associative_scan(_complex_linear_combine, (a_r, a_i, bu_re, bu_im), axis=1)
    y = (jnp.einsum("blgp,gcp->blgc", h_re, c_re.astype(f32))
         - jnp.einsum("blgp,gcp->blgc", h_im, c_im.astype(f32)))
    y = y.reshape(bsz, l, SSM_WIDTH) + d_skip.astype(f32) * uf.reshape(bsz, l, SSM_WIDTH)
    return y.astype(u.dtype)

def second_inputs(seed: int = 0) -> dict:
    key = jax.random.key(seed)
    ks = jax.random.split(key, 20)
    f32 = jnp.float32
    x = jax.random.normal(ks[0], (BATCH, SEQ, D_MODEL), f32)
    norm_gain = 1.0 + 0.02 * jax.random.normal(ks[1], (DEPTH, D_MODEL), f32)
    w_in = jax.random.normal(ks[2], (DEPTH, D_MODEL, IN_COLS), f32) * D_MODEL ** -0.5
    rel_bias = 0.1 * jax.random.normal(ks[3], (DEPTH, N_HEADS, N_REL), f32)
    n_idx = jnp.arange(SSM_STATE, dtype=f32)[None, None, :]
    ssm_a_re = -0.5 + 0.01 * jax.random.normal(ks[4], (DEPTH, SSM_GROUPS, SSM_STATE), f32)
    ssm_a_im = math.pi * n_idx + 0.01 * jax.random.normal(ks[5], (DEPTH, SSM_GROUPS, SSM_STATE), f32)
    ssm_log_dt = jax.random.uniform(ks[6], (DEPTH, SSM_GROUPS), f32,
                                    minval=math.log(DT_MIN), maxval=math.log(DT_MAX))
    b_scale = (2.0 * SSM_GROUP) ** -0.5
    ssm_b_re = jax.random.normal(ks[7], (DEPTH, SSM_GROUPS, SSM_STATE, SSM_GROUP), f32) * b_scale
    ssm_b_im = jax.random.normal(ks[8], (DEPTH, SSM_GROUPS, SSM_STATE, SSM_GROUP), f32) * b_scale
    c_scale = (2.0 * SSM_STATE) ** -0.5
    ssm_c_re = jax.random.normal(ks[9], (DEPTH, SSM_GROUPS, SSM_GROUP, SSM_STATE), f32) * c_scale
    ssm_c_im = jax.random.normal(ks[10], (DEPTH, SSM_GROUPS, SSM_GROUP, SSM_STATE), f32) * c_scale
    ssm_d = jax.random.normal(ks[11], (DEPTH, SSM_WIDTH), f32)
    w_glu = jax.random.normal(ks[12], (DEPTH, SSM_WIDTH, 2 * SSM_WIDTH), f32) * SSM_WIDTH ** -0.5
    b_glu = 0.01 * jax.random.normal(ks[13], (DEPTH, 2 * SSM_WIDTH), f32)
    w_attn_out = jax.random.normal(ks[14], (DEPTH, ATTN_WIDTH, D_MODEL), f32) * ATTN_WIDTH ** -0.5
    w_ssm_out = jax.random.normal(ks[15], (DEPTH, SSM_WIDTH, D_MODEL), f32) * SSM_WIDTH ** -0.5
    gate_bias = 0.01 * jax.random.normal(ks[16], (DEPTH, 2 * D_MODEL), f32)
    w_out = jax.random.normal(ks[17], (DEPTH, D_MODEL, D_MODEL), f32) * D_MODEL ** -0.5
    final_gain = 1.0 + 0.02 * jax.random.normal(ks[18], (D_MODEL,), f32)
    return {"x": x, "norm_gain": norm_gain, "w_in": w_in, "rel_bias": rel_bias,
            "ssm_a_re": ssm_a_re, "ssm_a_im": ssm_a_im, "ssm_log_dt": ssm_log_dt,
            "ssm_b_re": ssm_b_re, "ssm_b_im": ssm_b_im, "ssm_c_re": ssm_c_re, "ssm_c_im": ssm_c_im,
            "ssm_d": ssm_d, "w_glu": w_glu, "b_glu": b_glu, "w_attn_out": w_attn_out,
            "w_ssm_out": w_ssm_out, "gate_bias": gate_bias, "w_out": w_out, "final_gain": final_gain}

def second_block(x, norm_gain, w_in, rel_bias, ssm_a_re, ssm_a_im, ssm_log_dt, ssm_b_re, ssm_b_im,
              ssm_c_re, ssm_c_im, ssm_d, w_glu, b_glu, w_attn_out, w_ssm_out, gate_bias, w_out,
              final_gain):
    bsz, l, _ = x.shape
    for layer in range(DEPTH):
        h = rms_norm(x, norm_gain[layer])
        proj = h @ w_in[layer]
        q, k, v, z_a, u, z_s, g_a, g_s = jnp.split(proj, SPLITS, axis=-1)
        g_a = g_a + gate_bias[layer, :D_MODEL]
        g_s = g_s + gate_bias[layer, D_MODEL:]
        heads = lambda t: t.reshape(bsz, l, N_HEADS, HEAD_DIM)
        y_a = band_attention(heads(q), heads(k), heads(v), rel_bias[layer])
        y_a = (y_a * jax.nn.silu(z_a)) @ w_attn_out[layer]
        y_s = s5_ssm(u, ssm_a_re[layer], ssm_a_im[layer], ssm_log_dt[layer], ssm_b_re[layer],
                     ssm_b_im[layer], ssm_c_re[layer], ssm_c_im[layer], ssm_d[layer])
        y_s = jax.nn.gelu(y_s)
        glu_a, glu_b = jnp.split(y_s @ w_glu[layer] + b_glu[layer], 2, axis=-1)
        y_s = glu_a * jax.nn.sigmoid(glu_b)
        y_s = (y_s * jax.nn.silu(z_s)) @ w_ssm_out[layer]
        merged = jax.nn.sigmoid(g_a) * y_a + jax.nn.sigmoid(g_s) * y_s
        x = x + merged @ w_out[layer]
    return rms_norm(x, final_gain)


def setup_inputs(seed=0):
    out = dict(first_inputs(seed))
    for name, value in second_inputs(seed + 1).items():
        if name != "x":
            out[name + "_2"] = value
    return out


def reference(
    x, norm1_g, w_in, conv_w, conv_b, lru_wa_f, lru_ba_f, lru_wx_f, lru_bx_f, lru_lam_f,
    lru_wa_b, lru_ba_b, lru_wx_b, lru_bx_b, lru_lam_b, w_out, norm2_g, w_router, w_gate, w_up,
    w_down, normf_g, norm_gain_2, w_in_2, rel_bias_2, ssm_a_re_2, ssm_a_im_2, ssm_log_dt_2,
    ssm_b_re_2, ssm_b_im_2, ssm_c_re_2, ssm_c_im_2, ssm_d_2, w_glu_2, b_glu_2, w_attn_out_2,
    w_ssm_out_2, gate_bias_2, w_out_2, final_gain_2,
):
    x = first_block(
        x, norm1_g, w_in, conv_w, conv_b, lru_wa_f, lru_ba_f, lru_wx_f, lru_bx_f, lru_lam_f,
        lru_wa_b, lru_ba_b, lru_wx_b, lru_bx_b, lru_lam_b, w_out, norm2_g, w_router, w_gate,
        w_up, w_down, normf_g,
    )
    return second_block(
        x, norm_gain_2, w_in_2, rel_bias_2, ssm_a_re_2, ssm_a_im_2, ssm_log_dt_2, ssm_b_re_2,
        ssm_b_im_2, ssm_c_re_2, ssm_c_im_2, ssm_d_2, w_glu_2, b_glu_2, w_attn_out_2,
        w_ssm_out_2, gate_bias_2, w_out_2, final_gain_2,
    )


_drawn_inputs = setup_inputs


def setup_inputs(seed=0):
    import zlib

    import numpy as np

    out = dict(_drawn_inputs(seed))
    spreads = {}
    factors = {'norm1_g': 3.136,
     'conv_b': 2.914,
     'lru_ba_f': 8.0,
     'lru_bx_f': 8.0,
     'lru_ba_b': 8.0,
     'lru_bx_b': 8.0,
     'norm2_g': 3.665,
     'normf_g': 2.712,
     'norm_gain_2': 8.0,
     'rel_bias_2': 8.0,
     'ssm_a_re_2': 64.0,
     'ssm_a_im_2': 64.0,
     'ssm_log_dt_2': 64.0,
     'ssm_b_re_2': 64.0,
     'ssm_b_im_2': 64.0,
     'ssm_c_re_2': 64.0,
     'ssm_c_im_2': 64.0,
     'b_glu_2': 53.947,
     'gate_bias_2': 40.359,
     'final_gain_2': 7.792}
    for name, (base, spread) in spreads.items():
        noise = np.random.default_rng([zlib.crc32(name.encode()), seed]).standard_normal(out[name].shape)
        drawn = base * np.exp(spread * noise) if base else spread * noise
        out[name] = __import__('jax').numpy.asarray(drawn.astype(out[name].dtype))
    for name, factor in factors.items():
        out[name] = (out[name] * factor).astype(out[name].dtype)
    return out
```

```python
from contextlib import ExitStack

import numpy as np
import concourse.bass as bass
from concourse import mybir

f32 = mybir.dt.float32
ALU = mybir.AluOpType
ACT = mybir.ActivationFunctionType
AX = mybir.AxisListType.X

P = 128
S = 512
D = 1024
TT = S // P
KT = D // P
LRU = D // 2
CT = LRU // P
CONV = 4
CONV_LEFT = CONV // 2
NE = 16
CAP = 2 * S // NE
FF = 2 * D
EPS = 1e-6
GELU_C = 0.7978845608028654
GELU_A = 0.044715
LRU_C = 8.0

HEADS, DH = 8, 64
NREL, CHUNK = 192, 64
SCALE = DH ** -0.5
REL = 256
GRP, SG, NS = 32, 16, 64
T8 = P // SG
NCH = S // T8
GP = GRP // 2
CGP = GP // CT
CG = 2 * CGP
TWO_PI = 2 * np.pi
PI_HI = 6.28125
PI_MID = float(np.float32(np.round((TWO_PI - PI_HI) * 2 ** 20) / 2 ** 20))
PI_LO = float(np.float32(TWO_PI - PI_HI - PI_MID))
ROUND = 1.5 * 2 ** 23

UNIT = 2048
RING = 12
RING2 = 5
B1_UNITS = 13
E_UNITS = 24
MOE_END = B1_UNITS + NE * E_UNITS

COLS = [("g1", KT), ("g2", KT), ("gb2", KT), ("conv_w", CONV * CT), ("conv_b", CT),
        ("bias_lru", 4 * CT), ("lam", 2 * CT), ("b_glu", KT), ("gate_b", 2 * KT),
        ("a_re", GP), ("a_im", GP), ("log_dt", GP), ("skip", CT), ("rb_far", HEADS),
        ("w_router", KT * 2 * NE)]
COL, NCOLS = {}, 0
for _name, _w in COLS:
    COL[_name] = NCOLS
    NCOLS += _w
NCST = 3 * P + CAP + CG


class Jobs:

    def __init__(self, bank_full, unit_used):
        self.bank_full, self.unit_used = bank_full, unit_used
        self.uses, self.told, self.of, self.turn = [0] * 8, [0] * 8, {}, 0

    def add(self, name, bank=None, unit=None):
        if bank is None:
            bank = self.turn
            self.turn = (self.turn + 1) % 8
        if unit is None:
            self.told[bank] += 1
            end = (self.bank_full[bank], self.told[bank])
        else:
            end = (self.unit_used, unit + 1)
        self.of[name] = (bank, self.uses[bank], end)
        self.uses[bank] += 1

    def bank(self, name):
        return self.of[name][0]

    def before(self, name):
        return self.of[name][1]

    def end(self, name):
        return self.of[name][2]


def build(nc, x, cols_d, cst_d, wbd_d, w_in, dft_s, w_out, w_gate, w_up, w_down, gf_d, w_in2, relp,
          bc_d, w_glu, w_ao, w_so, w_out2, gfin_d, out, u_dram, y_dram):
    with ExitStack() as ctx:
        mem = ctx.enter_context(nc.sbuf_tensor("mem", [P, 53200], f32))
        ends = {}

        def area(name, off, *shape, parts=P):
            n = int(np.prod(shape))
            assert off >= 0 and off + n <= 53200, (name, off + n)
            ends[name] = off + n
            v = mem[0:parts, off:off + n]
            if len(shape) == 1:
                return v
            letters = "abcd"[:len(shape)]
            return v.rearrange(f"p ({' '.join(letters)}) -> p {' '.join(letters)}",
                               **dict(zip(letters[1:], shape[1:])))

        def flat(v):
            return v.rearrange("p a b -> p (a b)")

        ring = [area(f"ring{s}", s * UNIT, UNIT) for s in range(RING)]
        xres = area("xres", RING * UNIT, TT, D)
        nrm = area("nrm", ends["xres"], TT, D)
        hT = area("hT", ends["nrm"], KT, S)
        cols = area("cols", ends["hT"], NCOLS)
        cst = area("cst", ends["cols"], NCST)
        stat = area("stat", ends["cst"], 64)
        hbias = area("hbias", ends["stat"], 4 * CT + 3 * KT)
        kpos = area("kpos", ends["hbias"], 2 * CT)
        kneg = area("kneg", ends["kpos"], 2 * CT)
        Z = ends["kneg"]
        ident, dft, slotrow = cst[:, 0:P], cst[:, P:3 * P], cst[:, 3 * P:3 * P + CAP]
        group_of = cst[:, 3 * P + CAP:NCST]

        def col(name, i=0, n=1):
            return cols[:, COL[name] + i:COL[name] + i + n]

        mixT = area("mixT", Z, 2 * CT, S)
        lrux = area("lrux", ends["mixT"], CT, S + CONV)
        conv = area("conv", ends["lrux"], CT, S)
        gt = area("gt", ends["conv"], 2, 4, S)
        four = flat(nrm).rearrange("p (t g c) -> p t g c", t=TT, g=CT)
        aff = area("aff", Z, TT, NE + 1)
        posT = area("posT", ends["aff"], TT, NE + 1)
        sel = area("sel", ends["posT"], TT, CAP)
        gsel = area("gsel", ends["sel"], TT, 2, CAP)
        gselT = area("gselT", ends["gsel"], TT, P)
        xinT = area("xinT", ends["gselT"], KT, CAP)
        th = area("th", ends["xinT"], 2, 512)
        act = area("act", ends["th"], 2, 512)
        actT = area("actT", ends["act"], KT, P)
        eo = area("eo", ends["actT"], 512)
        score = area("score", ends["eo"], S, parts=NE)
        top = area("top", ends["score"], 8, parts=NE)
        taken = area("taken", ends["top"], S, parts=NE)
        rank = area("rank", ends["taken"], S, parts=NE)
        ones = area("ones", ends["rank"], S, parts=NE)
        logT = area("logT", ends["ones"], P)
        qT = area("qT", 0, CT, S)
        kT = area("kT", (RING2 + 1) * UNIT, CT, S)
        v_s = area("v_s", ends["kT"], TT, LRU)
        zaT = area("zaT", ends["v_s"], CT, S)
        zsT = area("zsT", ends["zaT"], CT, S)
        gaT = area("gaT", ends["zsT"], KT, S)
        assert ends["gaT"] <= RING * UNIT
        att = area("att", RING * UNIT + TT * D, TT, S)
        relb = area("relb", ends["att"], HEADS, REL)
        assert ends["relb"] <= ends["nrm"]
        pT = area("pT", Z, 10 * P)
        gfin = area("gfin", Z, D)
        rotc = area("rotc", ends["pT"], GP, NCH)
        rots = area("rots", ends["rotc"], GP, NCH)
        mag8 = area("mag8", ends["rots"], GP)
        pw_re = area("pw_re", ends["mag8"], GP, T8 + 1)
        pw_im = area("pw_im", ends["pw_re"], GP, T8 + 1)
        pw_in = area("pw_in", ends["pw_im"], GP, T8 + 1)
        bc = area("bc", ends["pw_in"], 4, GP, SG)
        bbd = area("bbd", ends["bc"], 2, GP, 2 * SG)
        uT = area("uT", ends["bbd"], CT, T8, NCH)
        ubuf = area("ubuf", ends["uT"], CG, NCH)
        ybuf = area("ybuf", ends["ubuf"], CG, NCH)
        hbd = area("hbd", ends["ybuf"], 2, CGP, 2, NCH)
        tmp = area("tmp", ends["hbd"], 2, 512)
        wext = area("wext", ends["tmp"], 2, CGP, P)
        wc = area("wc", ends["wext"], 2, CGP, (T8 + 1) * SG)
        st = area("st", ends["wc"], 2, CGP, P)
        kbd = area("kbd", ends["st"], T8 + 1, P)
        gsT = area("gsT", ends["tmp"], KT, S)
        gfb = area("gfb", ends["tmp"], D)
        prep = area("prep", ends["wext"], 24, GP)
        prot = area("prot", ends["prep"], 2, GP, NCH // 2)
        assert ends["gsT"] <= ends["kbd"] and ends["prot"] <= ends["kbd"] and ends["gfb"] <= ends["wext"]
        print('END', ends['kbd'], 53200)
        yT = qT
        ysT = kT

        bank = [ctx.enter_context(nc.psum_tensor(f"bank{b}", [P, 512], f32)) for b in range(8)]

        def sem(name):
            return ctx.enter_context(nc.semaphore(name))

        ring_full = [sem(f"ring_full{s}") for s in range(RING)]
        unit_used = sem("unit_used")
        bank_full = [sem(f"bank_full{b}") for b in range(8)]
        bank_read = [sem(f"bank_read{b}") for b in range(8)]
        x_in = [sem(f"x_in{t}") for t in range(TT)]
        cols_in, cst_in, gf_in, rel_in = sem("cols_in"), sem("cst_in"), sem("gf_in"), sem("rel_in")
        bc_in, gfin_in = sem("bc_in"), sem("gfin_in")
        dve_step, act_step, pool_step = sem("dve_step"), sem("act_step"), sem("pool_step")
        square_sum, root_mean, normed = sem("square_sum"), sem("root_mean"), sem("normed")
        pad_zero, halves, lam_exp, lam_ln, k_ready = (
            sem("pad_zero"), sem("halves"), sem("lam_exp"), sem("lam_ln"), sem("k_ready"))
        conv_ready, acts_ready, m2_ready, root_ready, lru_done = (
            sem("conv_ready"), sem("acts_ready"), sem("m2_ready"), sem("root_ready"), sem("lru_done"))
        gelu_in, gelu_tanh, gelu_done = sem("gelu_in"), sem("gelu_tanh"), sem("gelu_done")
        soft_in, soft_exp, aff_ready, pos_ready = (
            sem("soft_in"), sem("soft_exp"), sem("aff_ready"), sem("pos_ready"))
        sel_ready, tanh_ready, act_ready = sem("sel_ready"), sem("tanh_ready"), sem("act_ready")
        u_out, u_in, y_out, y_in = sem("u_out"), sem("u_in"), sem("y_out"), sem("y_in")
        prep_in, prep_exp, prep_sin, sin_arg = (
            sem("prep_in"), sem("prep_exp"), sem("prep_sin"), sem("sin_arg"))
        wext_ready, wc_ready, pw_ready, states_ready = (
            sem("wext_ready"), sem("wc_ready"), sem("pw_ready"), sem("states_ready"))
        bbd_ready, kbd_ready, ygelu_in, ytanh, y_ready = (
            sem("bbd_ready"), sem("kbd_ready"), sem("ygelu_in"), sem("ytanh"), sem("y_ready"))
        max_ready, exp_ready, prob_ready = sem("max_ready"), sem("exp_ready"), sem("prob_ready")
        th_ready, glu_ready, merged = sem("th_ready"), sem("glu_ready"), sem("merged")
        between, final_ready, stored = sem("between"), sem("final_ready"), sem("stored")

        jobs = Jobs(bank_full, unit_used)
        for k in range(KT):
            jobs.add(f"xT{k}", k)
        for n in range(12):
            jobs.add(f"in{n}", unit=n // 2 if n % 2 else None)
        for c in range(CT):
            for i in range(4):
                jobs.add(f"lru{c}_{i}", unit=6 if (c, i) == (CT - 1, 3) else None)
            for half in range(2):
                jobs.add(f"four{c}_{half}")
        for g in range(CT):
            jobs.add(f"mix{g}", unit=8 if g == CT - 1 else None)
        for o in range(8):
            jobs.add(f"out{o}", unit=12 if o == 7 else None)
        for k in range(KT):
            jobs.add(f"h2T{k}", k)
        jobs.add("logitT", 0)
        jobs.add("logits", 1)
        jobs.add("scoreT", 2)
        jobs.add("posT", 3)
        moe_uses, moe_told = list(jobs.uses), list(jobs.told)
        EU = [3, 2, 2, 1, 1, 2, 2, 2]
        EF = [3, 1, 1, 1, 1, 2, 2, 1]
        for b in range(8):
            jobs.uses[b] += NE * EU[b]
            jobs.told[b] += NE * EF[b]
        for k in range(KT):
            jobs.add(f"yT{k}", k)
        M = MOE_END
        for n in range(12):
            jobs.add(f"proj{n}", unit=M + n // 2 if n % 2 else None)
        for u in range(2):
            for t in range(TT):
                jobs.add(f"v{u}_{t}", unit=M + 6 + u if t == TT - 1 else None)
        GELU_STEP = 2 * CT + 1
        STEPS = 12
        for i in range(STEPS):
            if i < HEADS:
                for q in range(TT):
                    jobs.add(f"score{i}_{q}")
            for n in range(2):
                jobs.add(f"gate{2 * i + n}", unit=M + 8 + i if n else None)
            if i % 2 == 1 and i < 2 * CT:
                jobs.add(f"lags_{i // 2}")
            if i < HEADS:
                for b in range(3):
                    jobs.add(f"probT{i}_{b}")
                jobs.add(f"pv{i}")
            if i % 2 == 0 and 2 <= i <= 2 * CT:
                jobs.add(f"ssm{i // 2 - 1}")
            if i % 2 == 0 and i < 2 * CT:
                for name in ("st_re", "st_im"):
                    jobs.add(f"{name}_{i // 2}")
            if i % 2 == 1 and i < 2 * CT:
                jobs.add(f"state{i // 2}")
                jobs.add(f"near{i // 2}")
        for d in range(KT):
            jobs.add(f"ao{d}", unit=M + 20 + d // 4 if d % 4 == 3 else None)
        for n in range(8):
            jobs.add(f"glu{n}", unit=M + 22 + n // 4 if n % 4 == 3 else None)
        for d in range(KT):
            jobs.add(f"so{d}", unit=M + 24 + d // 4 if d % 4 == 3 else None)
        for o in range(8):
            jobs.add(f"fin{o}", unit=M + 29 if o == 7 else None)

        def full(eng, name):
            eng.wait_ge(*jobs.end(name))

        def was_read(eng, name):
            eng.wait_ge(bank_read[jobs.bank(name)], jobs.before(name) + 1)

        def read(name, ins):
            ins.then_inc(bank_read[jobs.bank(name)], 1)

        def slot_of(unit):
            return unit % RING if unit < MOE_END else 1 + (unit - MOE_END) % RING2

        loads_b1 = [sum(u % RING == s for u in range(B1_UNITS)) for s in range(RING)]

        def loaded(eng, unit):
            s = slot_of(unit)
            if unit < MOE_END:
                n = unit // RING + 1
            else:
                n = loads_b1[s] + 2 * NE + (unit - MOE_END) // RING2 + 1
            eng.wait_ge(ring_full[s], 16 * n)

        def view(unit, inner):
            return ring[slot_of(unit)].rearrange("p (k n) -> p k n", n=inner)

        block = ctx.enter_context(nc.Block())

        @block.sync
        def _(sp):
            def load(unit, src, inner):
                s = slot_of(unit)
                if unit >= MOE_END:
                    v = unit - MOE_END
                    last = max(u for u in range(MOE_END - RING, MOE_END) if u % RING == s) if v < RING2 else unit - RING2
                    sp.wait_ge(unit_used, last + 1)
                elif unit >= RING:
                    sp.wait_ge(unit_used, unit - RING + 1)
                sp.dma_start(view(unit, inner), src).then_inc(ring_full[s], 16)

            for t in range(TT):
                sp.dma_start(xres[:, t, :], x[t * P:(t + 1) * P, :]).then_inc(x_in[t], 16)
            w_in_k = w_in.rearrange("(k p) n -> p k n", p=P)
            for u, c in enumerate((0, 1, 4, 5, 2, 3)):
                load(u, w_in_k[:, :, 256 * c:256 * c + 256], 256)
            load(6, wbd_d.rearrange("p (k n) -> p k n", n=P), P)
            for i in range(2):
                load(7 + i, dft_s[i].rearrange("(k p) n -> p k n", p=P), S)
            w_out_m = w_out.rearrange("(m p) n -> p m n", p=P)
            for u, m in enumerate((4, 6, 0, 2)):
                load(9 + u, w_out_m[:, m:m + 2, :], D)

            with sp.Fori(0, NE) as e:
                for m in range(E_UNITS):
                    s = (B1_UNITS + m) % RING
                    if m < KT * 2:
                        w, k = (w_gate, w_up)[m % 2], m // 2
                        src = w[bass.ds(e, 1), k * P:(k + 1) * P, :].rearrange("a p n -> p (a n)")
                        dst = ring[s]
                    else:
                        j = m - 2 * KT
                        src = w_down[bass.ds(e, 1), 2 * j * P:(2 * j + 2) * P, :].rearrange(
                            "a (i p) n -> p (a i) n", i=2)
                        dst = ring[s].rearrange("p (i n) -> p i n", i=2)
                    sp.wait_ge(unit_used, e * E_UNITS + (B1_UNITS + m - RING + 1))
                    sp.dma_start(dst, src).then_inc(ring_full[s], 16)

            w2 = w_in2.rearrange("(k p) n -> p k n", p=P)
            order = [8, 9, 0, 1, 2, 3, 4, 5, 6, 7, 10, 11] + list(range(12, 20))
            for u, c in enumerate(order):
                load(MOE_END + u, w2[:, :, 256 * c:256 * c + 256], 256)
            for i in range(2):
                load(MOE_END + 20 + i, w_ao.rearrange("(k p) n -> p k n", p=P)[:, :, 512 * i:512 * i + 512], 512)
            for i in range(2):
                load(MOE_END + 22 + i,
                     w_glu.rearrange("(k p) n -> p k n", p=P)[:, :, 512 * (1 - i):512 * (1 - i) + 512], 512)
            for i in range(2):
                load(MOE_END + 24 + i, w_so.rearrange("(k p) n -> p k n", p=P)[:, :, 512 * i:512 * i + 512], 512)
            for i in range(4):
                load(MOE_END + 26 + i, w_out2.rearrange("(m p) n -> p m n", p=P)[:, 2 * i:2 * i + 2, :], D)

            for t in range(TT):
                sp.wait_ge(final_ready, t + 1)
                sp.dma_start(out[t * P:(t + 1) * P, :], xres[:, t, :]).then_inc(stored, 16)
            sp.wait_ge(stored, 16 * TT)

        @block.tensor
        def _(pe):
            def start(name, **kw):
                b = jobs.bank(name)
                if jobs.before(name):
                    pe.wait_ge(bank_read[b], jobs.before(name))
                return bank[b]

            def finish(name, ins):
                who, _ = jobs.end(name)
                ins.then_inc(who, 1)

            def transposes(prefix, ready0):
                for t in range(TT):
                    pe.wait_ge(normed, ready0 + t + 1)
                    for k in range(KT):
                        b = start(f"{prefix}{k}") if t == 0 else bank[k]
                        last = pe.transpose(b[:, t * P:(t + 1) * P], nrm[:, t, k * P:(k + 1) * P], ident)
                        if t == TT - 1:
                            finish(f"{prefix}{k}", last)

            def project(name, w, c0, rows, kn):
                b = start(name)
                for k in range(kn):
                    last = pe.matmul(b[:, :], w[:, k, c0:c0 + P], rows[:, k, :], start=(k == 0), stop=(k == kn - 1))
                finish(name, last)

            def out_project(prefix, rows, unit0, ms, rows_ready=None):
                for u, m0 in enumerate(ms):
                    unit = unit0 + u
                    if rows_ready:
                        rows_ready(m0)
                    loaded(pe, unit)
                    w = view(unit, D)
                    tail = u == len(ms) - 1
                    for o in range(8):
                        t, n = o // 2, o % 2
                        b = start(f"{prefix}{o}") if u == 0 else bank[jobs.bank(f"{prefix}{o}")]
                        for i in range(2):
                            last = pe.matmul(b[:, :], rows[:, m0 + i, t * P:(t + 1) * P], w[:, i, n * 512:n * 512 + 512],
                                             start=(u == 0 and i == 0), stop=(tail and i == 1))
                        if tail:
                            finish(f"{prefix}{o}", last)
                    if not tail:
                        last.then_inc(unit_used, 1)

            pe.wait_ge(cst_in, 16)
            transposes("xT", 0)
            for n in range(12):
                if n == 0:
                    for k in range(KT):
                        was_read(pe, f"xT{k}")
                if n % 2 == 0:
                    loaded(pe, n // 2)
                project(f"in{n}", view(n // 2, 256), (n % 2) * P, hT, KT)
            loaded(pe, 6)
            wbd = view(6, P)
            for c in range(CT):
                pe.wait_ge(conv_ready, c + 1)
                for i in range(4):
                    b = start(f"lru{c}_{i}")
                    finish(f"lru{c}_{i}", pe.matmul(b[:, :], wbd[:, 4 * i + c, :], conv[:, c, :], start=True, stop=True))
                if c == 0:
                    for g in range(CT):
                        was_read(pe, f"in{4 + g}")
                for half in range(2):
                    b = start(f"four{c}_{half}")
                    for i in range(2):
                        g = 2 * half + i
                        last = pe.matmul(b[:, 256 * i:256 * i + 256], mixT[:, CT + g, c * P:(c + 1) * P], dft,
                                         start=True, stop=True)
                    finish(f"four{c}_{half}", last)
            loaded(pe, 7)
            loaded(pe, 8)
            for c in range(CT):
                for half in range(2):
                    was_read(pe, f"four{c}_{half}")
            for g in range(CT):
                b = start(f"mix{g}")
                for i in range(2):
                    w = view(7 + i, S)
                    for t in range(TT):
                        last = pe.matmul(b[:, :], four[:, t, g, i * P:(i + 1) * P], w[:, t, :],
                                         start=(i == 0 and t == 0), stop=(i == 1 and t == TT - 1))
                    if i == 0 and g == CT - 1:
                        last.then_inc(unit_used, 1)
                finish(f"mix{g}", last)
            for g in range(CT):
                was_read(pe, f"mix{g}")
            out_project("out", mixT, 9, (4, 6, 0, 2), lambda m0: m0 < CT and pe.wait_ge(lru_done, m0 + 2))

            transposes("h2T", TT)
            for k in range(KT):
                was_read(pe, f"h2T{k}")
            b = start("logitT")
            wr = col("w_router", 0, KT * 2 * NE).rearrange("p (k e) -> p k e", k=KT)
            for k in range(KT):
                for t in range(TT):
                    last = pe.matmul(b[32 * t:32 * t + 32, 0:P], wr[:, k, :], hT[:, k, t * P:(t + 1) * P],
                                     start=(k == 0), stop=(k == KT - 1))
            finish("logitT", last)
            was_read(pe, "logitT")
            b = start("logits")
            finish("logits", pe.transpose(b[:, 0:P], logT, ident))
            pe.wait_ge(aff_ready, 1)
            b = start("scoreT")
            for t in range(TT):
                last = pe.transpose(b[0:NE, t * P:(t + 1) * P], aff[:, t, 0:NE], ident)
            finish("scoreT", last)
            pe.wait_ge(pos_ready, 1)
            b = start("posT")
            for t in range(TT):
                last = pe.transpose(b[:, t * NE:(t + 1) * NE], rank[:, t * P:(t + 1) * P], ident[0:NE, 0:NE])
            finish("posT", last)

            with pe.Fori(0, NE) as e:
                def bank_free(b, n):
                    pe.wait_ge(bank_read[b], e * EU[b] + (moe_uses[b] + n))

                def arrived(m):
                    s = (B1_UNITS + m) % RING
                    pe.wait_ge(ring_full[s], e * 32 + 16 * (loads_b1[s] + m // RING + 1))

                pe.wait_ge(sel_ready, 2 * e + 1)
                bank_free(0, 0)
                for k in range(KT):
                    for t in range(TT):
                        last = pe.matmul(bank[0][:, k * CAP:(k + 1) * CAP], nrm[:, t, k * P:(k + 1) * P], sel[:, t, :],
                                         start=(t == 0), stop=(t == TT - 1))
                last.then_inc(bank_full[0], 1)
                pe.wait_ge(sel_ready, 2 * e + 2)
                bank_free(0, 1)
                for t in range(TT):
                    last = pe.transpose(bank[0][:, t * P:(t + 1) * P], gsel[:, t, :, :].rearrange("p a b -> p (a b)"), ident)
                last.then_inc(bank_full[0], 1)
                for b in range(1, 5):
                    bank_free(b, 0)
                for m in range(2 * KT):
                    arrived(m)
                    k, w = m // 2, ring[(B1_UNITS + m) % RING]
                    for q in range(4):
                        o = 64 * (q % 2)
                        last = pe.matmul(bank[1 + 2 * (m % 2) + q // 2][o:o + 64, :], xinT[:, k, :],
                                         w[:, q * 512:(q + 1) * 512], start=(k == 0), stop=(k == KT - 1))
                    last.then_inc(unit_used, 1)
                for b in range(2):
                    pe.wait_ge(act_ready, 2 * e + (b + 1))
                    bank_free(5 + b, 0)
                    for q in range(4):
                        last = pe.transpose(bank[5 + b][:, q * P:(q + 1) * P], act[:, b, q * P:(q + 1) * P], ident)
                    last.then_inc(bank_full[5 + b], 1)
                bank_free(5, 1)
                bank_free(6, 1)
                bank_free(7, 0)
                for j in range(8):
                    arrived(2 * KT + j)
                    w = ring[(B1_UNITS + 2 * KT + j) % RING].rearrange("p (i n) -> p i n", i=2)
                    for i in range(2):
                        kt = 2 * j + i
                        at = 64 * (kt // 4 % 2)
                        for n in range(2):
                            last = pe.matmul(bank[7][64 * n:64 * n + 64, :], actT[:, kt // 8 * 4 + kt % 4, at:at + 64],
                                             w[:, i, n * 512:n * 512 + 512], start=(kt == 0), stop=(kt == 15))
                    last.then_inc(unit_used, 1)
                for o, b in enumerate((0, 7, 1, 2, 3, 4, 5, 6)):
                    t, n = o // 2, o % 2
                    if o == 0:
                        bank_free(7, 1)
                    bank_free(b, EU[b] - 1)
                    pe.matmul(bank[b][:, :], gselT[64 * n:64 * n + 64, t, :], eo[64 * n:64 * n + 64, :],
                              start=True, stop=True).then_inc(bank_full[b], 1)

            transposes("yT", 2 * TT)
            for k in range(KT):
                was_read(pe, f"yT{k}")
            for n in range(12):
                unit = M + n // 2
                if n % 2 == 0:
                    loaded(pe, unit)
                project(f"proj{n}", view(unit, 256), (n % 2) * P, hT, KT)
            for u in range(2):
                loaded(pe, M + 6 + u)
                w = view(M + 6 + u, 256)
                for t in range(TT):
                    b = start(f"v{u}_{t}")
                    for k in range(KT):
                        last = pe.matmul(b[:, 0:256], hT[:, k, t * P:(t + 1) * P], w[:, k, :],
                                         start=(k == 0), stop=(k == KT - 1))
                    finish(f"v{u}_{t}", last)
            for n in range(4, 12):
                was_read(pe, f"proj{n}")
            for u in range(2):
                for t in range(TT):
                    was_read(pe, f"v{u}_{t}")

            def head_scores(h):
                r = 64 * (h % 2)
                for q in range(TT):
                    b = start(f"score{h}_{q}")
                    nk = (q + 1) * P
                    finish(f"score{h}_{q}", pe.matmul(b[:, 0:nk], qT[r:r + 64, h // 2, q * P:(q + 1) * P],
                                                      kT[r:r + 64, h // 2, 0:nk], start=True, stop=True))

            def head_values(h):
                pe.wait_ge(prob_ready, h + 1)
                for piece, kts in enumerate(((0,), (1,), (2, 3))):
                    b = start(f"probT{h}_{piece}")
                    c = 0
                    for kt in kts:
                        for q in range(kt, TT):
                            last = pe.transpose(b[:, c:c + P], att[:, q, kt * P:(kt + 1) * P], ident)
                            c += P
                    finish(f"probT{h}_{piece}", last)
                r = 64 * (h % 2)
                b = start(f"pv{h}")
                for piece in range(3):
                    was_read(pe, f"probT{h}_{piece}")
                for q in range(TT):
                    for kt in range(q + 1):
                        at = ((0, 4, 7, 9)[kt] + q - kt) * P
                        last = pe.matmul(b[r:r + 64, q * P:(q + 1) * P], v_s[:, kt, h * DH:(h + 1) * DH],
                                         pT[:, at:at + P], start=(kt == 0), stop=(kt == q))
                finish(f"pv{h}", last)

            def ssm_tables(c):
                pe.wait_ge(wext_ready, c + 1)
                for i, name in enumerate(("st_re", "st_im")):
                    b = start(f"{name}_{c}")
                    for g in range(CGP):
                        last = pe.transpose(b[:, g * P:(g + 1) * P], wext[:, i, g, 0:P], ident)
                    finish(f"{name}_{c}", last)

            def ssm_lags(c):
                pe.wait_ge(bbd_ready, 1)
                pe.wait_ge(wc_ready, c + 1)
                b = start(f"lags_{c}")
                for ri in range(2):
                    for g in range(CGP):
                        last = pe.matmul(b[32 * g:32 * g + 32, 0:P], bbd[:, ri, c * CGP + g, :], wc[:, ri, g, 0:P],
                                         start=(ri == 0), stop=(ri == 1))
                finish(f"lags_{c}", last)

            def ssm_states(c):
                pe.wait_ge(u_in, 16 * T8 * (c + 1))
                was_read(pe, f"st_re_{c}")
                was_read(pe, f"st_im_{c}")
                b = start(f"state{c}")
                for ri in range(2):
                    for g in range(CG):
                        r = 64 * (g % 2)
                        at = ri * 256 + (g // 2) * NCH
                        last = pe.matmul(b[r:r + 64, at:at + NCH], st[:, ri, g // 2, r:r + 64], ubuf[:, g, :],
                                         start=True, stop=True)
                finish(f"state{c}", last)
                pe.wait_ge(kbd_ready, c + 1)
                b = start(f"near{c}")
                for lag in range(T8 + 1):
                    n = (T8 - lag % T8) * NCH
                    last = pe.matmul(b[:, S - n:S], kbd[:, lag, :],
                                     uT[:, c, :, :].rearrange("p t j -> p (t j)")[:, 0:n],
                                     start=(lag == 0), stop=(lag == T8))
                finish(f"near{c}", last)

            def ssm_out(c):
                pe.wait_ge(states_ready, c + 1)
                b = start(f"ssm{c}")
                for g in range(CGP):
                    for ri in range(2):
                        last = pe.matmul(b[:, g * P:(g + 1) * P], wc[:, ri, g, SG:SG + P],
                                         hbd[:, ri, g, :, :].rearrange("p a b -> p (a b)"),
                                         start=(ri == 0), stop=(ri == 1))
                finish(f"ssm{c}", last)

            for i in range(STEPS):
                if i < HEADS:
                    head_scores(i)
                unit = M + 8 + i
                loaded(pe, unit)
                for n in range(2):
                    project(f"gate{2 * i + n}", view(unit, 256), n * P, hT, KT)
                if i % 2 == 1 and i < 2 * CT:
                    ssm_lags(i // 2)
                if i < HEADS:
                    head_values(i)
                if i % 2 == 0 and 2 <= i <= 2 * CT:
                    ssm_out(i // 2 - 1)
                if i % 2 == 0 and i < 2 * CT:
                    ssm_tables(i // 2)
                if i % 2 == 1 and i < 2 * CT:
                    ssm_states(i // 2)
            was_read(pe, f"pv{HEADS - 2}")
            was_read(pe, f"pv{HEADS - 1}")
            for d in range(KT):
                if d % 4 == 0:
                    loaded(pe, M + 20 + d // 4)
                project(f"ao{d}", view(M + 20 + d // 4, 512), (d % 4) * P, zaT, CT)
            pe.wait_ge(y_ready, CT)
            for n in range(8):
                if n % 4 == 0:
                    loaded(pe, M + 22 + n // 4)
                project(f"glu{n}", view(M + 22 + n // 4, 512), (n % 4) * P, yT, CT)
            pe.wait_ge(glu_ready, CT)
            for d in range(KT):
                if d % 4 == 0:
                    loaded(pe, M + 24 + d // 4)
                project(f"so{d}", view(M + 24 + d // 4, 512), (d % 4) * P, ysT, CT)
            pe.wait_ge(merged, KT)
            out_project("fin", gaT, M + 26, (0, 2, 4, 6))

        @block.scalar
        def _(act_e):
            steps = [0]

            def link(ins):
                steps[0] += 1
                ins.then_inc(act_step, 1)
                act_e.wait_ge(act_step, steps[0])

            act_e.dma_start(cst, cst_d).then_inc(cst_in, 16)
            act_e.dma_start(cols, cols_d).then_inc(cols_in, 16)

            def squares(n0, first=None):
                for t in range(TT):
                    if first is not None:
                        first(t)
                    act_e.activation(nrm[:, t, :], xres[:, t, :], ACT.Square,
                                     accum_out=stat[:, n0 + t:n0 + t + 1]).then_inc(square_sum, 1)

            def scaled(prefix, gain):
                for k in range(KT):
                    full(act_e, f"{prefix}{k}")
                    read(f"{prefix}{k}", act_e.activation(hT[:, k, :], bank[k][:, :], ACT.Copy, scale=col(gain, k)))

            def copy_out(name, dst, src=None):
                full(act_e, name)
                read(name, act_e.activation(dst, bank[jobs.bank(name)][:, :] if src is None else src, ACT.Copy))

            squares(0, lambda t: act_e.wait_ge(x_in[t], 16))
            act_e.wait_ge(cols_in, 16)
            act_e.wait_ge(halves, 1)
            link(act_e.activation(kneg, kneg, ACT.Exp, scale=-1.0))
            act_e.activation(kneg, kneg, ACT.Ln, bias=1.0).then_inc(lam_ln, 1)
            scaled("xT", "g1")
            act_e.wait_ge(pad_zero, 1)
            for n in range(4):
                copy_out(f"in{n}", lrux[:, n, CONV_LEFT:CONV_LEFT + S])
            for n in range(4, 8):
                copy_out(f"in{n}", mixT[:, n, :])
            for n in range(8, 12):
                copy_out(f"in{n}", mixT[:, n - 8, :])
            act_e.wait_ge(k_ready, 1)
            for c in range(CT):
                for d in range(2):
                    i, tile = 2 * c + d, gt[:, d, :, :]
                    if c:
                        act_e.wait_ge(lru_done, c)
                    for j in range(2):
                        name = f"lru{c}_{2 * d + j}"
                        full(act_e, name)
                        read(name, act_e.activation(tile[:, j, :], bank[jobs.bank(name)][:, :], ACT.Tanh, scale=0.5,
                                                    bias=hbias[:, (2 * d + j) * CT + c:(2 * d + j) * CT + c + 1]))
                    was_read(act_e, f"lru{c}_{2 * d}")
                    k = CT * d + c
                    act_e.activation(tile[:, 2, :], tile[:, 0, :], ACT.Exp, scale=kpos[:, k:k + 1], bias=kpos[:, k:k + 1])
                    act_e.activation(tile[:, 3, :], tile[:, 0, :], ACT.Tanh, scale=kneg[:, k:k + 1],
                                     bias=kneg[:, k:k + 1]).then_inc(acts_ready, 1)
                act_e.wait_ge(gelu_in, c + 1)
                act_e.activation(lrux[:, c, 0:S], lrux[:, c, 0:S], ACT.Tanh, scale=GELU_C).then_inc(gelu_tanh, 1)
                for d in range(2):
                    act_e.wait_ge(m2_ready, 2 * c + d + 1)
                    act_e.activation(gt[:, d, 3, :], gt[:, d, 3, :], ACT.Sqrt).then_inc(root_ready, 1)
                for half in range(2):
                    copy_out(f"four{c}_{half}", four[:, c, 2 * half:2 * half + 2, :].rearrange("p a b -> p (a b)"))
            for g in range(CT):
                copy_out(f"mix{g}", mixT[:, CT + g, :])

            for t in range(TT):
                was_read(act_e, f"out{2 * t + 1}")
                act_e.activation(nrm[:, t, :], xres[:, t, :], ACT.Square,
                                 accum_out=stat[:, 8 + t:9 + t]).then_inc(square_sum, 1)
            scaled("h2T", "g2")
            copy_out("logitT", logT, bank[jobs.bank("logitT")][:, 0:P])
            act_e.wait_ge(soft_in, 1)
            b = bank[jobs.bank("logits")]
            for t in range(TT):
                last = act_e.activation(aff[:, t, 0:NE], b[:, 32 * t:32 * t + NE], ACT.Exp, bias=stat[:, 16 + t:17 + t],
                                        accum_out=stat[:, 20 + t:21 + t])
                if t < TT - 1:
                    last.then_inc(soft_exp, 1)
            read("logits", last)
            copy_out("scoreT", score, bank[jobs.bank("scoreT")][0:NE, :])
            full(act_e, "posT")
            read("posT", act_e.activation(posT[:, :, 0:NE], bank[jobs.bank("posT")][:, 0:TT * NE].rearrange("p (t e) -> p t e", t=TT),
                                          ACT.Copy))

            with act_e.Fori(0, NE) as e:
                def filled(b, n):
                    act_e.wait_ge(bank_full[b], e * EF[b] + (moe_told[b] + n + 1))

                filled(0, 1)
                act_e.activation(flat(gselT), bank[0][:, :], ACT.Copy).then_inc(bank_read[0], 1)
                act_e.wait_ge(unit_used, e * E_UNITS + (B1_UNITS + 2 * KT - 1))
                for b in range(2):
                    act_e.activation(th[:, b, :], bank[1 + b][:, :], ACT.Tanh, scale=0.5).then_inc(tanh_ready, 1)
                for b in range(2):
                    filled(5 + b, 0)
                    act_e.activation(actT[:, 4 * b:4 * b + 4, :].rearrange("p a b -> p (a b)"), bank[5 + b][:, :],
                                     ACT.Copy).then_inc(bank_read[5 + b], 1)
                act_e.wait_ge(unit_used, e * E_UNITS + (B1_UNITS + E_UNITS))
                act_e.activation(eo, bank[7][:, :], ACT.Copy).then_inc(bank_read[7], 1)

            for t in range(TT):
                act_e.wait_ge(bank_read[(7, 2, 4, 6)[t]], jobs.before(f"yT{(7, 2, 4, 6)[t]}"))
                act_e.activation(nrm[:, t, :], xres[:, t, :], ACT.Square,
                                 accum_out=stat[:, 24 + t:25 + t]).then_inc(square_sum, 1)
            for t in range(TT):
                act_e.wait_ge(between, t + 1)
                act_e.activation(nrm[:, t, :], xres[:, t, :], ACT.Square,
                                 accum_out=stat[:, 32 + t:33 + t]).then_inc(square_sum, 1)
            scaled("yT", "gb2")
            act_e.wait_ge(prep_in, 1)
            act_e.activation(prep[:, 0, :], col("log_dt", 0, GP), ACT.Exp).then_inc(prep_exp, 1)
            act_e.wait_ge(prep_in, 2)
            act_e.activation(prep[:, 3, :], prep[:, 1, :], ACT.Exp).then_inc(prep_exp, 1)
            act_e.activation(prep[:, 4, :], prep[:, 1, :], ACT.Exp, scale=float(T8)).then_inc(prep_exp, 1)
            act_e.wait_ge(sin_arg, 1)
            act_e.activation(prep[:, 7, :], prep[:, 5, :], ACT.Sin, scale=0.5).then_inc(prep_sin, 1)
            act_e.activation(prep[:, 6, :], prep[:, 5, :], ACT.Sin).then_inc(prep_sin, 1)

            def staged(c):
                name = f"proj{c}"
                full(act_e, name)
                read(name, act_e.activation(uT[:, c, :, :],
                                            bank[jobs.bank(name)][:, :].rearrange("p (j t) -> p t j", t=T8), ACT.Copy))

            for c in range(CT):
                staged(c)
            for n in range(4):
                copy_out(f"proj{4 + n}", qT[:, n, :])
            for n in range(4):
                copy_out(f"proj{8 + n}", kT[:, n, :])
            for u in range(2):
                for t in range(TT):
                    name = f"v{u}_{t}"
                    copy_out(name, v_s[:, t, 256 * u:256 * u + 256], bank[jobs.bank(name)][:, 0:256])

            for i in range(STEPS):
                if i < HEADS:
                    for q in range(TT):
                        nk = (q + 1) * P
                        act_e.wait_ge(max_ready, TT * i + q + 1)
                        act_e.activation(att[:, q, 0:nk], att[:, q, 0:nk], ACT.Exp, bias=stat[:, 40 + q:41 + q],
                                         accum_out=stat[:, 44 + q:45 + q]).then_inc(exp_ready, 1)
                for n in range(2):
                    name, g = f"gate{2 * i + n}", 2 * i + n
                    full(act_e, name)
                    src = bank[jobs.bank(name)][:, :]
                    if g < 2 * CT:
                        dst = (zaT if g < CT else zsT)[:, g % CT, :]
                        act_e.activation(dst, src, ACT.Tanh, scale=0.5).then_inc(th_ready, 1)
                    else:
                        j = g - 2 * CT
                        dst = (gaT if j < KT else gsT)[:, j % KT, :]
                        if j == KT:
                            full(act_e, f"ssm{CT - 1}")
                        read(name, act_e.activation(dst, src, ACT.Tanh, scale=0.5, bias=hbias[:, 24 + j:25 + j]))
                if i < HEADS:
                    for b in range(3):
                        w = (4, 3, 3)[b] * P
                        name = f"probT{i}_{b}"
                        copy_out(name, pT[:, (0, 4, 7)[b] * P:(0, 4, 7)[b] * P + w], bank[jobs.bank(name)][:, 0:w])
                if i % 2 == 0 and i < 2 * CT:
                    for ri, name in enumerate(("st_re", "st_im")):
                        copy_out(f"{name}_{i // 2}", flat(st[:, ri, :, :]))
                if i % 2 == 0 and 2 <= i <= 2 * CT:
                    c = i // 2 - 1
                    if c:
                        act_e.wait_ge(y_out, 16 * T8 * c)
                    copy_out(f"ssm{c}", flat(ybuf))
                if i % 2 == 1 and i < 2 * CT:
                    copy_out(f"near{i // 2}", uT[:, i // 2, :, :].rearrange("p t j -> p (t j)"))
                if i == GELU_STEP:
                    for c in range(CT):
                        act_e.wait_ge(ygelu_in, c + 1)
                        act_e.activation(tmp[:, c % 2, :], tmp[:, c % 2, :], ACT.Tanh, scale=GELU_C).then_inc(ytanh, 1)
            for n in range(CT):
                name = f"glu{n}"
                if n == 0:
                    full(act_e, f"score{HEADS - 1}_{TT - 1}")
                full(act_e, name)
                read(name, act_e.activation(ysT[:, n, :], bank[jobs.bank(name)][:, :], ACT.Tanh, scale=0.25,
                                            bias=hbias[:, 16 + CT + n:17 + CT + n]))
            for t in range(TT):
                was_read(act_e, f"fin{2 * t + 1}")
                act_e.activation(nrm[:, t, :], xres[:, t, :], ACT.Square,
                                 accum_out=stat[:, 48 + t:49 + t]).then_inc(square_sum, 1)

        @block.gpsimd
        def _(pool):
            steps = [0]

            def link(ins):
                steps[0] += 1
                ins.then_inc(pool_step, 1)
                pool.wait_ge(pool_step, steps[0])

            def roots(n0, count0):
                for t in range(TT):
                    pool.wait_ge(square_sum, count0 + t + 1)
                    c = stat[:, n0 + t:n0 + t + 1]
                    link(pool.tensor_scalar(c, c, 1.0 / D, EPS, ALU.mult, ALU.add))
                    pool.tensor_tensor(stat[:, n0 + 4 + t:n0 + 5 + t], c, stat[:, 62:63], ALU.pow).then_inc(root_mean, 1)

            pool.memset(lrux, 0.0).then_inc(pad_zero, 1)
            link(pool.memset(stat[:, 62:63], -0.5))
            roots(0, 0)
            for c in range(CT):
                was_read(pool, f"in{8 + c}")
                pool.wait_ge(conv_ready, c + 1)
                g, xg = lrux[:, c, 0:S], mixT[:, c, :]
                link(pool.tensor_tensor(g, xg, xg, ALU.mult))
                link(pool.tensor_scalar(g, g, GELU_A, 1.0, ALU.mult, ALU.add))
                pool.tensor_tensor(g, g, xg, ALU.mult).then_inc(gelu_in, 1)
            pool.wait_ge(lru_done, CT)
            pool.dma_start(gfb, gf_d.partition_broadcast(P)).then_inc(gf_in, 16)
            roots(8, TT)
            roots(24, 2 * TT)
            pool.wait_ge(bank_full[6], moe_told[6] + NE * EF[6])
            pool.dma_start(bc.rearrange("p a g c -> p (a g c)"), bc_d).then_inc(bc_in, 16)
            roots(32, 3 * TT)
            full(pool, f"yT{KT - 1}")
            for h in range(HEADS):
                pool.dma_start(relb[:, h, :], bass.AP(tensor=relp.tensor, offset=h * (REL + P), ap=[[1, P], [1, REL]])
                               ).then_inc(rel_in, 16)
            for c in range(CT):
                was_read(pool, f"proj{c}")
            pool.dma_start(u_dram.rearrange("(c p) t j -> p c t j", p=P), uT).then_inc(u_out, 16)
            pool.wait_ge(u_out, 16)

            def inputs(c):
                for t in range(T8):
                    pool.dma_start(ubuf[t * SG:(t + 1) * SG, :, :],
                                   u_dram[c * P:(c + 1) * P, t, :].rearrange("(g c) j -> c g j", c=SG)).then_inc(u_in, 16)

            inputs(0)
            for c in range(CT):
                pool.wait_ge(pw_ready, 1)
                if c:
                    full(pool, f"ssm{c - 1}")
                cs = slice(c * CGP, (c + 1) * CGP)

                def steps_of(pw):
                    return pw[:, cs, ts].unsqueeze(3).to_broadcast([P, CGP, ts.stop - ts.start, SG])

                def chans_of(v):
                    return v[:, cs, :].unsqueeze(2).to_broadcast([P, CGP, ts.stop - ts.start, SG])

                for ts in (slice(0, T8), slice(T8, T8 + 1)):
                    wr, wi = (wc[:, k, :, ts.start * SG:ts.stop * SG].rearrange("p g (t c) -> p g t c", c=SG)
                              for k in range(2))
                    sc = flat(ybuf)[:, 0:CGP * (ts.stop - ts.start) * SG].rearrange("p (g t c) -> p g t c", g=CGP, c=SG)
                    pool.tensor_tensor(wr, steps_of(pw_re), chans_of(bc[:, 2, :, :]), ALU.mult)
                    link(pool.tensor_tensor(sc, steps_of(pw_in), chans_of(bc[:, 3, :, :]), ALU.mult))
                    link(pool.tensor_tensor(wr, wr, sc, ALU.add))
                    pool.tensor_tensor(wi, steps_of(pw_in), chans_of(bc[:, 2, :, :]), ALU.mult)
                    link(pool.tensor_tensor(sc, steps_of(pw_re), chans_of(bc[:, 3, :, :]), ALU.mult))
                    last = pool.tensor_tensor(wi, wi, sc, ALU.subtract)
                    if ts.stop == T8:
                        link(last)
                last.then_inc(wc_ready, 1)
                if c + 1 < CT:
                    full(pool, f"state{c}")
                    inputs(c + 1)
                was_read(pool, f"ssm{c}")
                for t in range(T8):
                    pool.dma_start(y_dram[c * P:(c + 1) * P, t, :].rearrange("(g c) j -> c g j", c=SG),
                                   ybuf[t * SG:(t + 1) * SG, :, :]).then_inc(y_out, 16)
                pool.wait_ge(y_out, 16 * T8 * (c + 1))
            full(pool, f"score{HEADS - 1}_{TT - 1}")
            pool.dma_start(yT, y_dram.rearrange("(c p) t j -> p c (t j)", p=P)).then_inc(y_in, 16)
            full(pool, f"pv{HEADS - 1}")
            pool.dma_start(gfin, gfin_d.partition_broadcast(P)).then_inc(gfin_in, 16)
            roots(48, 4 * TT)

        @block.vector
        def _(dve):
            steps = [0]

            def link(ins):
                steps[0] += 1
                ins.then_inc(dve_step, 1)
                dve.wait_ge(dve_step, steps[0])

            def tt(out_, a, b, op):
                return dve.tensor_tensor(out_, a, b, op)

            def stt(out_, a, s, b, op0, op1):
                return dve.scalar_tensor_tensor(out_, a, s, b, op0, op1)

            def normalise(n0, count0):
                for t in range(TT):
                    dve.wait_ge(root_mean, count0 + t + 1)
                    dve.tensor_scalar(nrm[:, t, :], xres[:, t, :], stat[:, n0 + 4 + t:n0 + 5 + t], None,
                                      ALU.mult).then_inc(normed, 1)

            dve.wait_ge(cols_in, 16)
            link(dve.tensor_scalar(kneg, col("lam", 0, 2 * CT), -1.0, None, ALU.mult))
            tt(kneg, kneg, col("lam", 0, 2 * CT), ALU.max).then_inc(halves, 1)
            dve.tensor_scalar(hbias[:, 0:4 * CT], col("bias_lru", 0, 4 * CT), 0.5, None, ALU.mult)
            dve.tensor_scalar(hbias[:, 4 * CT:4 * CT + 3 * KT], col("b_glu", 0, 3 * KT), 0.5, None, ALU.mult)
            normalise(0, 0)
            dve.wait_ge(lam_ln, 1)
            link(dve.tensor_scalar(kpos, col("lam", 0, 2 * CT), 0.0, None, ALU.min))
            link(tt(kpos, kpos, kneg, ALU.subtract))
            link(dve.tensor_scalar(kpos, kpos, LRU_C / 2, None, ALU.mult))
            dve.tensor_scalar(kneg, kpos, -1.0, None, ALU.mult).then_inc(k_ready, 1)
            for c in range(CT):
                was_read(dve, f"in{c}")
                o = conv[:, c, :]
                link(dve.tensor_scalar(o, lrux[:, c, 0:S], col("conv_w", c), col("conv_b", c), ALU.mult, ALU.add))
                for k in range(1, CONV):
                    last = stt(o, lrux[:, c, k:k + S], col("conv_w", k * CT + c), o, ALU.mult, ALU.add)
                    if k < CONV - 1:
                        link(last)
                last.then_inc(conv_ready, 1)
            for c in range(CT):
                for d in range(2):
                    dve.wait_ge(acts_ready, 2 * c + d + 1)
                    link(tt(gt[:, d, 0, :], gt[:, d, 2, :], gt[:, d, 2, :], ALU.mult))
                    stt(gt[:, d, 3, :], gt[:, d, 0, :], 1.0, gt[:, d, 3, :], ALU.add, ALU.mult).then_inc(m2_ready, 1)
                dve.wait_ge(conv_ready, c + 1)
                for d in range(2):
                    link(stt(gt[:, d, 1, :], gt[:, d, 1, :], 1.0, conv[:, c, :], ALU.add, ALU.mult))
                for d in range(2):
                    dve.wait_ge(root_ready, 2 * c + d + 1)
                    link(stt(gt[:, d, 1, :], gt[:, d, 3, :], 0.5, gt[:, d, 1, :], ALU.mult, ALU.mult))
                    a, b, h = gt[:, d, 2, :], gt[:, d, 1, :], gt[:, d, 0, :]
                    if d:
                        a, b, h = a[:, ::-1], b[:, ::-1], h[:, ::-1]
                    link(dve.tensor_tensor_scan(h, a, b, 0.0, ALU.mult, ALU.add))
                link(tt(gt[:, 0, 0, :], gt[:, 0, 0, :], gt[:, 1, 0, :], ALU.add))
                dve.wait_ge(gelu_tanh, c + 1)
                link(stt(mixT[:, c, :], lrux[:, c, 0:S], 1.0, mixT[:, c, :], ALU.add, ALU.mult))
                stt(mixT[:, c, :], mixT[:, c, :], 0.5, gt[:, 0, 0, :], ALU.mult, ALU.mult).then_inc(lru_done, 1)

            def residual(prefix, scale):
                for o in range(8):
                    name = f"{prefix}{o}"
                    r = xres[:, o // 2, o % 2 * 512:o % 2 * 512 + 512]
                    full(dve, name)
                    read(name, stt(r, bank[jobs.bank(name)][:, :], scale, r, ALU.mult, ALU.add))

            residual("out", 1.0)

            normalise(8, TT)
            full(dve, "logits")
            b = bank[jobs.bank("logits")]
            for t in range(TT):
                last = dve.tensor_reduce(stat[:, 16 + t:17 + t], b[:, 32 * t:32 * t + NE], AX, ALU.max, negate=True)
            last.then_inc(soft_in, 1)
            full(dve, f"mix{CT - 1}")
            dve.memset(aff[:, :, NE:NE + 1], 0.0)
            dve.memset(posT[:, :, NE:NE + 1], -1.0)
            dve.memset(ones, 1.0)
            for t in range(TT):
                if t < TT - 1:
                    dve.wait_ge(soft_exp, t + 1)
                else:
                    was_read(dve, "logits")
                last = dve.reciprocal(stat[:, 20 + t:21 + t], stat[:, 20 + t:21 + t])
            link(last)
            for t in range(TT):
                last = dve.tensor_scalar(aff[:, t, 0:NE], aff[:, t, 0:NE], stat[:, 20 + t:21 + t], None, ALU.mult)
            last.then_inc(aff_ready, 1)
            was_read(dve, "scoreT")
            for _ in range(CAP // 8):
                link(dve.max(top, score))
                link(dve.match_replace(score, top, score, -1.0))
            link(dve.tensor_scalar(taken, score, -0.5, None, ALU.is_lt))
            link(dve.tensor_tensor_scan(rank, ones, taken, 0.0, ALU.mult, ALU.add))
            link(tt(rank, rank, taken, ALU.mult))
            dve.tensor_scalar(rank, rank, -1.0, None, ALU.add).then_inc(pos_ready, 1)
            was_read(dve, "posT")

            def select(e):
                return tt(sel, posT[:, :, bass.ds(e, 1)].to_broadcast([P, TT, CAP]),
                          slotrow.unsqueeze(1).to_broadcast([P, TT, CAP]), ALU.is_equal)

            def gated(e):
                return tt(gsel, sel.unsqueeze(2).to_broadcast([P, TT, 2, CAP]),
                          aff[:, :, bass.ds(e, 1)].unsqueeze(3).to_broadcast([P, TT, 2, CAP]), ALU.mult)

            select(0).then_inc(sel_ready, 1)
            dve.wait_ge(sel_ready, 1)
            gated(0).then_inc(sel_ready, 1)

            with dve.Fori(0, NE) as e:
                def filled(b, n):
                    dve.wait_ge(bank_full[b], e * EF[b] + (moe_told[b] + n + 1))

                filled(0, 0)
                tt(xinT, bank[0][:, :].rearrange("p (k c) -> p k c", k=KT),
                   col("g2", 0, KT).unsqueeze(2).to_broadcast([P, KT, CAP]), ALU.mult).then_inc(bank_read[0], 1)
                for b in range(2):
                    dve.wait_ge(tanh_ready, 2 * e + (b + 1))
                    stt(th[:, b, :], th[:, b, :], 1.0, bank[1 + b][:, :], ALU.add, ALU.mult).then_inc(bank_read[1 + b], 1)
                dve.wait_ge(unit_used, e * E_UNITS + (B1_UNITS + 2 * KT))
                for b in range(2):
                    dve.wait_ge(bank_read[1 + b], e * EU[1 + b] + (moe_uses[1 + b] + 1))
                    stt(act[:, b, :], th[:, b, :], 0.5, bank[3 + b][:, :], ALU.mult, ALU.mult).then_inc(act_ready, 1)
                select(e + 1).then_inc(sel_ready, 1)
                filled(0, 1)
                dve.wait_ge(sel_ready, 2 * e + 3)
                gated(e + 1).then_inc(sel_ready, 1)
                for o, b in enumerate((0, 7, 1, 2, 3, 4, 5, 6)):
                    r = xres[:, o // 2, o % 2 * 512:o % 2 * 512 + 512]
                    filled(b, EF[b] - 1)
                    tt(r, r, bank[b][:, :], ALU.add).then_inc(bank_read[b], 1)

            dve.wait_ge(gf_in, 16)
            for t in range(TT):
                dve.wait_ge(root_mean, 2 * TT + t + 1)
                stt(xres[:, t, :], xres[:, t, :], stat[:, 28 + t:29 + t], gfb, ALU.mult, ALU.mult).then_inc(between, 1)
            normalise(32, 3 * TT)

            def p(n):
                return prep[:, n, :]

            def cmul(dst, a, b, s):
                tt(s[0], a[0], b[0], ALU.mult)
                tt(s[1], a[1], b[1], ALU.mult)
                tt(s[2], a[0], b[1], ALU.mult)
                link(tt(s[3], a[1], b[0], ALU.mult))
                tt(dst[0], s[0], s[1], ALU.subtract)
                link(tt(dst[1], s[2], s[3], ALU.add))

            dve.wait_ge(between, TT)
            link(dve.memset(flat(prep), 0.0))
            dve.memset(stat[:, 63:64], 0.0).then_inc(prep_in, 1)
            dve.wait_ge(prep_exp, 1)
            tt(p(1), col("a_re", 0, GP), p(0), ALU.mult)
            link(tt(p(2), col("a_im", 0, GP), p(0), ALU.mult))
            link(dve.tensor_scalar(p(5), p(2), 1 / TWO_PI, ROUND, ALU.mult, ALU.add))
            dve.tensor_scalar(p(5), p(5), -ROUND, None, ALU.add).then_inc(prep_in, 1)
            dve.wait_ge(prep_in, 2)
            link(stt(p(8), p(5), -PI_HI, p(2), ALU.mult, ALU.add))
            link(stt(p(8), p(5), -PI_MID, p(8), ALU.mult, ALU.add))
            link(stt(p(5), p(5), -PI_LO, p(8), ALU.mult, ALU.add))
            dve.tensor_scalar(p(5), p(5), -3.1415925, 3.1415925, ALU.max, ALU.min).then_inc(sin_arg, 1)
            dve.wait_ge(prep_exp, 3)
            dve.wait_ge(prep_sin, 2)
            link(tt(p(9), p(7), p(7), ALU.mult))
            link(dve.tensor_scalar(p(9), p(9), -2.0, 1.0, ALU.mult, ALU.add))
            dve.memset(pw_re[:, :, 0], 1.0)
            dve.memset(pw_im[:, :, 0], 0.0)
            tt(pw_re[:, :, 1], p(3), p(9), ALU.mult)
            link(tt(pw_im[:, :, 1], p(3), p(6), ALU.mult))
            link(dve.tensor_scalar(p(10), pw_re[:, :, 1], -1.0, None, ALU.add))
            are, aim, nim = col("a_re", 0, GP), col("a_im", 0, GP), pw_im[:, :, 1]
            tt(p(11), are, are, ALU.mult)
            tt(p(12), aim, aim, ALU.mult)
            tt(p(13), p(10), are, ALU.mult)
            tt(p(14), nim, aim, ALU.mult)
            tt(p(15), nim, are, ALU.mult)
            link(tt(p(16), p(10), aim, ALU.mult))
            tt(p(11), p(11), p(12), ALU.add)
            tt(p(13), p(13), p(14), ALU.add)
            link(tt(p(15), p(15), p(16), ALU.subtract))
            link(dve.reciprocal(p(11), p(11)))
            tt(p(13), p(13), p(11), ALU.mult)
            link(tt(p(15), p(15), p(11), ALU.mult))

            def per_chan(v):
                return v.unsqueeze(2).to_broadcast([P, GP, SG])

            dve.wait_ge(bc_in, 16)
            sc = [prot[:, i, :, 0:SG] for i in range(2)] + [prot[:, i, :, SG:2 * SG] for i in range(2)]
            cmul((bc[:, 0, :, :], bc[:, 1, :, :]), (bc[:, 0, :, :], bc[:, 1, :, :]),
                 (per_chan(p(13)), per_chan(p(15))), sc)
            link(dve.memset(bbd.rearrange("p a g c -> p (a g c)"), 0.0))
            for a in range(2):
                q = slice(64 * a, 64 * a + 64)
                for ri in range(2):
                    last = dve.tensor_copy(bbd[q, ri, :, a * SG:(a + 1) * SG], bc[q, ri, :, :])
            last.then_inc(bbd_ready, 1)
            for k in range(2, T8 + 1):
                cmul((pw_re[:, :, k], pw_im[:, :, k]), (pw_re[:, :, k - 1], pw_im[:, :, k - 1]),
                     (pw_re[:, :, 1], pw_im[:, :, 1]), [p(17), p(18), p(19), p(20)])
            dve.tensor_scalar(pw_in, pw_im, -1.0, None, ALU.mult)
            for _ in range(3):
                cmul((p(9), p(6)), (p(9), p(6)), (p(9), p(6)), [p(17), p(18), p(19), p(20)])
            dve.memset(rotc[:, :, 0:1], 1.0)
            link(dve.memset(rots[:, :, 0:1], 0.0))
            n = 1
            while n < NCH:
                ec = p(9).unsqueeze(2).to_broadcast([P, GP, n])
                es = p(6).unsqueeze(2).to_broadcast([P, GP, n])
                lo, hi = slice(0, n), slice(n, 2 * n)
                s0, s1 = prot[:, 0, :, 0:n], prot[:, 1, :, 0:n]
                tt(s0, rotc[:, :, lo], ec, ALU.mult)
                link(tt(s1, rots[:, :, lo], es, ALU.mult))
                link(tt(rotc[:, :, hi], s0, s1, ALU.subtract))
                tt(s0, rotc[:, :, lo], es, ALU.mult)
                link(tt(s1, rots[:, :, lo], ec, ALU.mult))
                link(tt(rots[:, :, hi], s0, s1, ALU.add))
                n *= 2
                if n < NCH:
                    cmul((p(9), p(6)), (p(9), p(6)), (p(9), p(6)), [p(17), p(18), p(19), p(20)])
            dve.tensor_copy(mag8, p(4))
            dve.memset(mem[:, ends["ybuf"]:ends["hbd"]], 0.0).then_inc(pw_ready, 1)
            dve.wait_ge(pw_ready, 1)

            def input_table(c):
                cs = slice(c * CGP, (c + 1) * CGP)

                def steps_of(pw):
                    return pw[:, cs, T8 - 1::-1].unsqueeze(3).to_broadcast([P, CGP, T8, SG])

                def chans_of(v):
                    return v[:, cs, :].unsqueeze(2).to_broadcast([P, CGP, T8, SG])

                wr, wi = (wext[:, i, :, :].rearrange("p g (t c) -> p g t c", t=T8) for i in range(2))
                s = tmp[:, 1, :].rearrange("p (g t c) -> p g t c", g=CGP, t=T8)
                tt(wr, steps_of(pw_re), chans_of(bc[:, 0, :, :]), ALU.mult)
                link(tt(s, steps_of(pw_im), chans_of(bc[:, 1, :, :]), ALU.mult))
                link(tt(wr, wr, s, ALU.subtract))
                tt(wi, steps_of(pw_re), chans_of(bc[:, 1, :, :]), ALU.mult)
                link(tt(s, steps_of(pw_im), chans_of(bc[:, 0, :, :]), ALU.mult))
                tt(wi, wi, s, ALU.add).then_inc(wext_ready, 1)

            def states(c):
                cs = slice(c * CGP, (c + 1) * CGP)
                name = f"state{c}"
                full(dve, name)
                b = bank[jobs.bank(name)]
                vr, vi = (b[:, i * 256:(i + 1) * 256].rearrange("p (g j) -> p g j", g=CGP) for i in range(2))
                t0, t1, t2, t3 = (tmp[:, i // 2, i % 2 * 256:i % 2 * 256 + 256].rearrange("p (g j) -> p g j", g=CGP)
                                  for i in range(4))
                rc, rs = rotc[:, cs, :], rots[:, cs, :]
                tt(t0, vr, rc, ALU.mult)
                tt(t1, vi, rs, ALU.mult)
                tt(t2, vi, rc, ALU.mult)
                tt(t3, vr, rs, ALU.mult).then_inc(bank_read[jobs.bank(name)], 1)
                was_read(dve, name)
                tt(t0, t0, t1, ALU.add)
                link(tt(t2, t2, t3, ALU.subtract))
                for g in range(CGP):
                    dc = mag8[:, c * CGP + g:c * CGP + g + 1].to_broadcast([P, NCH])
                    dve.tensor_tensor_scan(t1[:, g, :], dc, t0[:, g, :], 0.0, ALU.mult, ALU.add)
                    last = dve.tensor_tensor_scan(t3[:, g, :], dc, t2[:, g, :], 0.0, ALU.mult, ALU.add)
                link(last)
                tt(t0, t1, rc, ALU.mult)
                link(tt(t2, t3, rs, ALU.mult))
                for a in range(2):
                    q = slice(64 * a, 64 * a + 64)
                    last = tt(hbd[q, 0, :, a, 1:NCH], t0[q, :, 0:NCH - 1], t2[q, :, 0:NCH - 1], ALU.subtract)
                link(last)
                tt(t0, t1, rs, ALU.mult)
                link(tt(t2, t3, rc, ALU.mult))
                for a in range(2):
                    q = slice(64 * a, 64 * a + 64)
                    last = tt(hbd[q, 1, :, a, 1:NCH], t0[q, :, 0:NCH - 1], t2[q, :, 0:NCH - 1], ALU.add)
                last.then_inc(states_ready, 1)
                dve.wait_ge(states_ready, c + 1)

            input_table(0)
            dve.wait_ge(rel_in, 16 * HEADS)
            link(dve.memset(relb[0:CHUNK, :, 0:CHUNK], -1e30))

            def gelu_end(c):
                dve.wait_ge(ytanh, c + 1)
                stt(yT[:, c, :], tmp[:, c % 2, :], 1.0, yT[:, c, :], ALU.add, ALU.mult).then_inc(y_ready, 1)
                dve.wait_ge(y_ready, c + 1)

            for i in range(STEPS):
                if i < HEADS:
                    if i:
                        full(dve, f"probT{i - 1}_2")
                    for q in range(TT):
                        name, nk = f"score{i}_{q}", (q + 1) * P
                        full(dve, name)
                        b = bank[jobs.bank(name)]
                        near = min(nk, REL)
                        if nk > near:
                            dve.tensor_scalar(att[:, q, 0:nk - near], b[:, 0:nk - near], SCALE, col("rb_far", i),
                                              ALU.mult, ALU.add)
                        read(name, stt(att[:, q, nk - near:nk], b[:, nk - near:nk], SCALE, relb[:, i, 0:near][:, ::-1],
                                       ALU.mult, ALU.add))
                        was_read(dve, name)
                        dve.tensor_reduce(stat[:, 40 + q:41 + q], att[:, q, 0:nk], AX, ALU.max,
                                          negate=True).then_inc(max_ready, 1)
                    for q in range(TT):
                        nk = (q + 1) * P
                        dve.wait_ge(exp_ready, TT * i + q + 1)
                        link(dve.reciprocal(stat[:, 56 + q:57 + q], stat[:, 44 + q:45 + q]))
                        last = dve.tensor_scalar(att[:, q, 0:nk], att[:, q, 0:nk], stat[:, 56 + q:57 + q], None, ALU.mult)
                    last.then_inc(prob_ready, 1)
                for n in range(2):
                    g = 2 * i + n
                    if g < 2 * CT:
                        name = f"gate{g}"
                        dst = (zaT if g < CT else zsT)[:, g % CT, :]
                        dve.wait_ge(th_ready, g + 1)
                        read(name, stt(dst, dst, 1.0, bank[jobs.bank(name)][:, :], ALU.add, ALU.mult))
                if i % 2 == 1 and i < 2 * CT:
                    c, name = i // 2, f"lags_{i // 2}"
                    full(dve, name)
                    if c:
                        full(dve, f"near{c - 1}")
                    dve.tensor_scalar(kbd[:, T8, :], ident, col("skip", c), None, ALU.mult)
                    read(name, tt(kbd[:, 0:T8, :].rearrange("p d (g c) -> p d g c", g=CG),
                                  bank[jobs.bank(name)][:, 0:P].rearrange("p (d c) -> p d c", d=T8).unsqueeze(2)
                                  .to_broadcast([P, T8, CG, SG]),
                                  group_of.unsqueeze(1).unsqueeze(3).to_broadcast([P, T8, CG, SG]), ALU.mult))
                    was_read(dve, name)
                    dve.memset(stat[:, 63:64], 0.0).then_inc(kbd_ready, 1)
                if i < HEADS:
                    name, r = f"pv{i}", slice(64 * (i % 2), 64 * (i % 2) + 64)
                    full(dve, name)
                    was_read(dve, f"gate{i // 2}")
                    z = zaT[r, i // 2, :]
                    read(name, stt(z, bank[jobs.bank(name)][r, :], 0.5, z, ALU.mult, ALU.mult))
                if i == GELU_STEP:
                    for c in range(CT):
                        y, near, s = yT[:, c, :], uT[:, c, :, :].rearrange("p t j -> p (t j)"), tmp[:, c % 2, :]
                        dve.wait_ge(y_in, 16)
                        was_read(dve, f"near{c}")
                        link(tt(y, y, near, ALU.add))
                        link(tt(s, y, y, ALU.mult))
                        link(dve.tensor_scalar(s, s, GELU_A, 1.0, ALU.mult, ALU.add))
                        tt(s, s, y, ALU.mult).then_inc(ygelu_in, 1)
                        if c:
                            gelu_end(c - 1)
                    gelu_end(CT - 1)
                if i % 2 == 1 and i < 2 * CT:
                    states(i // 2)
                    if i // 2 + 1 < CT:
                        input_table(i // 2 + 1)
            for d in range(KT):
                name = f"ao{d}"
                full(dve, name)
                was_read(dve, f"gate{2 * CT + d}")
                read(name, stt(gaT[:, d, :], gaT[:, d, :], 1.0, bank[jobs.bank(name)][:, :], ALU.add, ALU.mult))
            for c in range(CT):
                name = f"glu{CT + c}"
                full(dve, name)
                read(name, dve.tensor_scalar(tmp[:, 0, :], bank[jobs.bank(name)][:, :], 0.5, col("b_glu", c),
                                             ALU.mult, ALU.add))
                was_read(dve, name)
                was_read(dve, f"glu{c}")
                link(stt(tmp[:, 1, :], ysT[:, c, :], 1.0, tmp[:, 0, :], ALU.add, ALU.mult))
                stt(ysT[:, c, :].rearrange("p (j t) -> p t j", t=T8), tmp[:, 1, :].rearrange("p (t j) -> p t j", t=T8),
                    0.25, zsT[:, c, :].rearrange("p (j t) -> p t j", t=T8), ALU.mult, ALU.mult).then_inc(glu_ready, 1)
            for d in range(KT):
                name = f"so{d}"
                full(dve, name)
                was_read(dve, f"gate{2 * CT + KT + d}")
                read(name, stt(gsT[:, d, :], gsT[:, d, :], 1.0, bank[jobs.bank(name)][:, :], ALU.add, ALU.mult))
                was_read(dve, name)
                was_read(dve, f"ao{d}")
                tt(gaT[:, d, :], gaT[:, d, :], gsT[:, d, :], ALU.add).then_inc(merged, 1)
            residual("fin", 0.5)
            dve.wait_ge(gfin_in, 16)
            for t in range(TT):
                dve.wait_ge(root_mean, 4 * TT + t + 1)
                stt(xres[:, t, :], xres[:, t, :], stat[:, 52 + t:53 + t], gfin, ALU.mult, ALU.mult).then_inc(final_ready, 1)


_INS = ["x", "cols", "cst", "wbd", "w_in", "dft_s", "w_out", "w_gate", "w_up", "w_down", "gf", "w_in2",
        "relp", "bc", "w_glu", "w_ao", "w_so", "w_out2", "gfin"]


def lay_out(i):
    f = {k: np.ascontiguousarray(np.asarray(v)) for k, v in i.items()}

    def tiles(v):
        return v.reshape(-1, P).T

    def pairs(v):
        return v.reshape(GP, 2, NS, -1).transpose(1, 2, 0, 3).reshape(P, GP, -1)

    bd = np.zeros((P, 4, CT, P), np.float32)
    for j, name in enumerate(("lru_wa_f", "lru_wx_f", "lru_wa_b", "lru_wx_b")):
        w = f[name].reshape(CT, 2, 64, 64)
        for a in range(2):
            bd[64 * a:64 * a + 64, j, :, 64 * a:64 * a + 64] = w[:, a].transpose(1, 0, 2)
    parts = {
        "g1": tiles(f["norm1_g"]), "g2": tiles(f["norm2_g"]), "gb2": tiles(f["norm_gain_2"][0]),
        "conv_w": tiles(f["conv_w"].reshape(-1)), "conv_b": tiles(f["conv_b"]),
        "bias_lru": np.concatenate([tiles(f[n]) for n in ("lru_ba_f", "lru_bx_f", "lru_ba_b", "lru_bx_b")], 1),
        "lam": np.concatenate([tiles(f["lru_lam_f"]), tiles(f["lru_lam_b"])], 1),
        "b_glu": tiles(f["b_glu_2"][0]), "gate_b": tiles(f["gate_bias_2"][0]),
        "a_re": pairs(f["ssm_a_re_2"][0])[:, :, 0], "a_im": pairs(f["ssm_a_im_2"][0])[:, :, 0],
        "log_dt": pairs(np.repeat(f["ssm_log_dt_2"][0][:, None], NS, 1))[:, :, 0],
        "skip": tiles(f["ssm_d_2"][0]),
        "rb_far": np.repeat(f["rel_bias_2"][0][:, NREL - 1][None], P, 0),
        "w_router": np.pad(f["w_router"].reshape(KT, P, NE).transpose(1, 0, 2), ((0, 0), (0, 0), (0, NE))).reshape(P, -1),
    }
    cols = np.concatenate([parts[n] for n, _ in COLS], 1)
    c_re, c_im = (f[n][0].transpose(0, 2, 1) for n in ("ssm_c_re_2", "ssm_c_im_2"))
    bc = np.stack([pairs(f["ssm_b_re_2"][0]), pairs(f["ssm_b_im_2"][0]), pairs(c_re), pairs(c_im)], 1)
    n = np.arange(P)
    ang = 2 * np.pi * (np.outer(n, n) % P) / P
    cst = np.concatenate([np.eye(P), np.cos(ang), np.sin(ang), np.tile(np.arange(CAP), (P, 1)),
                          np.arange(P)[:, None] // SG == np.arange(CG)[None]], 1).astype(np.float32)
    n = np.arange(S)
    ang = 2 * np.pi * (np.outer(n, n) % S) / S
    dft_s = (np.stack([np.cos(ang), -np.sin(ang)]) / np.sqrt(S * P)).astype(np.float32)
    return {
        "x": f["x"][0], "cols": cols, "cst": cst, "wbd": bd.reshape(P, -1), "w_in": f["w_in"], "dft_s": dft_s,
        "w_out": f["w_out"], "w_gate": f["w_gate"], "w_up": f["w_up"], "w_down": f["w_down"],
        "gf": f["normf_g"], "w_in2": f["w_in_2"][0],
        "relp": np.pad(f["rel_bias_2"][0], ((0, 0), (CHUNK, REL + P - CHUNK - NREL)), mode="edge"),
        "bc": bc.reshape(P, -1), "w_glu": f["w_glu_2"][0], "w_ao": f["w_attn_out_2"][0],
        "w_so": f["w_ssm_out_2"][0], "w_out2": f["w_out_2"][0], "gfin": f["final_gain_2"],
    }


def kernel(**inputs):
    import concourse.bacc as bacc
    from concourse.bass_utils import run_bass_kernel_spmd

    nc = bacc.Bacc("TRN2", target_bir_lowering=False, num_devices=1)
    arrays, args = {}, []
    for name, a in lay_out(inputs).items():
        a = np.ascontiguousarray(a)
        arrays[f"in_{name}"] = a
        args.append(nc.dram_tensor(f"in_{name}", a.shape, mybir.dt.from_np(a.dtype), kind="ExternalInput").ap())
    args.append(nc.dram_tensor("out", (S, D), f32, kind="ExternalOutput").ap())
    args.append(nc.dram_tensor("u_scratch", (LRU, T8, NCH), f32, kind="Internal").ap())
    args.append(nc.dram_tensor("y_scratch", (LRU, T8, NCH), f32, kind="Internal").ap())
    build(nc, *args)
    r = run_bass_kernel_spmd(nc, [arrays], core_ids=[0])
    return r.results[0]["out"].reshape(1, S, D)
```

```python
from contextlib import ExitStack

import numpy as np
import concourse.bass as bass
from concourse import mybir

f32, f32r = mybir.dt.float32, mybir.dt.float32r
ALU = mybir.AluOpType
ACT = mybir.ActivationFunctionType
AX = mybir.AxisListType.X

P = 128
S = 512
D = 1024
TT = S // P
KT = D // P
LRU = D // 2
CT = LRU // P
CONV = 4
CONV_LEFT = CONV // 2
NE = 16
CAP = 2 * S // NE
FF = 2 * D
EPS = 1e-6
GELU_C = 0.7978845608028654
GELU_A = 0.044715
LRU_C = 8.0

HEADS, DH = 8, 64
NREL, CHUNK = 192, 64
SCALE = DH ** -0.5
REL = 256
GRP, SG, NS = 32, 16, 64
T8 = P // SG
NCH = S // T8
GP = GRP // 2
CGP = GP // CT
CG = 2 * CGP
TWO_PI = 2 * np.pi
PI_HI = 6.28125
PI_MID = float(np.float32(np.round((TWO_PI - PI_HI) * 2 ** 20) / 2 ** 20))
PI_LO = float(np.float32(TWO_PI - PI_HI - PI_MID))
ROUND = 1.5 * 2 ** 23

SBUF = 53200
UNIT = 2048
RING = 12
RING2 = 3
B1_UNITS = 13
E_UNITS = 24
MOE_END = B1_UNITS + NE * E_UNITS

COLS = [("g1", KT), ("g2", KT), ("gb2", KT), ("conv_w", CONV * CT), ("conv_b", CT),
        ("bias_lru", 4 * CT), ("lam", 2 * CT), ("b_glu", KT), ("gate_b", 2 * KT),
        ("a_re", GP), ("a_im", GP), ("log_dt", GP), ("skip", CT), ("rb_far", HEADS),
        ("w_router", KT * 2 * NE)]
COL, NCOLS = {}, 0
for _name, _w in COLS:
    COL[_name] = NCOLS
    NCOLS += _w
NCST = 3 * P + CAP + CG


class Jobs:

    def __init__(self, bank_full, unit_used):
        self.bank_full, self.unit_used = bank_full, unit_used
        self.uses, self.told, self.of, self.turn = [0] * 8, [0] * 8, {}, 0

    def add(self, name, bank=None, unit=None):
        if bank is None:
            bank = self.turn
            self.turn = (self.turn + 1) % 8
        if unit is None:
            self.told[bank] += 1
            end = (self.bank_full[bank], self.told[bank])
        else:
            end = (self.unit_used, unit + 1)
        self.of[name] = (bank, self.uses[bank], end)
        self.uses[bank] += 1

    def bank(self, name):
        return self.of[name][0]

    def before(self, name):
        return self.of[name][1]

    def end(self, name):
        return self.of[name][2]


def build(nc, x, cols_d, cst_d, wbd_d, w_in, dft_s, w_out, w_gate, w_up, w_down, gf_d, w_in2, relp,
          bc_d, w_glu, w_ao, w_so, w_out2, gfin_d, out, u_dram, y_dram, x_dram):
    with ExitStack() as ctx:
        base = (nc.sbuf_base + 31) // 32 * 32
        ends = {}

        def area(name, off, *shape, parts=P, dtype=f32):
            n = int(np.prod(shape))
            assert off >= 0 and off + n <= SBUF, (name, off + n)
            ends[name] = off + -(-n // 8) * 8
            v = nc.alloc_sbuf_tensor_at(name, [P, n], dtype, offset=base + 4 * off)[0:parts, :]
            if len(shape) == 1:
                return v
            letters = "abcd"[:len(shape)]
            return v.rearrange(f"p ({' '.join(letters)}) -> p {' '.join(letters)}",
                               **dict(zip(letters[1:], shape[1:])))

        def area_r(name, off, *shape):
            return area(name, off, *shape, dtype=f32r)

        def flat(v):
            return v.rearrange("p a b -> p (a b)")

        ring = [area(f"ring{s}", s * UNIT, UNIT) for s in range(RING)]
        ring_r = [area_r(f"ring{s}_r", s * UNIT, UNIT) for s in range(RING)]
        xres = area("xres", RING * UNIT, TT, D)
        nrm = area("nrm", ends["xres"], TT, D)
        hT = area("hT", ends["nrm"], KT, S)
        hT_hi = area_r("hT_hi", ends["nrm"], KT, S)
        hT_lo = area_r("hT_lo", ends["xres"], KT, S)
        cols = area("cols", ends["hT"], NCOLS)
        cst = area("cst", ends["cols"], NCST)
        stat = area("stat", ends["cst"], 64)
        hbias = area("hbias", ends["stat"], 4 * CT + 3 * KT)
        kpos = area("kpos", ends["hbias"], 2 * CT)
        kneg = area("kneg", ends["kpos"], 2 * CT)
        Z = ends["kneg"]
        ident, dft, slotrow = cst[:, 0:P], cst[:, P:3 * P], cst[:, 3 * P:3 * P + CAP]
        group_of = cst[:, 3 * P + CAP:NCST]

        def col(name, i=0, n=1):
            return cols[:, COL[name] + i:COL[name] + i + n]

        mixT = area("mixT", Z, 2 * CT, S)
        lrux = area("lrux", ends["mixT"], CT, S + CONV)
        conv = area("conv", ends["lrux"], CT, S)
        gt = area("gt", ends["conv"], 2, 4, S)
        hi_b1 = [area_r(f"hi{i}", ends["conv"] + i * UNIT, UNIT) for i in range(2)]
        mix_hi = hT_hi
        mix_lo = area_r("mix_lo", Z, 2 * CT, S)
        four = flat(nrm).rearrange("p (t g c) -> p t g c", t=TT, g=CT)
        aff = area("aff", Z, TT, NE + 1)
        posT = area("posT", ends["aff"], TT, NE + 1)
        sel = area("sel", ends["posT"], TT, CAP)
        gsel = area("gsel", ends["sel"], TT, 2, CAP)
        gselT = area("gselT", ends["gsel"], TT, P)
        xinT = area("xinT", ends["gselT"], KT, CAP)
        th = area("th", ends["xinT"], 2, 512)
        act = area("act", ends["th"], 2, 512)
        actT = area("actT", ends["act"], KT, P)
        eo = area("eo", ends["actT"], 512)
        score = area("score", ends["eo"], S, parts=NE)
        top = area("top", ends["score"], 8, parts=NE)
        taken = area("taken", ends["top"], S, parts=NE)
        rank = area("rank", ends["taken"], S, parts=NE)
        ones = area("ones", ends["rank"], S, parts=NE)
        logT = area("logT", ends["ones"], P)
        qT = area("qT", 0, CT, S)
        kT = area("kT", (RING2 + 3) * UNIT, CT, S)
        v_s = area("v_s", ends["kT"], TT, LRU)
        zaT = area("zaT", ends["v_s"], CT, S)
        zsT = area("zsT", ends["zaT"], CT, S)
        gaT = area("gaT", ends["zsT"], KT, S)
        assert ends["gaT"] <= RING * UNIT
        hi_b2 = [ring_r[RING2 + 1 + i] for i in range(2)]
        att = area("att", RING * UNIT, TT, S)
        relb = area("relb", ends["att"], HEADS, REL)
        assert ends["relb"] <= ends["xres"]
        pT = area("pT", Z, 10 * P)
        gfin = area("gfin", Z, D)
        rotc = area("rotc", ends["pT"], GP, NCH)
        rots = area("rots", ends["rotc"], GP, NCH)
        mag8 = area("mag8", ends["rots"], GP)
        pw_re = area("pw_re", ends["mag8"], GP, T8 + 1)
        pw_im = area("pw_im", ends["pw_re"], GP, T8 + 1)
        pw_in = area("pw_in", ends["pw_im"], GP, T8 + 1)
        bc = area("bc", ends["pw_in"], 4, GP, SG)
        bbd = area("bbd", ends["bc"], 2, GP, 2 * SG)
        uT = area("uT", ends["bbd"], CT, T8, NCH)
        ubuf = area("ubuf", ends["uT"], CG, NCH)
        ybuf = area("ybuf", ends["ubuf"], CG, NCH)
        hbd = area("hbd", ends["ybuf"], 2, CGP, 2, NCH)
        tmp = area("tmp", ends["hbd"], 2, 512)
        wext = area("wext", ends["tmp"], 2, CGP, P)
        wc = area("wc", ends["wext"], 2, CGP, (T8 + 1) * SG)
        st = area("st", ends["wc"], 2, CGP, P)
        kbd = area("kbd", ends["st"], T8 + 1, P)
        gsT = area("gsT", ends["tmp"], KT, S)
        gfb = area("gfb", ends["tmp"], D)
        prep = area("prep", ends["wext"], 24, GP)
        prot = area("prot", ends["prep"], 2, GP, NCH // 2)
        assert ends["gsT"] <= ends["kbd"] and ends["prot"] <= ends["kbd"] and ends["gfb"] <= ends["wext"]
        za_hi = area_r("za_hi", ends["pT"], CT, S)
        y_hi = area_r("y_hi", ends["za_hi"], CT, S)
        ga_hi = area_r("ga_hi", ends["pT"], KT, S)
        ys_hi = area_r("ys_hi", ends["bbd"], CT, S)
        za_lo, y_lo, ys_lo, ga_lo = (area_r(f"{n}_lo", ends[n] - w * S, w, S)
                                     for n, w in (("zaT", CT), ("qT", CT), ("kT", CT), ("gaT", KT)))
        assert ends["ga_hi"] <= ends["bbd"]
        yT = qT
        ysT = kT

        bank = [ctx.enter_context(nc.psum_tensor(f"bank{b}", [P, 512], f32)) for b in range(8)]

        def sem(name):
            return ctx.enter_context(nc.semaphore(name))

        ring_full = [sem(f"ring_full{s}") for s in range(RING)]
        unit_used = sem("unit_used")
        w_hi, w_lo = sem("w_hi"), sem("w_lo")
        hi_ready, lo_ready = sem("hi_ready"), sem("lo_ready")
        x_saved, x_back = sem("x_saved"), sem("x_back")
        bank_full = [sem(f"bank_full{b}") for b in range(8)]
        bank_read = [sem(f"bank_read{b}") for b in range(8)]
        x_in = [sem(f"x_in{t}") for t in range(TT)]
        cols_in, cst_in, gf_in, rel_in = sem("cols_in"), sem("cst_in"), sem("gf_in"), sem("rel_in")
        bc_in, gfin_in = sem("bc_in"), sem("gfin_in")
        dve_step, act_step, pool_step = sem("dve_step"), sem("act_step"), sem("pool_step")
        square_sum, root_mean, normed = sem("square_sum"), sem("root_mean"), sem("normed")
        pad_zero, halves, lam_exp, lam_ln, k_ready = (
            sem("pad_zero"), sem("halves"), sem("lam_exp"), sem("lam_ln"), sem("k_ready"))
        conv_ready, acts_ready, m2_ready, root_ready, lru_done = (
            sem("conv_ready"), sem("acts_ready"), sem("m2_ready"), sem("root_ready"), sem("lru_done"))
        gelu_in, gelu_tanh, gelu_done = sem("gelu_in"), sem("gelu_tanh"), sem("gelu_done")
        soft_in, soft_exp, aff_ready, pos_ready = (
            sem("soft_in"), sem("soft_exp"), sem("aff_ready"), sem("pos_ready"))
        sel_ready, tanh_ready, act_ready = sem("sel_ready"), sem("tanh_ready"), sem("act_ready")
        u_out, u_in, y_out, y_in = sem("u_out"), sem("u_in"), sem("y_out"), sem("y_in")
        prep_in, prep_exp, prep_sin, sin_arg = (
            sem("prep_in"), sem("prep_exp"), sem("prep_sin"), sem("sin_arg"))
        wext_ready, wc_ready, pw_ready, states_ready = (
            sem("wext_ready"), sem("wc_ready"), sem("pw_ready"), sem("states_ready"))
        bbd_ready, kbd_ready, ygelu_in, ytanh, y_ready = (
            sem("bbd_ready"), sem("kbd_ready"), sem("ygelu_in"), sem("ytanh"), sem("y_ready"))
        max_ready, exp_ready, prob_ready = sem("max_ready"), sem("exp_ready"), sem("prob_ready")
        th_ready, glu_ready, merged = sem("th_ready"), sem("glu_ready"), sem("merged")
        between, final_ready, stored = sem("between"), sem("final_ready"), sem("stored")

        jobs = Jobs(bank_full, unit_used)
        for k in range(KT):
            jobs.add(f"xT{k}", k)
        for n in range(12):
            jobs.add(f"in{n}", unit=n // 2 if n % 2 else None)
        for c in range(CT):
            for i in range(4):
                jobs.add(f"lru{c}_{i}", unit=6 if (c, i) == (CT - 1, 3) else None)
            for half in range(2):
                jobs.add(f"four{c}_{half}")
        for g in range(CT):
            jobs.add(f"mix{g}", unit=8 if g == CT - 1 else None)
        for o in range(8):
            jobs.add(f"out{o}", unit=12 if o == 7 else None)
        for k in range(KT):
            jobs.add(f"h2T{k}", k)
        jobs.add("logitT", 0)
        jobs.add("logits", 1)
        jobs.add("scoreT", 2)
        jobs.add("posT", 3)
        moe_uses, moe_told = list(jobs.uses), list(jobs.told)
        EU = [3, 2, 2, 1, 1, 2, 2, 2]
        EF = [3, 1, 1, 1, 1, 2, 2, 1]
        for b in range(8):
            jobs.uses[b] += NE * EU[b]
            jobs.told[b] += NE * EF[b]
        for k in range(KT):
            jobs.add(f"yT{k}", k)
        M = MOE_END
        for n in range(12):
            jobs.add(f"proj{n}", unit=M + n // 2 if n % 2 else None)
        for u in range(2):
            for t in range(TT):
                jobs.add(f"v{u}_{t}", unit=M + 6 + u if t == TT - 1 else None)
        GELU_STEP = 2 * CT + 1
        STEPS = 12
        for i in range(STEPS):
            if i < HEADS:
                for q in range(TT):
                    jobs.add(f"score{i}_{q}")
            for n in range(2):
                jobs.add(f"gate{2 * i + n}", unit=M + 8 + i if n else None)
            if i % 2 == 1 and i < 2 * CT:
                jobs.add(f"lags_{i // 2}")
            if i < HEADS:
                for b in range(3):
                    jobs.add(f"probT{i}_{b}")
                jobs.add(f"pv{i}")
            if i % 2 == 0 and 2 <= i <= 2 * CT:
                jobs.add(f"ssm{i // 2 - 1}")
            if i % 2 == 0 and i < 2 * CT:
                for name in ("st_re", "st_im"):
                    jobs.add(f"{name}_{i // 2}")
            if i % 2 == 1 and i < 2 * CT:
                jobs.add(f"state{i // 2}")
                jobs.add(f"near{i // 2}")
        for n in range(8):
            jobs.add(f"glu{n}", unit=M + 20 + n // 4 if n % 4 == 3 else None)
        for d in range(KT):
            jobs.add(f"ao{d}", unit=M + 22 + d // 4 if d % 4 == 3 else None)
        for d in range(KT):
            jobs.add(f"so{d}", unit=M + 24 + d // 4 if d % 4 == 3 else None)
        for o in range(8):
            jobs.add(f"fin{o}", unit=M + 29 if o == 7 else None)

        def full(eng, name):
            eng.wait_ge(*jobs.end(name))

        def was_read(eng, name):
            eng.wait_ge(bank_read[jobs.bank(name)], jobs.before(name) + 1)

        def read(name, ins):
            ins.then_inc(bank_read[jobs.bank(name)], 1)

        def slot_of(unit):
            return unit % RING if unit < MOE_END else 1 + (unit - MOE_END) % RING2

        loads_b1 = [sum(u % RING == s for u in range(B1_UNITS)) for s in range(RING)]

        def loaded(eng, unit):
            s = slot_of(unit)
            if unit < MOE_END:
                n = unit // RING + 1
            else:
                n = loads_b1[s] + 2 * NE + (unit - MOE_END) // RING2 + 1
            eng.wait_ge(ring_full[s], 16 * n)

        def view(unit, inner):
            return ring[slot_of(unit)].rearrange("p (k n) -> p k n", n=inner)

        split_units = [*range(6), *range(9, 13), *range(M, M + 30)]
        split_tiles = [f"{n}{k}" for n, w in (("xT", KT), ("lru", CT), ("mix", CT), ("yT", KT), ("za", CT), ("y", CT),
                                              ("ys", CT), ("ga", KT)) for k in range(w)]
        in_sbuf = [t for t in split_tiles if t not in jobs.of]

        def hi_of(unit):
            if unit >= M:
                return hi_b2[(unit - M) % 2]
            return hi_b1[unit % 2 if unit < 6 else (unit - 9) % 2]

        def high_stands(eng, tile):
            eng.wait_ge(hi_ready, split_tiles.index(tile) + 1)

        def both_stand(eng, tile):
            if tile in jobs.of:
                was_read(eng, tile)
            else:
                eng.wait_ge(lo_ready, in_sbuf.index(tile) + 1)

        def view_r(v, inner):
            return v.rearrange("p (k n) -> p k n", n=inner)

        def both(unit, inner):
            return view_r(hi_of(unit), inner), view_r(ring_r[slot_of(unit)], inner)

        block = ctx.enter_context(nc.Block())

        @block.sync
        def _(sp):
            def load(unit, src, inner):
                s = slot_of(unit)
                if unit >= MOE_END:
                    v = unit - MOE_END
                    last = max(u for u in range(MOE_END - RING, MOE_END) if u % RING == s) if v < RING2 else unit - RING2
                    sp.wait_ge(unit_used, last + 1)
                elif unit >= RING:
                    sp.wait_ge(unit_used, unit - RING + 1)
                sp.dma_start(view(unit, inner), src).then_inc(ring_full[s], 16)

            for t in range(TT):
                sp.dma_start(xres[:, t, :], x[t * P:(t + 1) * P, :]).then_inc(x_in[t], 16)
            w_in_k = w_in.rearrange("(k p) n -> p k n", p=P)
            for u, c in enumerate((0, 1, 4, 5, 2, 3)):
                load(u, w_in_k[:, :, 256 * c:256 * c + 256], 256)
            load(6, wbd_d.rearrange("p (k n) -> p k n", n=P), P)
            for i in range(2):
                load(7 + i, dft_s[i].rearrange("(k p) n -> p k n", p=P), S)
            w_out_m = w_out.rearrange("(m p) n -> p m n", p=P)
            for u, m in enumerate((4, 6, 0, 2)):
                load(9 + u, w_out_m[:, m:m + 2, :], D)

            with sp.Fori(0, NE) as e:
                for m in range(E_UNITS):
                    s = (B1_UNITS + m) % RING
                    if m < KT * 2:
                        w, k = (w_gate, w_up)[m % 2], m // 2
                        src = w[bass.ds(e, 1), k * P:(k + 1) * P, :].rearrange("a p n -> p (a n)")
                        dst = ring[s]
                    else:
                        j = m - 2 * KT
                        src = w_down[bass.ds(e, 1), 2 * j * P:(2 * j + 2) * P, :].rearrange(
                            "a (i p) n -> p (a i) n", i=2)
                        dst = ring[s].rearrange("p (i n) -> p i n", i=2)
                    sp.wait_ge(unit_used, e * E_UNITS + (B1_UNITS + m - RING + 1))
                    sp.dma_start(dst, src).then_inc(ring_full[s], 16)

            w2 = w_in2.rearrange("(k p) n -> p k n", p=P)
            order = [8, 9, 0, 1, 2, 3, 4, 5, 6, 7, 10, 11] + list(range(12, 20))
            for u, c in enumerate(order):
                load(MOE_END + u, w2[:, :, 256 * c:256 * c + 256], 256)
                if u == RING2 - 1:
                    for t in range(TT):
                        sp.wait_ge(between, t + 1)
                        sp.dma_start(x_dram[t * P:(t + 1) * P, :], xres[:, t, :]).then_inc(x_saved, 16)
            sp.wait_ge(x_saved, 16 * TT)
            sp.wait_ge(*jobs.end(f"pv{HEADS - 1}"))
            sp.dma_start(xres, x_dram.rearrange("(t p) n -> p t n", p=P)).then_inc(x_back, 16)
            for i in range(2):
                load(MOE_END + 20 + i,
                     w_glu.rearrange("(k p) n -> p k n", p=P)[:, :, 512 * (1 - i):512 * (1 - i) + 512], 512)
            for i in range(2):
                load(MOE_END + 22 + i, w_ao.rearrange("(k p) n -> p k n", p=P)[:, :, 512 * i:512 * i + 512], 512)
            for i in range(2):
                load(MOE_END + 24 + i, w_so.rearrange("(k p) n -> p k n", p=P)[:, :, 512 * i:512 * i + 512], 512)
            for i in range(4):
                load(MOE_END + 26 + i, w_out2.rearrange("(m p) n -> p m n", p=P)[:, 2 * i:2 * i + 2, :], D)

            for t in range(TT):
                sp.wait_ge(final_ready, t + 1)
                sp.dma_start(out[t * P:(t + 1) * P, :], xres[:, t, :]).then_inc(stored, 16)
            sp.wait_ge(stored, 16 * TT)

        @block.tensor
        def _(pe):
            def start(name, **kw):
                b = jobs.bank(name)
                if jobs.before(name):
                    pe.wait_ge(bank_read[b], jobs.before(name))
                return bank[b]

            def finish(name, ins):
                who, _ = jobs.end(name)
                ins.then_inc(who, 1)

            def transposes(prefix, ready0):
                for t in range(TT):
                    pe.wait_ge(normed, ready0 + t + 1)
                    for k in range(KT):
                        b = start(f"{prefix}{k}") if t == 0 else bank[k]
                        last = pe.transpose(b[:, t * P:(t + 1) * P], nrm[:, t, k * P:(k + 1) * P], ident)
                        if t == TT - 1:
                            finish(f"{prefix}{k}", last)

            def split(unit):
                pe.wait_ge(w_lo, split_units.index(unit) + 1)

            def product(dst, a, b, first, last):
                pe.matmul(dst, a[0], b[1], start=first, stop=False)
                pe.matmul(dst, a[1], b[0], start=False, stop=False)
                return pe.matmul(dst, a[0], b[0], start=False, stop=last)

            def project(name, w, c0, rows, kn, tiles=None):
                if tiles is None:
                    b = start(name)
                for k in range(kn):
                    if tiles is not None:
                        both_stand(pe, f"{tiles}{k}")
                        if k == 0:
                            b = start(name)
                    last = product(b[:, :], [v[:, k, c0:c0 + P] for v in w], [v[:, k, :] for v in rows],
                                   k == 0, k == kn - 1)
                finish(name, last)

            def out_project(prefix, rows, unit0, ms, rows_ready):
                for u, m0 in enumerate(ms):
                    unit = unit0 + u
                    for m in range(m0, m0 + 2):
                        both_stand(pe, rows_ready(m))
                    split(unit)
                    w = both(unit, D)
                    tail = u == len(ms) - 1
                    for o in range(8):
                        t, n = o // 2, o % 2
                        b = start(f"{prefix}{o}") if u == 0 else bank[jobs.bank(f"{prefix}{o}")]
                        for i in range(2):
                            last = product(b[:, :], [v[:, m0 + i, t * P:(t + 1) * P] for v in rows],
                                           [v[:, i, n * 512:n * 512 + 512] for v in w], u == 0 and i == 0, tail and i == 1)
                        if tail:
                            finish(f"{prefix}{o}", last)
                    if not tail:
                        last.then_inc(unit_used, 1)

            pe.wait_ge(cst_in, 16)
            transposes("xT", 0)
            for n in range(12):
                if n % 2 == 0:
                    split(n // 2)
                project(f"in{n}", both(n // 2, 256), (n % 2) * P, (hT_hi, hT_lo), KT, None if n else "xT")
            loaded(pe, 6)
            wbd = view(6, P)
            for c in range(CT):
                pe.wait_ge(conv_ready, c + 1)
                for i in range(4):
                    b = start(f"lru{c}_{i}")
                    finish(f"lru{c}_{i}", pe.matmul(b[:, :], wbd[:, 4 * i + c, :], conv[:, c, :], start=True, stop=True))
                if c == 0:
                    for g in range(CT):
                        was_read(pe, f"in{4 + g}")
                for half in range(2):
                    b = start(f"four{c}_{half}")
                    for i in range(2):
                        g = 2 * half + i
                        last = pe.matmul(b[:, 256 * i:256 * i + 256], mixT[:, CT + g, c * P:(c + 1) * P], dft,
                                         start=True, stop=True)
                    finish(f"four{c}_{half}", last)
            loaded(pe, 7)
            loaded(pe, 8)
            for c in range(CT):
                for half in range(2):
                    was_read(pe, f"four{c}_{half}")
            for g in range(CT):
                b = start(f"mix{g}")
                for i in range(2):
                    w = view(7 + i, S)
                    for t in range(TT):
                        last = pe.matmul(b[:, :], four[:, t, g, i * P:(i + 1) * P], w[:, t, :],
                                         start=(i == 0 and t == 0), stop=(i == 1 and t == TT - 1))
                    if i == 0 and g == CT - 1:
                        last.then_inc(unit_used, 1)
                finish(f"mix{g}", last)
            out_project("out", (mix_hi, mix_lo), 9, (4, 6, 0, 2),
                        lambda m: f"mix{m - CT}" if m >= CT else f"lru{m}")

            transposes("h2T", TT)
            for k in range(KT):
                was_read(pe, f"h2T{k}")
            b = start("logitT")
            wr = col("w_router", 0, KT * 2 * NE).rearrange("p (k e) -> p k e", k=KT)
            for k in range(KT):
                for t in range(TT):
                    last = pe.matmul(b[32 * t:32 * t + 32, 0:P], wr[:, k, :], hT[:, k, t * P:(t + 1) * P],
                                     start=(k == 0), stop=(k == KT - 1))
            finish("logitT", last)
            was_read(pe, "logitT")
            b = start("logits")
            finish("logits", pe.transpose(b[:, 0:P], logT, ident))
            pe.wait_ge(aff_ready, 1)
            b = start("scoreT")
            for t in range(TT):
                last = pe.transpose(b[0:NE, t * P:(t + 1) * P], aff[:, t, 0:NE], ident)
            finish("scoreT", last)
            pe.wait_ge(pos_ready, 1)
            b = start("posT")
            for t in range(TT):
                last = pe.transpose(b[:, t * NE:(t + 1) * NE], rank[:, t * P:(t + 1) * P], ident[0:NE, 0:NE])
            finish("posT", last)

            with pe.Fori(0, NE) as e:
                def bank_free(b, n):
                    pe.wait_ge(bank_read[b], e * EU[b] + (moe_uses[b] + n))

                def arrived(m):
                    s = (B1_UNITS + m) % RING
                    pe.wait_ge(ring_full[s], e * 32 + 16 * (loads_b1[s] + m // RING + 1))

                pe.wait_ge(sel_ready, 2 * e + 1)
                bank_free(0, 0)
                for k in range(KT):
                    for t in range(TT):
                        last = pe.matmul(bank[0][:, k * CAP:(k + 1) * CAP], nrm[:, t, k * P:(k + 1) * P], sel[:, t, :],
                                         start=(t == 0), stop=(t == TT - 1))
                last.then_inc(bank_full[0], 1)
                pe.wait_ge(sel_ready, 2 * e + 2)
                bank_free(0, 1)
                for t in range(TT):
                    last = pe.transpose(bank[0][:, t * P:(t + 1) * P], gsel[:, t, :, :].rearrange("p a b -> p (a b)"), ident)
                last.then_inc(bank_full[0], 1)
                for b in range(1, 5):
                    bank_free(b, 0)
                for m in range(2 * KT):
                    arrived(m)
                    k, w = m // 2, ring[(B1_UNITS + m) % RING]
                    for q in range(4):
                        o = 64 * (q % 2)
                        last = pe.matmul(bank[1 + 2 * (m % 2) + q // 2][o:o + 64, :], xinT[:, k, :],
                                         w[:, q * 512:(q + 1) * 512], start=(k == 0), stop=(k == KT - 1))
                    last.then_inc(unit_used, 1)
                for b in range(2):
                    pe.wait_ge(act_ready, 2 * e + (b + 1))
                    bank_free(5 + b, 0)
                    for q in range(4):
                        last = pe.transpose(bank[5 + b][:, q * P:(q + 1) * P], act[:, b, q * P:(q + 1) * P], ident)
                    last.then_inc(bank_full[5 + b], 1)
                bank_free(5, 1)
                bank_free(6, 1)
                bank_free(7, 0)
                for j in range(8):
                    arrived(2 * KT + j)
                    w = ring[(B1_UNITS + 2 * KT + j) % RING].rearrange("p (i n) -> p i n", i=2)
                    for i in range(2):
                        kt = 2 * j + i
                        at = 64 * (kt // 4 % 2)
                        for n in range(2):
                            last = pe.matmul(bank[7][64 * n:64 * n + 64, :], actT[:, kt // 8 * 4 + kt % 4, at:at + 64],
                                             w[:, i, n * 512:n * 512 + 512], start=(kt == 0), stop=(kt == 15))
                    last.then_inc(unit_used, 1)
                for o, b in enumerate((0, 7, 1, 2, 3, 4, 5, 6)):
                    t, n = o // 2, o % 2
                    if o == 0:
                        bank_free(7, 1)
                    bank_free(b, EU[b] - 1)
                    pe.matmul(bank[b][:, :], gselT[64 * n:64 * n + 64, t, :], eo[64 * n:64 * n + 64, :],
                              start=True, stop=True).then_inc(bank_full[b], 1)

            transposes("yT", 2 * TT)
            h_both = (hT_hi, hT_lo)
            for n in range(12):
                unit = M + n // 2
                if n % 2 == 0:
                    split(unit)
                project(f"proj{n}", both(unit, 256), (n % 2) * P, h_both, KT, None if n else "yT")
            for u in range(2):
                split(M + 6 + u)
                w = both(M + 6 + u, 256)
                for t in range(TT):
                    b = start(f"v{u}_{t}")
                    for k in range(KT):
                        last = product(b[:, 0:256], [v[:, k, t * P:(t + 1) * P] for v in h_both],
                                       [v[:, k, :] for v in w], k == 0, k == KT - 1)
                    finish(f"v{u}_{t}", last)
            for n in range(4, 12):
                was_read(pe, f"proj{n}")
            for u in range(2):
                for t in range(TT):
                    was_read(pe, f"v{u}_{t}")

            def head_scores(h):
                r = 64 * (h % 2)
                for q in range(TT):
                    b = start(f"score{h}_{q}")
                    nk = (q + 1) * P
                    finish(f"score{h}_{q}", pe.matmul(b[:, 0:nk], qT[r:r + 64, h // 2, q * P:(q + 1) * P],
                                                      kT[r:r + 64, h // 2, 0:nk], start=True, stop=True))

            def head_values(h):
                pe.wait_ge(prob_ready, h + 1)
                for piece, kts in enumerate(((0,), (1,), (2, 3))):
                    b = start(f"probT{h}_{piece}")
                    c = 0
                    for kt in kts:
                        for q in range(kt, TT):
                            last = pe.transpose(b[:, c:c + P], att[:, q, kt * P:(kt + 1) * P], ident)
                            c += P
                    finish(f"probT{h}_{piece}", last)
                r = 64 * (h % 2)
                b = start(f"pv{h}")
                for piece in range(3):
                    was_read(pe, f"probT{h}_{piece}")
                for q in range(TT):
                    for kt in range(q + 1):
                        at = ((0, 4, 7, 9)[kt] + q - kt) * P
                        last = pe.matmul(b[r:r + 64, q * P:(q + 1) * P], v_s[:, kt, h * DH:(h + 1) * DH],
                                         pT[:, at:at + P], start=(kt == 0), stop=(kt == q))
                finish(f"pv{h}", last)

            def ssm_tables(c):
                pe.wait_ge(wext_ready, c + 1)
                for i, name in enumerate(("st_re", "st_im")):
                    b = start(f"{name}_{c}")
                    for g in range(CGP):
                        last = pe.transpose(b[:, g * P:(g + 1) * P], wext[:, i, g, 0:P], ident)
                    finish(f"{name}_{c}", last)

            def ssm_lags(c):
                pe.wait_ge(bbd_ready, 1)
                pe.wait_ge(wc_ready, c + 1)
                b = start(f"lags_{c}")
                for ri in range(2):
                    for g in range(CGP):
                        last = pe.matmul(b[32 * g:32 * g + 32, 0:P], bbd[:, ri, c * CGP + g, :], wc[:, ri, g, 0:P],
                                         start=(ri == 0), stop=(ri == 1))
                finish(f"lags_{c}", last)

            def ssm_states(c):
                pe.wait_ge(u_in, 16 * T8 * (c + 1))
                was_read(pe, f"st_re_{c}")
                was_read(pe, f"st_im_{c}")
                b = start(f"state{c}")
                for ri in range(2):
                    for g in range(CG):
                        r = 64 * (g % 2)
                        at = ri * 256 + (g // 2) * NCH
                        last = pe.matmul(b[r:r + 64, at:at + NCH], st[:, ri, g // 2, r:r + 64], ubuf[:, g, :],
                                         start=True, stop=True)
                finish(f"state{c}", last)
                pe.wait_ge(kbd_ready, c + 1)
                b = start(f"near{c}")
                for lag in range(T8 + 1):
                    n = (T8 - lag % T8) * NCH
                    last = pe.matmul(b[:, S - n:S], kbd[:, lag, :],
                                     uT[:, c, :, :].rearrange("p t j -> p (t j)")[:, 0:n],
                                     start=(lag == 0), stop=(lag == T8))
                finish(f"near{c}", last)

            def ssm_out(c):
                pe.wait_ge(states_ready, c + 1)
                b = start(f"ssm{c}")
                for g in range(CGP):
                    for ri in range(2):
                        last = pe.matmul(b[:, g * P:(g + 1) * P], wc[:, ri, g, SG:SG + P],
                                         hbd[:, ri, g, :, :].rearrange("p a b -> p (a b)"),
                                         start=(ri == 0), stop=(ri == 1))
                finish(f"ssm{c}", last)

            for i in range(STEPS):
                if i < HEADS:
                    head_scores(i)
                unit = M + 8 + i
                split(unit)
                for n in range(2):
                    project(f"gate{2 * i + n}", both(unit, 256), n * P, h_both, KT)
                if i % 2 == 1 and i < 2 * CT:
                    ssm_lags(i // 2)
                if i < HEADS:
                    head_values(i)
                if i % 2 == 0 and 2 <= i <= 2 * CT:
                    ssm_out(i // 2 - 1)
                if i % 2 == 0 and i < 2 * CT:
                    ssm_tables(i // 2)
                if i % 2 == 1 and i < 2 * CT:
                    ssm_states(i // 2)
            for name, tile, unit, rows in (("glu", "y", M + 20, (y_hi, y_lo)), ("ao", "za", M + 22, (za_hi, za_lo)),
                                           ("so", "ys", M + 24, (ys_hi, ys_lo))):
                for d in range(KT):
                    if d % 4 == 0:
                        split(unit + d // 4)
                    project(f"{name}{d}", both(unit + d // 4, 512), (d % 4) * P, rows, CT, None if d else tile)
            out_project("fin", (ga_hi, ga_lo), M + 26, (0, 2, 4, 6), lambda m: f"ga{m}")

        @block.scalar
        def _(act_e):
            steps = [0]

            def link(ins):
                steps[0] += 1
                ins.then_inc(act_step, 1)
                act_e.wait_ge(act_step, steps[0])

            act_e.dma_start(cst, cst_d).then_inc(cst_in, 16)
            act_e.dma_start(cols, cols_d).then_inc(cols_in, 16)

            def squares(n0, first=None):
                for t in range(TT):
                    if first is not None:
                        first(t)
                    act_e.activation(nrm[:, t, :], xres[:, t, :], ACT.Square,
                                     accum_out=stat[:, n0 + t:n0 + t + 1]).then_inc(square_sum, 1)

            def scaled(prefix, gain):
                for k in range(KT):
                    full(act_e, f"{prefix}{k}")
                    read(f"{prefix}{k}", act_e.activation(hT[:, k, :], bank[k][:, :], ACT.Copy, scale=col(gain, k)))

            def scaled_hi(prefix, gain):
                for k in range(KT):
                    full(act_e, f"{prefix}{k}")
                    tile_hi(hT_hi[:, k, :], bank[k][:, :], scale=col(gain, k))

            def copy_out(name, dst, src=None):
                full(act_e, name)
                read(name, act_e.activation(dst, bank[jobs.bank(name)][:, :] if src is None else src, ACT.Copy))

            def weights_hi(unit):
                loaded(act_e, unit)
                if unit == 9:
                    act_e.wait_ge(lru_done, CT)
                elif unit in (M, M + 1):
                    s = RING2 + 1 + unit - M
                    act_e.wait_ge(unit_used, 1 + max(u for u in range(M - RING, M) if u % RING == s))
                elif unit > 1 and unit != 10:
                    act_e.wait_ge(unit_used, unit - 1)
                act_e.activation(hi_of(unit), ring[slot_of(unit)], ACT.Copy).then_inc(w_hi, 1)

            def tile_hi(dst, src, **kw):
                act_e.activation(dst, src, ACT.Copy, **kw).then_inc(hi_ready, 1)

            squares(0, lambda t: act_e.wait_ge(x_in[t], 16))
            weights_hi(0)
            act_e.wait_ge(cols_in, 16)
            act_e.wait_ge(halves, 1)
            link(act_e.activation(kneg, kneg, ACT.Exp, scale=-1.0))
            act_e.activation(kneg, kneg, ACT.Ln, bias=1.0).then_inc(lam_ln, 1)
            scaled_hi("xT", "g1")
            weights_hi(1)
            act_e.wait_ge(pad_zero, 1)
            for n in range(12):
                if n % 2 == 0 and 1 <= n // 2 < 5:
                    weights_hi(n // 2 + 1)
                copy_out(f"in{n}", lrux[:, n, CONV_LEFT:CONV_LEFT + S] if n < CT else mixT[:, n if n < 8 else n - 8, :])
            act_e.wait_ge(k_ready, 1)
            for c in range(CT):
                for d in range(2):
                    i, tile = 2 * c + d, gt[:, d, :, :]
                    if c:
                        act_e.wait_ge(lru_done, c)
                        if not d:
                            tile_hi(mix_hi[:, c - 1, :], mixT[:, c - 1, :])
                    for j in range(2):
                        name = f"lru{c}_{2 * d + j}"
                        full(act_e, name)
                        read(name, act_e.activation(tile[:, j, :], bank[jobs.bank(name)][:, :], ACT.Tanh, scale=0.5,
                                                    bias=hbias[:, (2 * d + j) * CT + c:(2 * d + j) * CT + c + 1]))
                    was_read(act_e, f"lru{c}_{2 * d}")
                    k = CT * d + c
                    act_e.activation(tile[:, 2, :], tile[:, 0, :], ACT.Exp, scale=kpos[:, k:k + 1], bias=kpos[:, k:k + 1])
                    act_e.activation(tile[:, 3, :], tile[:, 0, :], ACT.Tanh, scale=kneg[:, k:k + 1],
                                     bias=kneg[:, k:k + 1]).then_inc(acts_ready, 1)
                act_e.wait_ge(gelu_in, c + 1)
                act_e.activation(lrux[:, c, 0:S], lrux[:, c, 0:S], ACT.Tanh, scale=GELU_C).then_inc(gelu_tanh, 1)
                for d in range(2):
                    act_e.wait_ge(m2_ready, 2 * c + d + 1)
                    act_e.activation(gt[:, d, 3, :], gt[:, d, 3, :], ACT.Sqrt).then_inc(root_ready, 1)
                for half in range(2):
                    copy_out(f"four{c}_{half}", four[:, c, 2 * half:2 * half + 2, :].rearrange("p a b -> p (a b)"))
            weights_hi(9)
            tile_hi(mix_hi[:, CT - 1, :], mixT[:, CT - 1, :])
            weights_hi(10)
            for g in range(CT):
                full(act_e, f"mix{g}")
                tile_hi(mix_hi[:, CT + g, :], bank[jobs.bank(f"mix{g}")][:, :])
            weights_hi(11)
            weights_hi(12)

            for t in range(TT):
                was_read(act_e, f"out{2 * t + 1}")
                act_e.activation(nrm[:, t, :], xres[:, t, :], ACT.Square,
                                 accum_out=stat[:, 8 + t:9 + t]).then_inc(square_sum, 1)
            scaled("h2T", "g2")
            copy_out("logitT", logT, bank[jobs.bank("logitT")][:, 0:P])
            act_e.wait_ge(soft_in, 1)
            b = bank[jobs.bank("logits")]
            for t in range(TT):
                last = act_e.activation(aff[:, t, 0:NE], b[:, 32 * t:32 * t + NE], ACT.Exp, bias=stat[:, 16 + t:17 + t],
                                        accum_out=stat[:, 20 + t:21 + t])
                if t < TT - 1:
                    last.then_inc(soft_exp, 1)
            read("logits", last)
            copy_out("scoreT", score, bank[jobs.bank("scoreT")][0:NE, :])
            full(act_e, "posT")
            read("posT", act_e.activation(posT[:, :, 0:NE], bank[jobs.bank("posT")][:, 0:TT * NE].rearrange("p (t e) -> p t e", t=TT),
                                          ACT.Copy))

            with act_e.Fori(0, NE) as e:
                def filled(b, n):
                    act_e.wait_ge(bank_full[b], e * EF[b] + (moe_told[b] + n + 1))

                filled(0, 1)
                act_e.activation(flat(gselT), bank[0][:, :], ACT.Copy).then_inc(bank_read[0], 1)
                act_e.wait_ge(unit_used, e * E_UNITS + (B1_UNITS + 2 * KT - 1))
                for b in range(2):
                    act_e.activation(th[:, b, :], bank[1 + b][:, :], ACT.Tanh, scale=0.5).then_inc(tanh_ready, 1)
                for b in range(2):
                    filled(5 + b, 0)
                    act_e.activation(actT[:, 4 * b:4 * b + 4, :].rearrange("p a b -> p (a b)"), bank[5 + b][:, :],
                                     ACT.Copy).then_inc(bank_read[5 + b], 1)
                act_e.wait_ge(unit_used, e * E_UNITS + (B1_UNITS + E_UNITS))
                act_e.activation(eo, bank[7][:, :], ACT.Copy).then_inc(bank_read[7], 1)

            weights_hi(M)
            weights_hi(M + 1)
            for t in range(TT):
                act_e.wait_ge(bank_read[(7, 2, 4, 6)[t]], jobs.before(f"yT{(7, 2, 4, 6)[t]}"))
                act_e.activation(nrm[:, t, :], xres[:, t, :], ACT.Square,
                                 accum_out=stat[:, 24 + t:25 + t]).then_inc(square_sum, 1)
            for t in range(TT):
                act_e.wait_ge(between, t + 1)
                act_e.activation(nrm[:, t, :], xres[:, t, :], ACT.Square,
                                 accum_out=stat[:, 32 + t:33 + t]).then_inc(square_sum, 1)
            scaled_hi("yT", "gb2")
            act_e.wait_ge(prep_in, 1)
            act_e.activation(prep[:, 0, :], col("log_dt", 0, GP), ACT.Exp).then_inc(prep_exp, 1)
            act_e.wait_ge(prep_in, 2)
            act_e.activation(prep[:, 3, :], prep[:, 1, :], ACT.Exp).then_inc(prep_exp, 1)
            act_e.activation(prep[:, 4, :], prep[:, 1, :], ACT.Exp, scale=float(T8)).then_inc(prep_exp, 1)
            act_e.wait_ge(sin_arg, 1)
            act_e.activation(prep[:, 7, :], prep[:, 5, :], ACT.Sin, scale=0.5).then_inc(prep_sin, 1)
            act_e.activation(prep[:, 6, :], prep[:, 5, :], ACT.Sin).then_inc(prep_sin, 1)

            def staged(c):
                name = f"proj{c}"
                full(act_e, name)
                read(name, act_e.activation(uT[:, c, :, :],
                                            bank[jobs.bank(name)][:, :].rearrange("p (j t) -> p t j", t=T8), ACT.Copy))

            for n in range(12):
                if n % 2 == 0 and n:
                    weights_hi(M + n // 2 + 1)
                if n < 4:
                    staged(n)
                else:
                    copy_out(f"proj{n}", (qT if n < 8 else kT)[:, n % 4, :])
            for u in range(2):
                weights_hi(M + u + 7)
                for t in range(TT):
                    name = f"v{u}_{t}"
                    copy_out(name, v_s[:, t, 256 * u:256 * u + 256], bank[jobs.bank(name)][:, 0:256])

            for i in range(STEPS):
                if i < HEADS:
                    for q in range(TT):
                        nk = (q + 1) * P
                        act_e.wait_ge(max_ready, TT * i + q + 1)
                        act_e.activation(att[:, q, 0:nk], att[:, q, 0:nk], ACT.Exp, bias=stat[:, 40 + q:41 + q],
                                         accum_out=stat[:, 44 + q:45 + q]).then_inc(exp_ready, 1)
                weights_hi(M + 9 + i)
                for n in range(2):
                    name, g = f"gate{2 * i + n}", 2 * i + n
                    full(act_e, name)
                    src = bank[jobs.bank(name)][:, :]
                    if g < 2 * CT:
                        dst = (zaT if g < CT else zsT)[:, g % CT, :]
                        act_e.activation(dst, src, ACT.Tanh, scale=0.5).then_inc(th_ready, 1)
                    else:
                        j = g - 2 * CT
                        dst = (gaT if j < KT else gsT)[:, j % KT, :]
                        if j == KT:
                            full(act_e, f"ssm{CT - 1}")
                        read(name, act_e.activation(dst, src, ACT.Tanh, scale=0.5, bias=hbias[:, 24 + j:25 + j]))
                if i < HEADS:
                    for b in range(3):
                        w = (4, 3, 3)[b] * P
                        name = f"probT{i}_{b}"
                        copy_out(name, pT[:, (0, 4, 7)[b] * P:(0, 4, 7)[b] * P + w], bank[jobs.bank(name)][:, 0:w])
                if i % 2 == 0 and i < 2 * CT:
                    for ri, name in enumerate(("st_re", "st_im")):
                        copy_out(f"{name}_{i // 2}", flat(st[:, ri, :, :]))
                if i % 2 == 0 and 2 <= i <= 2 * CT:
                    c = i // 2 - 1
                    if c:
                        act_e.wait_ge(y_out, 16 * T8 * c)
                    copy_out(f"ssm{c}", flat(ybuf))
                if i % 2 == 1 and i < 2 * CT:
                    copy_out(f"near{i // 2}", uT[:, i // 2, :, :].rearrange("p t j -> p (t j)"))
                if i == HEADS:
                    act_e.wait_ge(states_ready, CT)
                    for c in range(CT):
                        was_read(act_e, f"pv{2 * c + 1}")
                        tile_hi(za_hi[:, c, :], zaT[:, c, :])
                if i in (GELU_STEP, GELU_STEP + 1):
                    cs = range(2 * (i - GELU_STEP), 2 * (i - GELU_STEP) + 2)
                    for c in cs:
                        act_e.wait_ge(ygelu_in, c + 1)
                        act_e.activation(tmp[:, c % 2, :], tmp[:, c % 2, :], ACT.Tanh, scale=GELU_C).then_inc(ytanh, 1)
                    for c in cs:
                        act_e.wait_ge(y_ready, c + 1)
                        tile_hi(y_hi[:, c, :], yT[:, c, :])
            weights_hi(M + 21)
            for n in range(CT):
                name = f"glu{n}"
                if n == 0:
                    full(act_e, f"score{HEADS - 1}_{TT - 1}")
                full(act_e, name)
                read(name, act_e.activation(ysT[:, n, :], bank[jobs.bank(name)][:, :], ACT.Tanh, scale=0.25,
                                            bias=hbias[:, 16 + CT + n:17 + CT + n]))
            weights_hi(M + 22)
            for c in range(CT):
                act_e.wait_ge(glu_ready, c + 1)
                tile_hi(ys_hi[:, c, :], ysT[:, c, :])
            for u in range(23, 27):
                weights_hi(M + u)
            for d in range(KT):
                act_e.wait_ge(merged, d + 1)
                tile_hi(ga_hi[:, d, :], gaT[:, d, :])
            for u in range(27, 30):
                weights_hi(M + u)
            for t in range(TT):
                was_read(act_e, f"fin{2 * t + 1}")
                act_e.activation(nrm[:, t, :], xres[:, t, :], ACT.Square,
                                 accum_out=stat[:, 48 + t:49 + t]).then_inc(square_sum, 1)

        @block.gpsimd
        def _(pool):
            steps = [0]

            def link(ins):
                steps[0] += 1
                ins.then_inc(pool_step, 1)
                pool.wait_ge(pool_step, steps[0])

            def roots(n0, count0):
                for t in range(TT):
                    pool.wait_ge(square_sum, count0 + t + 1)
                    c = stat[:, n0 + t:n0 + t + 1]
                    link(pool.tensor_scalar(c, c, 1.0 / D, EPS, ALU.mult, ALU.add))
                    pool.tensor_tensor(stat[:, n0 + 4 + t:n0 + 5 + t], c, stat[:, 62:63], ALU.pow).then_inc(root_mean, 1)

            pool.memset(lrux, 0.0).then_inc(pad_zero, 1)
            link(pool.memset(stat[:, 62:63], -0.5))
            roots(0, 0)
            for c in range(CT):
                was_read(pool, f"in{8 + c}")
                pool.wait_ge(conv_ready, c + 1)
                g, xg = lrux[:, c, 0:S], mixT[:, c, :]
                link(pool.tensor_tensor(g, xg, xg, ALU.mult))
                link(pool.tensor_scalar(g, g, GELU_A, 1.0, ALU.mult, ALU.add))
                pool.tensor_tensor(g, g, xg, ALU.mult).then_inc(gelu_in, 1)
            full(pool, "out7")
            pool.dma_start(gfb, gf_d.partition_broadcast(P)).then_inc(gf_in, 16)
            roots(8, TT)
            roots(24, 2 * TT)
            pool.wait_ge(bank_full[6], moe_told[6] + NE * EF[6])
            pool.dma_start(bc.rearrange("p a g c -> p (a g c)"), bc_d).then_inc(bc_in, 16)
            roots(32, 3 * TT)
            pool.wait_ge(x_saved, 16 * TT)
            pool.wait_ge(normed, 3 * TT)
            for h in range(HEADS):
                pool.dma_start(relb[:, h, :], bass.AP(tensor=relp.tensor, offset=h * (REL + P), ap=[[1, P], [1, REL]])
                               ).then_inc(rel_in, 16)
            for c in range(CT):
                was_read(pool, f"proj{c}")
            pool.dma_start(u_dram.rearrange("(c p) t j -> p c t j", p=P), uT).then_inc(u_out, 16)
            pool.wait_ge(u_out, 16)

            def inputs(c):
                for t in range(T8):
                    pool.dma_start(ubuf[t * SG:(t + 1) * SG, :, :],
                                   u_dram[c * P:(c + 1) * P, t, :].rearrange("(g c) j -> c g j", c=SG)).then_inc(u_in, 16)

            def output_table(c):
                if c:
                    was_read(pool, f"score1_{TT - 1}")
                    scratch = flat(relb[:, 0:2, :])
                else:
                    scratch = flat(ybuf)
                cs = slice(c * CGP, (c + 1) * CGP)

                def steps_of(pw):
                    return pw[:, cs, ts].unsqueeze(3).to_broadcast([P, CGP, ts.stop - ts.start, SG])

                def chans_of(v):
                    return v[:, cs, :].unsqueeze(2).to_broadcast([P, CGP, ts.stop - ts.start, SG])

                for ts in (slice(0, T8), slice(T8, T8 + 1)):
                    wr, wi = (wc[:, k, :, ts.start * SG:ts.stop * SG].rearrange("p g (t c) -> p g t c", c=SG)
                              for k in range(2))
                    sc = scratch[:, 0:CGP * (ts.stop - ts.start) * SG].rearrange("p (g t c) -> p g t c", g=CGP, c=SG)
                    pool.tensor_tensor(wr, steps_of(pw_re), chans_of(bc[:, 2, :, :]), ALU.mult)
                    link(pool.tensor_tensor(sc, steps_of(pw_in), chans_of(bc[:, 3, :, :]), ALU.mult))
                    link(pool.tensor_tensor(wr, wr, sc, ALU.add))
                    pool.tensor_tensor(wi, steps_of(pw_in), chans_of(bc[:, 2, :, :]), ALU.mult)
                    link(pool.tensor_tensor(sc, steps_of(pw_re), chans_of(bc[:, 3, :, :]), ALU.mult))
                    last = pool.tensor_tensor(wi, wi, sc, ALU.subtract)
                    if ts.stop == T8:
                        link(last)
                last.then_inc(wc_ready, 1)

            inputs(0)
            pool.wait_ge(pw_ready, 1)
            output_table(0)
            for c in range(CT):
                if c + 1 < CT:
                    full(pool, f"state{c}")
                    inputs(c + 1)
                    full(pool, f"ssm{c}")
                    output_table(c + 1)
                was_read(pool, f"ssm{c}")
                for t in range(T8):
                    pool.dma_start(y_dram[c * P:(c + 1) * P, t, :].rearrange("(g c) j -> c g j", c=SG),
                                   ybuf[t * SG:(t + 1) * SG, :, :]).then_inc(y_out, 16)
            pool.wait_ge(y_out, 16 * T8 * CT)
            full(pool, f"score{HEADS - 1}_{TT - 1}")
            pool.dma_start(yT, y_dram.rearrange("(c p) t j -> p c (t j)", p=P)).then_inc(y_in, 16)
            full(pool, f"pv{HEADS - 1}")
            pool.dma_start(gfin, gfin_d.partition_broadcast(P)).then_inc(gfin_in, 16)
            roots(48, 4 * TT)

        @block.vector
        def _(dve):
            steps = [0]

            def link(ins):
                steps[0] += 1
                ins.then_inc(dve_step, 1)
                dve.wait_ge(dve_step, steps[0])

            def tt(out_, a, b, op):
                return dve.tensor_tensor(out_, a, b, op)

            def stt(out_, a, s, b, op0, op1):
                return dve.scalar_tensor_tensor(out_, a, s, b, op0, op1)

            def normalise(n0, count0):
                for t in range(TT):
                    dve.wait_ge(root_mean, count0 + t + 1)
                    dve.tensor_scalar(nrm[:, t, :], xres[:, t, :], stat[:, n0 + 4 + t:n0 + 5 + t], None,
                                      ALU.mult).then_inc(normed, 1)

            def weights_lo(unit):
                dve.wait_ge(w_hi, split_units.index(unit) + 1)
                tt(ring_r[slot_of(unit)], ring[slot_of(unit)], hi_of(unit), ALU.subtract).then_inc(w_lo, 1)

            def tile_lo(tile, dst, src, hi):
                high_stands(dve, tile)
                tt(dst, src, hi, ALU.subtract).then_inc(lo_ready, 1)

            def scaled_lo(prefix, gain):
                for k in range(KT):
                    if k >= 3 * KT // 4:
                        full(dve, f"{prefix}{KT - 1}")
                    high_stands(dve, f"{prefix}{k}")
                    read(f"{prefix}{k}", stt(hT_lo[:, k, :], bank[k][:, :], col(gain, k), hT_hi[:, k, :], ALU.mult,
                                             ALU.subtract))

            dve.wait_ge(cols_in, 16)
            link(dve.tensor_scalar(kneg, col("lam", 0, 2 * CT), -1.0, None, ALU.mult))
            tt(kneg, kneg, col("lam", 0, 2 * CT), ALU.max).then_inc(halves, 1)
            dve.tensor_scalar(hbias[:, 0:4 * CT], col("bias_lru", 0, 4 * CT), 0.5, None, ALU.mult)
            dve.tensor_scalar(hbias[:, 4 * CT:4 * CT + 3 * KT], col("b_glu", 0, 3 * KT), 0.5, None, ALU.mult)
            normalise(0, 0)
            weights_lo(0)
            scaled_lo("xT", "g1")
            weights_lo(1)
            dve.wait_ge(lam_ln, 1)
            link(dve.tensor_scalar(kpos, col("lam", 0, 2 * CT), 0.0, None, ALU.min))
            link(tt(kpos, kpos, kneg, ALU.subtract))
            link(dve.tensor_scalar(kpos, kpos, LRU_C / 2, None, ALU.mult))
            dve.tensor_scalar(kneg, kpos, -1.0, None, ALU.mult).then_inc(k_ready, 1)
            for c in range(CT):
                was_read(dve, f"in{c}")
                o = conv[:, c, :]
                link(dve.tensor_scalar(o, lrux[:, c, 0:S], col("conv_w", c), col("conv_b", c), ALU.mult, ALU.add))
                for k in range(1, CONV):
                    last = stt(o, lrux[:, c, k:k + S], col("conv_w", k * CT + c), o, ALU.mult, ALU.add)
                    if k < CONV - 1:
                        link(last)
                last.then_inc(conv_ready, 1)
                if c in (1, 3):
                    weights_lo(2 if c == 1 else 3)
            weights_lo(4)
            weights_lo(5)
            for c in range(CT):
                for d in range(2):
                    dve.wait_ge(acts_ready, 2 * c + d + 1)
                    link(tt(gt[:, d, 0, :], gt[:, d, 2, :], gt[:, d, 2, :], ALU.mult))
                    stt(gt[:, d, 3, :], gt[:, d, 0, :], 1.0, gt[:, d, 3, :], ALU.add, ALU.mult).then_inc(m2_ready, 1)
                dve.wait_ge(conv_ready, c + 1)
                for d in range(2):
                    link(stt(gt[:, d, 1, :], gt[:, d, 1, :], 1.0, conv[:, c, :], ALU.add, ALU.mult))
                for d in range(2):
                    dve.wait_ge(root_ready, 2 * c + d + 1)
                    link(stt(gt[:, d, 1, :], gt[:, d, 3, :], 0.5, gt[:, d, 1, :], ALU.mult, ALU.mult))
                    a, b, h = gt[:, d, 2, :], gt[:, d, 1, :], gt[:, d, 0, :]
                    if d:
                        a, b, h = a[:, ::-1], b[:, ::-1], h[:, ::-1]
                    link(dve.tensor_tensor_scan(h, a, b, 0.0, ALU.mult, ALU.add))
                link(tt(gt[:, 0, 0, :], gt[:, 0, 0, :], gt[:, 1, 0, :], ALU.add))
                dve.wait_ge(gelu_tanh, c + 1)
                link(stt(mixT[:, c, :], lrux[:, c, 0:S], 1.0, mixT[:, c, :], ALU.add, ALU.mult))
                stt(mixT[:, c, :], mixT[:, c, :], 0.5, gt[:, 0, 0, :], ALU.mult, ALU.mult).then_inc(lru_done, 1)
                if c:
                    tile_lo(f"lru{c - 1}", mix_lo[:, c - 1, :], mixT[:, c - 1, :], mix_hi[:, c - 1, :])
            weights_lo(9)
            tile_lo(f"lru{CT - 1}", mix_lo[:, CT - 1, :], mixT[:, CT - 1, :], mix_hi[:, CT - 1, :])
            weights_lo(10)
            for g in range(CT):
                high_stands(dve, f"mix{g}")
                read(f"mix{g}", tt(mix_lo[:, CT + g, :], bank[jobs.bank(f"mix{g}")][:, :], mix_hi[:, CT + g, :],
                                   ALU.subtract))
            weights_lo(11)
            weights_lo(12)

            def residual(prefix, scale):
                for o in range(8):
                    name = f"{prefix}{o}"
                    r = xres[:, o // 2, o % 2 * 512:o % 2 * 512 + 512]
                    full(dve, name)
                    read(name, stt(r, bank[jobs.bank(name)][:, :], scale, r, ALU.mult, ALU.add))

            residual("out", 1.0)

            normalise(8, TT)
            full(dve, "logits")
            b = bank[jobs.bank("logits")]
            for t in range(TT):
                last = dve.tensor_reduce(stat[:, 16 + t:17 + t], b[:, 32 * t:32 * t + NE], AX, ALU.max, negate=True)
            last.then_inc(soft_in, 1)
            full(dve, f"mix{CT - 1}")
            dve.memset(aff[:, :, NE:NE + 1], 0.0)
            dve.memset(posT[:, :, NE:NE + 1], -1.0)
            dve.memset(ones, 1.0)
            for t in range(TT):
                if t < TT - 1:
                    dve.wait_ge(soft_exp, t + 1)
                else:
                    was_read(dve, "logits")
                last = dve.reciprocal(stat[:, 20 + t:21 + t], stat[:, 20 + t:21 + t])
            link(last)
            for t in range(TT):
                last = dve.tensor_scalar(aff[:, t, 0:NE], aff[:, t, 0:NE], stat[:, 20 + t:21 + t], None, ALU.mult)
            last.then_inc(aff_ready, 1)
            was_read(dve, "scoreT")
            for _ in range(CAP // 8):
                link(dve.max(top, score))
                link(dve.match_replace(score, top, score, -1.0))
            link(dve.tensor_scalar(taken, score, -0.5, None, ALU.is_lt))
            link(dve.tensor_tensor_scan(rank, ones, taken, 0.0, ALU.mult, ALU.add))
            link(tt(rank, rank, taken, ALU.mult))
            dve.tensor_scalar(rank, rank, -1.0, None, ALU.add).then_inc(pos_ready, 1)
            was_read(dve, "posT")

            def select(e):
                return tt(sel, posT[:, :, bass.ds(e, 1)].to_broadcast([P, TT, CAP]),
                          slotrow.unsqueeze(1).to_broadcast([P, TT, CAP]), ALU.is_equal)

            def gated(e):
                return tt(gsel, sel.unsqueeze(2).to_broadcast([P, TT, 2, CAP]),
                          aff[:, :, bass.ds(e, 1)].unsqueeze(3).to_broadcast([P, TT, 2, CAP]), ALU.mult)

            select(0).then_inc(sel_ready, 1)
            dve.wait_ge(sel_ready, 1)
            gated(0).then_inc(sel_ready, 1)

            with dve.Fori(0, NE) as e:
                def filled(b, n):
                    dve.wait_ge(bank_full[b], e * EF[b] + (moe_told[b] + n + 1))

                filled(0, 0)
                tt(xinT, bank[0][:, :].rearrange("p (k c) -> p k c", k=KT),
                   col("g2", 0, KT).unsqueeze(2).to_broadcast([P, KT, CAP]), ALU.mult).then_inc(bank_read[0], 1)
                for b in range(2):
                    dve.wait_ge(tanh_ready, 2 * e + (b + 1))
                    stt(th[:, b, :], th[:, b, :], 1.0, bank[1 + b][:, :], ALU.add, ALU.mult).then_inc(bank_read[1 + b], 1)
                dve.wait_ge(unit_used, e * E_UNITS + (B1_UNITS + 2 * KT))
                for b in range(2):
                    dve.wait_ge(bank_read[1 + b], e * EU[1 + b] + (moe_uses[1 + b] + 1))
                    stt(act[:, b, :], th[:, b, :], 0.5, bank[3 + b][:, :], ALU.mult, ALU.mult).then_inc(act_ready, 1)
                select(e + 1).then_inc(sel_ready, 1)
                filled(0, 1)
                dve.wait_ge(sel_ready, 2 * e + 3)
                gated(e + 1).then_inc(sel_ready, 1)
                for o, b in enumerate((0, 7, 1, 2, 3, 4, 5, 6)):
                    r = xres[:, o // 2, o % 2 * 512:o % 2 * 512 + 512]
                    filled(b, EF[b] - 1)
                    tt(r, r, bank[b][:, :], ALU.add).then_inc(bank_read[b], 1)

            dve.wait_ge(gf_in, 16)
            for t in range(TT):
                dve.wait_ge(root_mean, 2 * TT + t + 1)
                stt(xres[:, t, :], xres[:, t, :], stat[:, 28 + t:29 + t], gfb, ALU.mult, ALU.mult).then_inc(between, 1)
            normalise(32, 3 * TT)
            weights_lo(M)
            weights_lo(M + 1)
            scaled_lo("yT", "gb2")

            def p(n):
                return prep[:, n, :]

            def cmul(dst, a, b, s):
                tt(s[0], a[0], b[0], ALU.mult)
                tt(s[1], a[1], b[1], ALU.mult)
                tt(s[2], a[0], b[1], ALU.mult)
                link(tt(s[3], a[1], b[0], ALU.mult))
                tt(dst[0], s[0], s[1], ALU.subtract)
                link(tt(dst[1], s[2], s[3], ALU.add))

            dve.wait_ge(between, TT)
            link(dve.memset(flat(prep), 0.0))
            dve.memset(stat[:, 63:64], 0.0).then_inc(prep_in, 1)
            dve.wait_ge(prep_exp, 1)
            tt(p(1), col("a_re", 0, GP), p(0), ALU.mult)
            link(tt(p(2), col("a_im", 0, GP), p(0), ALU.mult))
            link(dve.tensor_scalar(p(5), p(2), 1 / TWO_PI, ROUND, ALU.mult, ALU.add))
            dve.tensor_scalar(p(5), p(5), -ROUND, None, ALU.add).then_inc(prep_in, 1)
            dve.wait_ge(prep_in, 2)
            link(stt(p(8), p(5), -PI_HI, p(2), ALU.mult, ALU.add))
            link(stt(p(8), p(5), -PI_MID, p(8), ALU.mult, ALU.add))
            link(stt(p(5), p(5), -PI_LO, p(8), ALU.mult, ALU.add))
            dve.tensor_scalar(p(5), p(5), -3.1415925, 3.1415925, ALU.max, ALU.min).then_inc(sin_arg, 1)
            dve.wait_ge(prep_exp, 3)
            dve.wait_ge(prep_sin, 2)
            link(tt(p(9), p(7), p(7), ALU.mult))
            link(dve.tensor_scalar(p(9), p(9), -2.0, 1.0, ALU.mult, ALU.add))
            dve.memset(pw_re[:, :, 0], 1.0)
            dve.memset(pw_im[:, :, 0], 0.0)
            tt(pw_re[:, :, 1], p(3), p(9), ALU.mult)
            link(tt(pw_im[:, :, 1], p(3), p(6), ALU.mult))
            link(dve.tensor_scalar(p(10), pw_re[:, :, 1], -1.0, None, ALU.add))
            are, aim, nim = col("a_re", 0, GP), col("a_im", 0, GP), pw_im[:, :, 1]
            tt(p(11), are, are, ALU.mult)
            tt(p(12), aim, aim, ALU.mult)
            tt(p(13), p(10), are, ALU.mult)
            tt(p(14), nim, aim, ALU.mult)
            tt(p(15), nim, are, ALU.mult)
            link(tt(p(16), p(10), aim, ALU.mult))
            tt(p(11), p(11), p(12), ALU.add)
            tt(p(13), p(13), p(14), ALU.add)
            link(tt(p(15), p(15), p(16), ALU.subtract))
            link(dve.reciprocal(p(11), p(11)))
            tt(p(13), p(13), p(11), ALU.mult)
            link(tt(p(15), p(15), p(11), ALU.mult))

            weights_lo(M + 2)

            def per_chan(v):
                return v.unsqueeze(2).to_broadcast([P, GP, SG])

            dve.wait_ge(bc_in, 16)
            sc = [prot[:, i, :, 0:SG] for i in range(2)] + [prot[:, i, :, SG:2 * SG] for i in range(2)]
            cmul((bc[:, 0, :, :], bc[:, 1, :, :]), (bc[:, 0, :, :], bc[:, 1, :, :]),
                 (per_chan(p(13)), per_chan(p(15))), sc)
            link(dve.memset(bbd.rearrange("p a g c -> p (a g c)"), 0.0))
            for a in range(2):
                q = slice(64 * a, 64 * a + 64)
                for ri in range(2):
                    last = dve.tensor_copy(bbd[q, ri, :, a * SG:(a + 1) * SG], bc[q, ri, :, :])
            last.then_inc(bbd_ready, 1)
            weights_lo(M + 3)
            for k in range(2, T8 + 1):
                cmul((pw_re[:, :, k], pw_im[:, :, k]), (pw_re[:, :, k - 1], pw_im[:, :, k - 1]),
                     (pw_re[:, :, 1], pw_im[:, :, 1]), [p(17), p(18), p(19), p(20)])
            dve.tensor_scalar(pw_in, pw_im, -1.0, None, ALU.mult)
            weights_lo(M + 4)
            for _ in range(3):
                cmul((p(9), p(6)), (p(9), p(6)), (p(9), p(6)), [p(17), p(18), p(19), p(20)])
            dve.memset(rotc[:, :, 0:1], 1.0)
            link(dve.memset(rots[:, :, 0:1], 0.0))
            n = 1
            while n < NCH:
                ec = p(9).unsqueeze(2).to_broadcast([P, GP, n])
                es = p(6).unsqueeze(2).to_broadcast([P, GP, n])
                lo, hi = slice(0, n), slice(n, 2 * n)
                s0, s1 = prot[:, 0, :, 0:n], prot[:, 1, :, 0:n]
                tt(s0, rotc[:, :, lo], ec, ALU.mult)
                link(tt(s1, rots[:, :, lo], es, ALU.mult))
                link(tt(rotc[:, :, hi], s0, s1, ALU.subtract))
                tt(s0, rotc[:, :, lo], es, ALU.mult)
                link(tt(s1, rots[:, :, lo], ec, ALU.mult))
                link(tt(rots[:, :, hi], s0, s1, ALU.add))
                n *= 2
                if n == NCH // 2:
                    weights_lo(M + 5)
                if n < NCH:
                    cmul((p(9), p(6)), (p(9), p(6)), (p(9), p(6)), [p(17), p(18), p(19), p(20)])
            dve.tensor_copy(mag8, p(4))
            dve.memset(hbd.rearrange("p a b c d -> p (a b c d)"), 0.0).then_inc(pw_ready, 1)
            dve.wait_ge(pw_ready, 1)

            def input_table(c):
                cs = slice(c * CGP, (c + 1) * CGP)

                def steps_of(pw):
                    return pw[:, cs, T8 - 1::-1].unsqueeze(3).to_broadcast([P, CGP, T8, SG])

                def chans_of(v):
                    return v[:, cs, :].unsqueeze(2).to_broadcast([P, CGP, T8, SG])

                wr, wi = (wext[:, i, :, :].rearrange("p g (t c) -> p g t c", t=T8) for i in range(2))
                s = tmp[:, 1, :].rearrange("p (g t c) -> p g t c", g=CGP, t=T8)
                tt(wr, steps_of(pw_re), chans_of(bc[:, 0, :, :]), ALU.mult)
                link(tt(s, steps_of(pw_im), chans_of(bc[:, 1, :, :]), ALU.mult))
                link(tt(wr, wr, s, ALU.subtract))
                tt(wi, steps_of(pw_re), chans_of(bc[:, 1, :, :]), ALU.mult)
                link(tt(s, steps_of(pw_im), chans_of(bc[:, 0, :, :]), ALU.mult))
                tt(wi, wi, s, ALU.add).then_inc(wext_ready, 1)

            def states(c):
                cs = slice(c * CGP, (c + 1) * CGP)
                name = f"state{c}"
                full(dve, name)
                b = bank[jobs.bank(name)]
                vr, vi = (b[:, i * 256:(i + 1) * 256].rearrange("p (g j) -> p g j", g=CGP) for i in range(2))
                t0, t1, t2, t3 = (tmp[:, i // 2, i % 2 * 256:i % 2 * 256 + 256].rearrange("p (g j) -> p g j", g=CGP)
                                  for i in range(4))
                rc, rs = rotc[:, cs, :], rots[:, cs, :]
                tt(t0, vr, rc, ALU.mult)
                tt(t1, vi, rs, ALU.mult)
                tt(t2, vi, rc, ALU.mult)
                tt(t3, vr, rs, ALU.mult).then_inc(bank_read[jobs.bank(name)], 1)
                was_read(dve, name)
                tt(t0, t0, t1, ALU.add)
                link(tt(t2, t2, t3, ALU.subtract))
                for g in range(CGP):
                    dc = mag8[:, c * CGP + g:c * CGP + g + 1].to_broadcast([P, NCH])
                    dve.tensor_tensor_scan(t1[:, g, :], dc, t0[:, g, :], 0.0, ALU.mult, ALU.add)
                    last = dve.tensor_tensor_scan(t3[:, g, :], dc, t2[:, g, :], 0.0, ALU.mult, ALU.add)
                link(last)
                tt(t0, t1, rc, ALU.mult)
                link(tt(t2, t3, rs, ALU.mult))
                for a in range(2):
                    q = slice(64 * a, 64 * a + 64)
                    last = tt(hbd[q, 0, :, a, 1:NCH], t0[q, :, 0:NCH - 1], t2[q, :, 0:NCH - 1], ALU.subtract)
                link(last)
                tt(t0, t1, rs, ALU.mult)
                link(tt(t2, t3, rc, ALU.mult))
                for a in range(2):
                    q = slice(64 * a, 64 * a + 64)
                    last = tt(hbd[q, 1, :, a, 1:NCH], t0[q, :, 0:NCH - 1], t2[q, :, 0:NCH - 1], ALU.add)
                last.then_inc(states_ready, 1)
                dve.wait_ge(states_ready, c + 1)

            weights_lo(M + 6)
            input_table(0)
            weights_lo(M + 7)
            weights_lo(M + 8)
            dve.wait_ge(rel_in, 16 * HEADS)
            link(dve.memset(relb[0:CHUNK, :, 0:CHUNK], -1e30))

            def gelu_end(c):
                dve.wait_ge(ytanh, c + 1)
                stt(yT[:, c, :], tmp[:, c % 2, :], 1.0, yT[:, c, :], ALU.add, ALU.mult).then_inc(y_ready, 1)
                dve.wait_ge(y_ready, c + 1)

            for i in range(STEPS):
                if i < HEADS:
                    if i:
                        full(dve, f"probT{i - 1}_2")
                    for q in range(TT):
                        name, nk = f"score{i}_{q}", (q + 1) * P
                        full(dve, name)
                        b = bank[jobs.bank(name)]
                        near = min(nk, REL)
                        if nk > near:
                            dve.tensor_scalar(att[:, q, 0:nk - near], b[:, 0:nk - near], SCALE, col("rb_far", i),
                                              ALU.mult, ALU.add)
                        read(name, stt(att[:, q, nk - near:nk], b[:, nk - near:nk], SCALE, relb[:, i, 0:near][:, ::-1],
                                       ALU.mult, ALU.add))
                        was_read(dve, name)
                        dve.tensor_reduce(stat[:, 40 + q:41 + q], att[:, q, 0:nk], AX, ALU.max,
                                          negate=True).then_inc(max_ready, 1)
                    for q in range(TT):
                        nk = (q + 1) * P
                        dve.wait_ge(exp_ready, TT * i + q + 1)
                        link(dve.reciprocal(stat[:, 56 + q:57 + q], stat[:, 44 + q:45 + q]))
                        last = dve.tensor_scalar(att[:, q, 0:nk], att[:, q, 0:nk], stat[:, 56 + q:57 + q], None, ALU.mult)
                    last.then_inc(prob_ready, 1)
                weights_lo(M + 9 + i)
                if i == HEADS:
                    for c in range(CT):
                        tile_lo(f"za{c}", za_lo[:, c, :], zaT[:, c, :], za_hi[:, c, :])
                for n in range(2):
                    g = 2 * i + n
                    if g < 2 * CT:
                        name = f"gate{g}"
                        dst = (zaT if g < CT else zsT)[:, g % CT, :]
                        dve.wait_ge(th_ready, g + 1)
                        read(name, stt(dst, dst, 1.0, bank[jobs.bank(name)][:, :], ALU.add, ALU.mult))
                if i % 2 == 1 and i < 2 * CT:
                    c, name = i // 2, f"lags_{i // 2}"
                    full(dve, name)
                    if c:
                        full(dve, f"near{c - 1}")
                    dve.tensor_scalar(kbd[:, T8, :], ident, col("skip", c), None, ALU.mult)
                    read(name, tt(kbd[:, 0:T8, :].rearrange("p d (g c) -> p d g c", g=CG),
                                  bank[jobs.bank(name)][:, 0:P].rearrange("p (d c) -> p d c", d=T8).unsqueeze(2)
                                  .to_broadcast([P, T8, CG, SG]),
                                  group_of.unsqueeze(1).unsqueeze(3).to_broadcast([P, T8, CG, SG]), ALU.mult))
                    was_read(dve, name)
                    dve.memset(stat[:, 63:64], 0.0).then_inc(kbd_ready, 1)
                if i < HEADS:
                    name, r = f"pv{i}", slice(64 * (i % 2), 64 * (i % 2) + 64)
                    full(dve, name)
                    was_read(dve, f"gate{i // 2}")
                    z = zaT[r, i // 2, :]
                    read(name, stt(z, bank[jobs.bank(name)][r, :], 0.5, z, ALU.mult, ALU.mult))
                if i in (GELU_STEP, GELU_STEP + 1):
                    cs = range(2 * (i - GELU_STEP), 2 * (i - GELU_STEP) + 2)
                    for c in cs:
                        y, near, s = yT[:, c, :], uT[:, c, :, :].rearrange("p t j -> p (t j)"), tmp[:, c % 2, :]
                        dve.wait_ge(y_in, 16)
                        was_read(dve, f"near{c}")
                        link(tt(y, y, near, ALU.add))
                        link(tt(s, y, y, ALU.mult))
                        link(dve.tensor_scalar(s, s, GELU_A, 1.0, ALU.mult, ALU.add))
                        tt(s, s, y, ALU.mult).then_inc(ygelu_in, 1)
                    for c in cs:
                        gelu_end(c)
                    for c in cs:
                        tile_lo(f"y{c}", y_lo[:, c, :], yT[:, c, :], y_hi[:, c, :])
                if i % 2 == 1 and i < 2 * CT:
                    states(i // 2)
                    if i // 2 + 1 < CT:
                        input_table(i // 2 + 1)
            weights_lo(M + 21)
            weights_lo(M + 22)
            for c in range(CT):
                name = f"glu{CT + c}"
                full(dve, name)
                read(name, dve.tensor_scalar(tmp[:, 0, :], bank[jobs.bank(name)][:, :], 0.5, col("b_glu", c),
                                             ALU.mult, ALU.add))
                was_read(dve, name)
                was_read(dve, f"glu{c}")
                link(stt(tmp[:, 1, :], ysT[:, c, :], 1.0, tmp[:, 0, :], ALU.add, ALU.mult))
                stt(ysT[:, c, :].rearrange("p (j t) -> p t j", t=T8), tmp[:, 1, :].rearrange("p (t j) -> p t j", t=T8),
                    0.25, zsT[:, c, :].rearrange("p (j t) -> p t j", t=T8), ALU.mult, ALU.mult).then_inc(glu_ready, 1)
                dve.wait_ge(glu_ready, c + 1)
            weights_lo(M + 23)
            for c in range(CT):
                tile_lo(f"ys{c}", ys_lo[:, c, :], ysT[:, c, :], ys_hi[:, c, :])
            for d in range(KT):
                if d == 4:
                    weights_lo(M + 24)
                name = f"ao{d}"
                full(dve, name)
                was_read(dve, f"gate{2 * CT + d}")
                read(name, stt(gaT[:, d, :], gaT[:, d, :], 1.0, bank[jobs.bank(name)][:, :], ALU.add, ALU.mult))
            weights_lo(M + 25)
            for d in range(KT):
                if d == 4:
                    weights_lo(M + 26)
                name = f"so{d}"
                full(dve, name)
                was_read(dve, f"gate{2 * CT + KT + d}")
                read(name, stt(gsT[:, d, :], gsT[:, d, :], 1.0, bank[jobs.bank(name)][:, :], ALU.add, ALU.mult))
                if d:
                    tile_lo(f"ga{d - 1}", ga_lo[:, d - 1, :], gaT[:, d - 1, :], ga_hi[:, d - 1, :])
                was_read(dve, name)
                was_read(dve, f"ao{d}")
                tt(gaT[:, d, :], gaT[:, d, :], gsT[:, d, :], ALU.add).then_inc(merged, 1)
            tile_lo(f"ga{KT - 1}", ga_lo[:, KT - 1, :], gaT[:, KT - 1, :], ga_hi[:, KT - 1, :])
            for u in range(27, 30):
                weights_lo(M + u)
            dve.wait_ge(x_back, 16)
            residual("fin", 0.5)
            dve.wait_ge(gfin_in, 16)
            for t in range(TT):
                dve.wait_ge(root_mean, 4 * TT + t + 1)
                stt(xres[:, t, :], xres[:, t, :], stat[:, 52 + t:53 + t], gfin, ALU.mult, ALU.mult).then_inc(final_ready, 1)


_INS = ["x", "cols", "cst", "wbd", "w_in", "dft_s", "w_out", "w_gate", "w_up", "w_down", "gf", "w_in2",
        "relp", "bc", "w_glu", "w_ao", "w_so", "w_out2", "gfin"]


def lay_out(i):
    f = {k: np.ascontiguousarray(np.asarray(v)) for k, v in i.items()}

    def tiles(v):
        return v.reshape(-1, P).T

    def pairs(v):
        return v.reshape(GP, 2, NS, -1).transpose(1, 2, 0, 3).reshape(P, GP, -1)

    bd = np.zeros((P, 4, CT, P), np.float32)
    for j, name in enumerate(("lru_wa_f", "lru_wx_f", "lru_wa_b", "lru_wx_b")):
        w = f[name].reshape(CT, 2, 64, 64)
        for a in range(2):
            bd[64 * a:64 * a + 64, j, :, 64 * a:64 * a + 64] = w[:, a].transpose(1, 0, 2)
    parts = {
        "g1": tiles(f["norm1_g"]), "g2": tiles(f["norm2_g"]), "gb2": tiles(f["norm_gain_2"][0]),
        "conv_w": tiles(f["conv_w"].reshape(-1)), "conv_b": tiles(f["conv_b"]),
        "bias_lru": np.concatenate([tiles(f[n]) for n in ("lru_ba_f", "lru_bx_f", "lru_ba_b", "lru_bx_b")], 1),
        "lam": np.concatenate([tiles(f["lru_lam_f"]), tiles(f["lru_lam_b"])], 1),
        "b_glu": tiles(f["b_glu_2"][0]), "gate_b": tiles(f["gate_bias_2"][0]),
        "a_re": pairs(f["ssm_a_re_2"][0])[:, :, 0], "a_im": pairs(f["ssm_a_im_2"][0])[:, :, 0],
        "log_dt": pairs(np.repeat(f["ssm_log_dt_2"][0][:, None], NS, 1))[:, :, 0],
        "skip": tiles(f["ssm_d_2"][0]),
        "rb_far": np.repeat(f["rel_bias_2"][0][:, NREL - 1][None], P, 0),
        "w_router": np.pad(f["w_router"].reshape(KT, P, NE).transpose(1, 0, 2), ((0, 0), (0, 0), (0, NE))).reshape(P, -1),
    }
    cols = np.concatenate([parts[n] for n, _ in COLS], 1)
    c_re, c_im = (f[n][0].transpose(0, 2, 1) for n in ("ssm_c_re_2", "ssm_c_im_2"))
    bc = np.stack([pairs(f["ssm_b_re_2"][0]), pairs(f["ssm_b_im_2"][0]), pairs(c_re), pairs(c_im)], 1)
    n = np.arange(P)
    ang = 2 * np.pi * (np.outer(n, n) % P) / P
    cst = np.concatenate([np.eye(P), np.cos(ang), np.sin(ang), np.tile(np.arange(CAP), (P, 1)),
                          np.arange(P)[:, None] // SG == np.arange(CG)[None]], 1).astype(np.float32)
    n = np.arange(S)
    ang = 2 * np.pi * (np.outer(n, n) % S) / S
    dft_s = (np.stack([np.cos(ang), -np.sin(ang)]) / np.sqrt(S * P)).astype(np.float32)
    return {
        "x": f["x"][0], "cols": cols, "cst": cst, "wbd": bd.reshape(P, -1), "w_in": f["w_in"], "dft_s": dft_s,
        "w_out": f["w_out"], "w_gate": f["w_gate"], "w_up": f["w_up"], "w_down": f["w_down"],
        "gf": f["normf_g"], "w_in2": f["w_in_2"][0],
        "relp": np.pad(f["rel_bias_2"][0], ((0, 0), (CHUNK, REL + P - CHUNK - NREL)), mode="edge"),
        "bc": bc.reshape(P, -1), "w_glu": f["w_glu_2"][0], "w_ao": f["w_attn_out_2"][0],
        "w_so": f["w_ssm_out_2"][0], "w_out2": f["w_out_2"][0], "gfin": f["final_gain_2"],
    }


def kernel(**inputs):
    import concourse.bacc as bacc
    from concourse.bass_utils import run_bass_kernel_spmd

    nc = bacc.Bacc("TRN2", target_bir_lowering=False, num_devices=1)
    arrays, args = {}, []
    for name, a in lay_out(inputs).items():
        a = np.ascontiguousarray(a)
        arrays[f"in_{name}"] = a
        args.append(nc.dram_tensor(f"in_{name}", a.shape, mybir.dt.from_np(a.dtype), kind="ExternalInput").ap())
    args.append(nc.dram_tensor("out", (S, D), f32, kind="ExternalOutput").ap())
    args.append(nc.dram_tensor("u_scratch", (LRU, T8, NCH), f32, kind="Internal").ap())
    args.append(nc.dram_tensor("y_scratch", (LRU, T8, NCH), f32, kind="Internal").ap())
    args.append(nc.dram_tensor("x_scratch", (S, D), f32, kind="Internal").ap())
    build(nc, *args)
    r = run_bass_kernel_spmd(nc, [arrays], core_ids=[0])
    return r.results[0]["out"].reshape(1, S, D)
```

```python
from contextlib import ExitStack

import numpy as np
import concourse.bass as bass
from concourse import mybir

f32, f32r = mybir.dt.float32, mybir.dt.float32r
ALU = mybir.AluOpType
ACT = mybir.ActivationFunctionType
AX = mybir.AxisListType.X

P = 128
S = 512
D = 1024
TT = S // P
KT = D // P
LRU = D // 2
CT = LRU // P
CONV = 4
CONV_LEFT = CONV // 2
NE = 16
CAP = 2 * S // NE
FF = 2 * D
EPS = 1e-6
GELU_C = 0.7978845608028654
GELU_A = 0.044715
LRU_C = 8.0

HEADS, DH = 8, 64
NREL, CHUNK = 192, 64
SCALE = DH ** -0.5
REL = 256
GRP, SG, NS = 32, 16, 64
T8 = P // SG
NCH = S // T8
GP = GRP // 2
CGP = GP // CT
CG = 2 * CGP
TWO_PI = 2 * np.pi
PI_HI = 6.28125
PI_MID = float(np.float32(np.round((TWO_PI - PI_HI) * 2 ** 20) / 2 ** 20))
PI_LO = float(np.float32(TWO_PI - PI_HI - PI_MID))
ROUND = 1.5 * 2 ** 23

SBUF = 53200
UNIT = 2048
RING = 12
RING2 = 3
B1_UNITS = 13
E_UNITS = 24
EARLY = 6
MOE_END = B1_UNITS + NE * E_UNITS

COLS = [("g1", KT), ("g2", KT), ("gb2", KT), ("conv_w", CONV * CT), ("conv_b", CT),
        ("bias_lru", 4 * CT), ("lam", 2 * CT), ("b_glu", KT), ("gate_b", 2 * KT),
        ("a_re", GP), ("a_im", GP), ("log_dt", GP), ("skip", CT), ("rb_far", HEADS),
        ("w_router", KT * 2 * NE)]
COL, NCOLS = {}, 0
for _name, _w in COLS:
    COL[_name] = NCOLS
    NCOLS += _w
NCST = 3 * P + CAP + CG


class Jobs:

    def __init__(self, bank_full, unit_used):
        self.bank_full, self.unit_used = bank_full, unit_used
        self.uses, self.told, self.of, self.turn = [0] * 8, [0] * 8, {}, 0

    def add(self, name, bank=None, unit=None):
        if bank is None:
            bank = self.turn
            self.turn = (self.turn + 1) % 8
        if unit is None:
            self.told[bank] += 1
            end = (self.bank_full[bank], self.told[bank])
        else:
            end = (self.unit_used, unit + 1)
        self.of[name] = (bank, self.uses[bank], end)
        self.uses[bank] += 1

    def bank(self, name):
        return self.of[name][0]

    def before(self, name):
        return self.of[name][1]

    def end(self, name):
        return self.of[name][2]


def build(nc, x, cols_d, cst_d, wbd_d, w_in, dft_s, w_out, w_gate, w_up, w_down, gf_d, w_in2, relp,
          bc_d, w_glu, w_ao, w_so, w_out2, gfin_d, out, u_dram, y_dram, x_dram):
    with ExitStack() as ctx:
        base = (nc.sbuf_base + 31) // 32 * 32
        ends = {}

        def area(name, off, *shape, parts=P, dtype=f32):
            n = int(np.prod(shape))
            assert off >= 0 and off + n <= SBUF, (name, off + n)
            ends[name] = off + -(-n // 8) * 8
            v = nc.alloc_sbuf_tensor_at(name, [P, n], dtype, offset=base + 4 * off)[0:parts, :]
            if len(shape) == 1:
                return v
            letters = "abcd"[:len(shape)]
            return v.rearrange(f"p ({' '.join(letters)}) -> p {' '.join(letters)}",
                               **dict(zip(letters[1:], shape[1:])))

        def area_r(name, off, *shape):
            return area(name, off, *shape, dtype=f32r)

        def flat(v):
            return v.rearrange("p a b -> p (a b)")

        ring = [area(f"ring{s}", s * UNIT, UNIT) for s in range(RING)]
        ring_r = [area_r(f"ring{s}_r", s * UNIT, UNIT) for s in range(RING)]
        xres = area("xres", RING * UNIT, TT, D)
        nrm = area("nrm", ends["xres"], TT, D)
        hT = area("hT", ends["nrm"], KT, S)
        hT_hi = area_r("hT_hi", ends["nrm"], KT, S)
        hT_lo = area_r("hT_lo", ends["xres"], KT, S)
        cols = area("cols", ends["hT"], NCOLS)
        cst = area("cst", ends["cols"], NCST)
        stat = area("stat", ends["cst"], 64)
        hbias = area("hbias", ends["stat"], 4 * CT + 3 * KT)
        kpos = area("kpos", ends["hbias"], 2 * CT)
        kneg = area("kneg", ends["kpos"], 2 * CT)
        Z = ends["kneg"]
        ident, dft, slotrow = cst[:, 0:P], cst[:, P:3 * P], cst[:, 3 * P:3 * P + CAP]
        group_of = cst[:, 3 * P + CAP:NCST]

        def col(name, i=0, n=1):
            return cols[:, COL[name] + i:COL[name] + i + n]

        mixT = area("mixT", Z, 2 * CT, S)
        lrux = area("lrux", ends["mixT"], CT, S + CONV)
        conv = area("conv", ends["lrux"], CT, S)
        gt = area("gt", ends["conv"], 2, 4, S)
        hi_b1 = [area_r(f"hi{i}", ends["conv"] + i * UNIT, UNIT) for i in range(2)]
        mix_hi = hT_hi
        mix_lo = area_r("mix_lo", Z, 2 * CT, S)
        hi_dft = [area_r("hi_cos", ends["gt"], UNIT), ring_r[5]]
        four_hi = area_r("four_hi", 0, TT, CT, 2 * P)
        four_lo = area_r("four_lo", ends["four_hi"], TT, CT, 2 * P)
        aff = area("aff", Z, TT, NE + 1)
        posT = area("posT", ends["aff"], TT, NE + 1)
        sel = area("sel", ends["posT"], TT, CAP)
        gsel = area("gsel", ends["sel"], TT, 2, CAP)
        gselT = area("gselT", ends["gsel"], TT, P)
        xinT = area("xinT", ends["gselT"], KT, CAP)
        xg = area("xg", ends["xinT"], 512)
        th = area("th", ends["xg"], 2, 512)
        act = area("act", ends["th"], 2, 512)
        actT = area("actT", ends["act"], KT, P)
        eo = area("eo", ends["actT"], 512)
        score = area("score", ends["xg"], S, parts=NE)
        top = area("top", ends["score"], 8, parts=NE)
        taken = area("taken", ends["top"], S, parts=NE)
        rank = area("rank", ends["taken"], S, parts=NE)
        ones = area("ones", ends["rank"], S, parts=NE)
        logT = area("logT", ends["ones"], P)
        assert ends["logT"] <= ends["eo"]
        early = [area(f"early{i}", ends["eo"] + i * UNIT, UNIT) for i in range(EARLY - 2)]
        early += [area(f"early{EARLY - 2 + i}", ends["nrm"] + i * UNIT, UNIT) for i in range(2)]
        qT = area("qT", 0, CT, S)
        kT = area("kT", (RING2 + 3) * UNIT, CT, S)
        v_s = area("v_s", ends["kT"], TT, LRU)
        zaT = area("zaT", ends["v_s"], CT, S)
        zsT = area("zsT", ends["zaT"], CT, S)
        gaT = area("gaT", ends["zsT"], KT, S)
        assert ends["gaT"] <= RING * UNIT
        hi_b2 = [ring_r[RING2 + 1 + i] for i in range(2)]
        att = area("att", RING * UNIT, TT, S)
        relb = area("relb", ends["att"], HEADS, REL)
        assert ends["relb"] <= ends["xres"]
        pT = area("pT", Z, 10 * P)
        gfin = area("gfin", Z, D)
        rotc = area("rotc", ends["pT"], GP, NCH)
        rots = area("rots", ends["rotc"], GP, NCH)
        mag8 = area("mag8", ends["rots"], GP)
        pw_re = area("pw_re", ends["mag8"], GP, T8 + 1)
        pw_im = area("pw_im", ends["pw_re"], GP, T8 + 1)
        pw_in = area("pw_in", ends["pw_im"], GP, T8 + 1)
        bc = area("bc", ends["pw_in"], 4, GP, SG)
        bbd = area("bbd", ends["bc"], 2, GP, 2 * SG)
        uT = area("uT", ends["bbd"], CT, T8, NCH)
        ubuf = area("ubuf", ends["uT"], CG, NCH)
        ybuf = area("ybuf", ends["ubuf"], CG, NCH)
        hbd = area("hbd", ends["ybuf"], 2, CGP, 2, NCH)
        tmp = area("tmp", ends["hbd"], 2, 512)
        wext = area("wext", ends["tmp"], 2, CGP, P)
        wc = area("wc", ends["wext"], 2, CGP, (T8 + 1) * SG)
        st = area("st", ends["wc"], 2, CGP, P)
        kbd = area("kbd", ends["st"], T8 + 1, P)
        gsT = area("gsT", ends["tmp"], KT, S)
        gfb = area("gfb", ends["tmp"], D)
        prep = area("prep", ends["wext"], 24, GP)
        prot = area("prot", ends["prep"], 2, GP, NCH // 2)
        assert ends["gsT"] <= ends["kbd"] and ends["prot"] <= ends["kbd"] and ends["gfb"] <= ends["wext"]
        za_hi = area_r("za_hi", ends["pT"], CT, S)
        y_hi = area_r("y_hi", ends["za_hi"], CT, S)
        ga_hi = area_r("ga_hi", ends["pT"], KT, S)
        ys_hi = area_r("ys_hi", ends["bbd"], CT, S)
        za_lo, y_lo, ys_lo, ga_lo = (area_r(f"{n}_lo", ends[n] - w * S, w, S)
                                     for n, w in (("zaT", CT), ("qT", CT), ("kT", CT), ("gaT", KT)))
        assert ends["ga_hi"] <= ends["bbd"]
        yT = qT
        ysT = kT

        bank = [ctx.enter_context(nc.psum_tensor(f"bank{b}", [P, 512], f32)) for b in range(8)]

        def sem(name):
            return ctx.enter_context(nc.semaphore(name))

        ring_full = [sem(f"ring_full{s}") for s in range(RING)]
        early_in = [sem(f"early_in{i}") for i in range(EARLY)]
        unit_used = sem("unit_used")
        w_hi, w_lo = sem("w_hi"), sem("w_lo")
        hi_ready, lo_ready = sem("hi_ready"), sem("lo_ready")
        x_saved, x_back = sem("x_saved"), sem("x_back")
        bank_full = [sem(f"bank_full{b}") for b in range(8)]
        bank_read = [sem(f"bank_read{b}") for b in range(8)]
        x_in = [sem(f"x_in{t}") for t in range(TT)]
        cols_in, cst_in, gf_in, rel_in = sem("cols_in"), sem("cst_in"), sem("gf_in"), sem("rel_in")
        bc_in, gfin_in = sem("bc_in"), sem("gfin_in")
        dve_step, act_step, pool_step = sem("dve_step"), sem("act_step"), sem("pool_step")
        square_sum, root_mean, normed = sem("square_sum"), sem("root_mean"), sem("normed")
        pad_zero, halves, lam_ln, k_ready = (
            sem("pad_zero"), sem("halves"), sem("lam_ln"), sem("k_ready"))
        conv_ready, acts_ready, m2_ready, root_ready, lru_done = (
            sem("conv_ready"), sem("acts_ready"), sem("m2_ready"), sem("root_ready"), sem("lru_done"))
        gelu_in, gelu_tanh, gt_free = sem("gelu_in"), sem("gelu_tanh"), sem("gt_free")
        soft_in, soft_exp, aff_ready, pos_ready = (
            sem("soft_in"), sem("soft_exp"), sem("aff_ready"), sem("pos_ready"))
        sel_ready, tanh_ready, act_ready = sem("sel_ready"), sem("tanh_ready"), sem("act_ready")
        u_out, u_in, y_out, y_in = sem("u_out"), sem("u_in"), sem("y_out"), sem("y_in")
        prep_in, prep_exp, prep_sin, sin_arg = (
            sem("prep_in"), sem("prep_exp"), sem("prep_sin"), sem("sin_arg"))
        wext_ready, wc_ready, pw_ready, states_ready = (
            sem("wext_ready"), sem("wc_ready"), sem("pw_ready"), sem("states_ready"))
        bbd_ready, ygelu_in, ytanh, y_ready = (
            sem("bbd_ready"), sem("ygelu_in"), sem("ytanh"), sem("y_ready"))
        max_ready, exp_ready, prob_ready = sem("max_ready"), sem("exp_ready"), sem("prob_ready")
        th_ready, glu_ready, merged = sem("th_ready"), sem("glu_ready"), sem("merged")
        between, final_ready, stored = sem("between"), sem("final_ready"), sem("stored")

        jobs = Jobs(bank_full, unit_used)
        for k in range(KT):
            jobs.add(f"xT{k}", k)
        order_b1 = [("in", n) for n in range(9)] + [("four", c) for c in range(CT)] + [
            ("lru", 0), ("in", 9), ("in", 10), ("lru", 1), ("in", 11), ("lru", 2), ("mix", 0), ("mix", 1),
            ("lru", 3), ("mix", 2), ("mix", 3)]
        for what, n in order_b1:
            if what == "in":
                jobs.add(f"in{n}", unit=n // 2 if n % 2 else None)
            elif what == "four":
                for half in range(2):
                    jobs.add(f"four{n}_{half}")
            elif what == "lru":
                for i in range(4):
                    jobs.add(f"lru{n}_{i}", unit=6 if (n, i) == (CT - 1, 3) else None)
            else:
                jobs.add(f"mix{n}", unit=8 if n == CT - 1 else None)
        for o in range(8):
            jobs.add(f"out{o}", unit=12 if o == 7 else None)
        for k in range(KT):
            jobs.add(f"h2T{k}", k)
        jobs.add("logitT", 0)
        jobs.add("logits", 1)
        jobs.add("scoreT", 2)
        jobs.add("posT", 3)
        moe_uses, moe_told = list(jobs.uses), list(jobs.told)
        EU = [3, 2, 2, 1, 1, 2, 2, 3]
        EF = [3, 1, 1, 1, 1, 2, 2, 2]
        for b in range(8):
            jobs.uses[b] += NE * EU[b]
            jobs.told[b] += NE * EF[b]
        for k in range(KT):
            jobs.add(f"yT{k}", k)
        M = MOE_END
        for n in range(12):
            jobs.add(f"proj{n}", unit=M + n // 2 if n % 2 else None)
        for u in range(2):
            for t in range(TT):
                jobs.add(f"v{u}_{t}", unit=M + 6 + u if t == TT - 1 else None)
        GELU_STEP = 2 * CT + 2
        STEPS = 12
        for i in range(STEPS):
            if i < HEADS:
                for q in range(TT):
                    jobs.add(f"score{i}_{q}")
            for n in range(2):
                jobs.add(f"gate{2 * i + n}", unit=M + 8 + i if n else None)
            if i % 2 == 1 and i < 2 * CT:
                jobs.add(f"lags_{i // 2}")
            if i < HEADS:
                for b in range(3):
                    jobs.add(f"probT{i}_{b}")
                jobs.add(f"pv{i}")
            if i % 2 == 0 and 2 <= i <= 2 * CT:
                jobs.add(f"ssm{i // 2 - 1}")
            if i % 2 == 0 and i < 2 * CT:
                for name in ("st_re", "st_im"):
                    jobs.add(f"{name}_{i // 2}")
            if i % 2 == 1 and i < 2 * CT:
                jobs.add(f"state{i // 2}")
                jobs.add(f"near{i // 2}")
        last_units = [("ao", 0), ("glu", 0), ("glu", 4), ("ao", 4), ("so", 0), ("so", 4)]
        for u, (what, n0) in enumerate(last_units):
            for n in range(n0, n0 + 4):
                jobs.add(f"{what}{n}", unit=M + 20 + u if n == n0 + 3 else None)
        for o in range(8):
            jobs.add(f"fin{o}", unit=M + 29 if o == 7 else None)

        def full(eng, name):
            eng.wait_ge(*jobs.end(name))

        def was_read(eng, name):
            eng.wait_ge(bank_read[jobs.bank(name)], jobs.before(name) + 1)

        def read(name, ins):
            ins.then_inc(bank_read[jobs.bank(name)], 1)

        def slot_of(unit):
            return unit % RING if unit < MOE_END else 1 + (unit - MOE_END) % RING2

        def moe_slot(n):
            assert n < RING or n >= RING + EARLY
            return (B1_UNITS + (n if n < RING else n - EARLY)) % RING

        in_ring = [n for n in range(NE * E_UNITS) if n < RING or n >= RING + EARLY]
        last_of = {moe_slot(n): B1_UNITS + n for n in in_ring}
        loads_b1 = [sum(u % RING == s for u in range(B1_UNITS)) for s in range(RING)]
        loads_e0 = [sum(moe_slot(n) == s for n in in_ring if n < E_UNITS) for s in range(RING)]

        def loaded(eng, unit):
            s = slot_of(unit)
            if unit < MOE_END:
                n = unit // RING + 1
            else:
                n = loads_b1[s] + loads_e0[s] + 2 * (NE - 1) + (unit - MOE_END) // RING2 + 1
            eng.wait_ge(ring_full[s], 16 * n)

        def view(unit, inner):
            return ring[slot_of(unit)].rearrange("p (k n) -> p k n", n=inner)

        split_units = [*range(6), *range(7, 13), *range(M, M + 30)]
        split_tiles = [f"{n}{k}" for n, w in (("xT", KT), ("four", CT), ("mix", CT), ("lru", CT), ("yT", KT), ("za", CT), ("y", CT),
                                              ("ys", CT), ("ga", KT)) for k in range(w)]
        split_tiles = [h for t in split_tiles for h in ([t + "_0", t + "_1"] if t[:4] == "four" else [t])]
        in_sbuf = [t for t in split_tiles if t not in jobs.of]

        def hi_of(unit):
            if unit >= M:
                return hi_b2[(unit - M) % 2]
            if unit < 6:
                return ring_r[RING - 2 + unit % 2]
            return hi_dft[unit - 7] if unit < 9 else hi_b1[(unit - 9) % 2]

        def high_stands(eng, tile):
            eng.wait_ge(hi_ready, split_tiles.index(tile) + 1)

        def both_stand(eng, tile):
            if tile in jobs.of:
                was_read(eng, tile)
            else:
                eng.wait_ge(lo_ready, in_sbuf.index(tile) + 1)

        def view_r(v, inner):
            return v.rearrange("p (k n) -> p k n", n=inner)

        def both(unit, inner):
            return view_r(hi_of(unit), inner), view_r(ring_r[slot_of(unit)], inner)

        block = ctx.enter_context(nc.Block())

        @block.sync
        def _(sp):
            def load(unit, src, inner):
                s = slot_of(unit)
                if unit >= MOE_END:
                    v = unit - MOE_END
                    last = last_of[s] if v < RING2 else unit - RING2
                    sp.wait_ge(unit_used, last + 1)
                elif unit >= RING:
                    sp.wait_ge(unit_used, unit - RING + 1)
                sp.dma_start(view(unit, inner), src).then_inc(ring_full[s], 16)

            for t in range(TT):
                sp.dma_start(xres[:, t, :], x[t * P:(t + 1) * P, :]).then_inc(x_in[t], 16)
            w_in_k = w_in.rearrange("(k p) n -> p k n", p=P)
            for u, c in enumerate((0, 1, 4, 5, 2, 3)):
                load(u, w_in_k[:, :, 256 * c:256 * c + 256], 256)
            load(6, wbd_d.rearrange("p (k n) -> p k n", n=P), P)
            for i in range(2):
                load(7 + i, dft_s[i].rearrange("(k p) n -> p k n", p=P), S)
            w_out_m = w_out.rearrange("(m p) n -> p m n", p=P)
            for u, m in enumerate((4, 6, 0, 2)):
                if u in (1, 2):
                    sp.wait_ge(unit_used, 4 + u)
                if u == 3:
                    sp.wait_ge(unit_used, 9)
                load(9 + u, w_out_m[:, m:m + 2, :], D)

            def load_expert(e, m, dst, arrived):
                if m < KT * 2:
                    w, k = (w_gate, w_up)[m % 2], m // 2
                    src = w[bass.ds(e, 1), k * P:(k + 1) * P, :].rearrange("a p n -> p (a n)")
                else:
                    j = m - 2 * KT
                    src = w_down[bass.ds(e, 1), 2 * j * P:(2 * j + 2) * P, :].rearrange("a (i p) n -> p (a i) n", i=2)
                    dst = dst.rearrange("p (i n) -> p i n", i=2)
                sp.dma_start(dst, src).then_inc(arrived, 16)

            for n in range(2 * E_UNITS):
                e, m = n // E_UNITS, n % E_UNITS
                if RING <= n < RING + EARLY:
                    i = n - RING
                    if i == 0:
                        sp.wait_ge(unit_used, B1_UNITS)
                    elif i == EARLY - 2:
                        sp.wait_ge(*jobs.end("logitT"))
                    load_expert(e, m, early[i], early_in[i])
                    continue
                if n < RING:
                    former = B1_UNITS + n - RING
                elif n < 2 * RING + EARLY:
                    former = B1_UNITS + n - RING - EARLY
                else:
                    former = B1_UNITS + n - RING
                sp.wait_ge(unit_used, former + 1)
                load_expert(e, m, ring[moe_slot(n)], ring_full[moe_slot(n)])
            with sp.Fori(2, NE) as e:
                for m in range(E_UNITS):
                    s = moe_slot(2 * E_UNITS + m)
                    sp.wait_ge(unit_used, e * E_UNITS + (B1_UNITS + m - RING + 1))
                    load_expert(e, m, ring[s], ring_full[s])

            w2 = w_in2.rearrange("(k p) n -> p k n", p=P)
            order = [8, 9, 0, 1, 2, 3, 4, 5, 6, 7, 10, 11] + list(range(12, 20))
            for u, c in enumerate(order):
                load(MOE_END + u, w2[:, :, 256 * c:256 * c + 256], 256)
                if u == RING2 - 1:
                    for t in range(TT):
                        sp.wait_ge(between, t + 1)
                        sp.dma_start(x_dram[t * P:(t + 1) * P, :], xres[:, t, :]).then_inc(x_saved, 16)
            sp.wait_ge(x_saved, 16 * TT)
            sp.wait_ge(*jobs.end(f"pv{HEADS - 1}"))
            sp.dma_start(xres, x_dram.rearrange("(t p) n -> p t n", p=P)).then_inc(x_back, 16)
            k_ao, k_glu, k_so = (w.rearrange("(k p) n -> p k n", p=P) for w in (w_ao, w_glu, w_so))
            for u, (k_w, c) in enumerate(((k_ao, 0), (k_glu, 512), (k_glu, 0), (k_ao, 512), (k_so, 0), (k_so, 512))):
                load(MOE_END + 20 + u, k_w[:, :, c:c + 512], 512)
            for i in range(4):
                load(MOE_END + 26 + i, w_out2.rearrange("(m p) n -> p m n", p=P)[:, 2 * i:2 * i + 2, :], D)

            for t in range(TT):
                sp.wait_ge(final_ready, t + 1)
                sp.dma_start(out[t * P:(t + 1) * P, :], xres[:, t, :]).then_inc(stored, 16)
            sp.wait_ge(stored, 16 * TT)

        @block.tensor
        def _(pe):
            def start(name, **kw):
                b = jobs.bank(name)
                if jobs.before(name):
                    pe.wait_ge(bank_read[b], jobs.before(name))
                return bank[b]

            def finish(name, ins):
                who, _ = jobs.end(name)
                ins.then_inc(who, 1)

            def transposes(prefix, ready0):
                for t in range(TT):
                    pe.wait_ge(normed, ready0 + t + 1)
                    for k in range(KT):
                        b = start(f"{prefix}{k}") if t == 0 else bank[k]
                        last = pe.transpose(b[:, t * P:(t + 1) * P], nrm[:, t, k * P:(k + 1) * P], ident)
                        if t == TT - 1:
                            finish(f"{prefix}{k}", last)

            def split(unit):
                pe.wait_ge(w_lo, split_units.index(unit) + 1)

            def product(dst, a, b, first, last):
                pe.matmul(dst, a[0], b[1], start=first, stop=False)
                pe.matmul(dst, a[1], b[0], start=False, stop=False)
                return pe.matmul(dst, a[0], b[0], start=False, stop=last)

            def project(name, w, c0, rows, kn, tiles=None):
                if tiles is None:
                    b = start(name)
                for k in range(kn):
                    if tiles is not None:
                        both_stand(pe, f"{tiles}{k}")
                        if k == 0:
                            b = start(name)
                    last = product(b[:, :], [v[:, k, c0:c0 + P] for v in w], [v[:, k, :] for v in rows],
                                   k == 0, k == kn - 1)
                finish(name, last)

            def out_project(prefix, rows, unit0, ms, rows_ready):
                for u, m0 in enumerate(ms):
                    unit = unit0 + u
                    for m in range(m0, m0 + 2):
                        both_stand(pe, rows_ready(m))
                    split(unit)
                    w = both(unit, D)
                    tail = u == len(ms) - 1
                    for o in range(8):
                        t, n = o // 2, o % 2
                        b = start(f"{prefix}{o}") if u == 0 else bank[jobs.bank(f"{prefix}{o}")]
                        for i in range(2):
                            last = product(b[:, :], [v[:, m0 + i, t * P:(t + 1) * P] for v in rows],
                                           [v[:, i, n * 512:n * 512 + 512] for v in w], u == 0 and i == 0, tail and i == 1)
                        if tail:
                            finish(f"{prefix}{o}", last)
                    if not tail:
                        last.then_inc(unit_used, 1)

            pe.wait_ge(cst_in, 16)
            transposes("xT", 0)
            for what, n in order_b1:
                if what == "in":
                    if n % 2 == 0:
                        split(n // 2)
                    project(f"in{n}", both(n // 2, 256), (n % 2) * P, (hT_hi, hT_lo), KT, None if n else "xT")
                elif what == "four":
                    if n == 0:
                        for g in range(CT):
                            was_read(pe, f"in{4 + g}")
                    for half in range(2):
                        b = start(f"four{n}_{half}")
                        for i in range(2):
                            g = 2 * half + i
                            last = pe.matmul(b[:, 256 * i:256 * i + 256], mixT[:, CT + g, n * P:(n + 1) * P], dft,
                                             start=True, stop=True)
                        finish(f"four{n}_{half}", last)
                elif what == "lru":
                    if n == 0:
                        loaded(pe, 6)
                        wbd = view(6, P)
                    pe.wait_ge(conv_ready, n + 1)
                    for i in range(4):
                        b = start(f"lru{n}_{i}")
                        finish(f"lru{n}_{i}", pe.matmul(b[:, :], wbd[:, 4 * i + n, :], conv[:, n, :], start=True, stop=True))
                else:
                    if n == 0:
                        split(7)
                        for c in range(CT):
                            for half in range(2):
                                both_stand(pe, f"four{c}_{half}")
                    b = start(f"mix{n}")
                    for i in range(2):
                        if i == 1 and n == 0:
                            split(8)
                        w = both(7 + i, S)
                        for t in range(TT):
                            last = product(b[:, :], [v[:, t, n, i * P:(i + 1) * P] for v in (four_hi, four_lo)],
                                           [v[:, t, :] for v in w], i == 0 and t == 0, i == 1 and t == TT - 1)
                        if i == 0 and n == CT - 1:
                            last.then_inc(unit_used, 1)
                    finish(f"mix{n}", last)
            out_project("out", (mix_hi, mix_lo), 9, (4, 6, 0, 2),
                        lambda m: f"mix{m - CT}" if m >= CT else f"lru{m}")

            transposes("h2T", TT)
            b = start("logitT")
            wr = col("w_router", 0, KT * 2 * NE).rearrange("p (k e) -> p k e", k=KT)
            for k in range(KT):
                was_read(pe, f"h2T{k}")
                for t in range(TT):
                    last = pe.matmul(b[32 * t:32 * t + 32, 0:P], wr[:, k, :], hT[:, k, t * P:(t + 1) * P],
                                     start=(k == 0), stop=(k == KT - 1))
            finish("logitT", last)
            was_read(pe, "logitT")
            b = start("logits")
            finish("logits", pe.transpose(b[:, 0:P], logT, ident))
            pe.wait_ge(aff_ready, 1)
            b = start("scoreT")
            for t in range(TT):
                last = pe.transpose(b[0:NE, t * P:(t + 1) * P], aff[:, t, 0:NE], ident)
            finish("scoreT", last)
            pe.wait_ge(pos_ready, 1)
            b = start("posT")
            for t in range(TT):
                last = pe.transpose(b[:, t * NE:(t + 1) * NE], rank[:, t * P:(t + 1) * P], ident[0:NE, 0:NE])
            finish("posT", last)

            def expert(e, first):
                def bank_free(b, n):
                    pe.wait_ge(bank_read[b], e * EU[b] + (moe_uses[b] + n))

                def arrived(m):
                    if first and RING <= m < RING + EARLY:
                        pe.wait_ge(early_in[m - RING], 16)
                        return early[m - RING]
                    s = moe_slot(m if first else E_UNITS + m)
                    if first:
                        pe.wait_ge(ring_full[s], 16 * (loads_b1[s] + (1 if m < RING else loads_e0[s])))
                    else:
                        pe.wait_ge(ring_full[s], e * 32 + 16 * (loads_b1[s] + loads_e0[s] - 2 + m // RING + 1))
                    return ring[s]

                pe.wait_ge(sel_ready, 2 * e + 1)
                bank_free(0, 0)
                for t in range(TT):
                    for q in range(2):
                        last = pe.matmul(bank[0][CAP * q:CAP * q + CAP, :], sel[:, t, :],
                                         nrm[:, t, 512 * q:512 * q + 512], start=(t == 0), stop=(t == TT - 1))
                last.then_inc(bank_full[0], 1)
                pe.wait_ge(sel_ready, 2 * e + 2)
                bank_free(7, 0)
                for t in range(TT):
                    last = pe.transpose(bank[7][:, t * P:(t + 1) * P], gsel[:, t, :, :].rearrange("p a b -> p (a b)"), ident)
                last.then_inc(bank_full[7], 1)
                bank_free(0, 1)
                for j in range(4):
                    last = pe.transpose(bank[0][:, j * P:(j + 1) * P], xg[:, j * P:(j + 1) * P], ident)
                last.then_inc(bank_full[0], 1)
                bank_free(0, 2)
                for b in range(1, 5):
                    bank_free(b, 0)
                for m in range(2 * KT):
                    k, w = m // 2, arrived(m)
                    for q in range(4):
                        o = 64 * (q % 2)
                        last = pe.matmul(bank[1 + 2 * (m % 2) + q // 2][o:o + 64, :], xinT[:, k, :],
                                         w[:, q * 512:(q + 1) * 512], start=(k == 0), stop=(k == KT - 1))
                    last.then_inc(unit_used, 1)
                for b in range(2):
                    pe.wait_ge(act_ready, 2 * e + (b + 1))
                    bank_free(5 + b, 0)
                    for q in range(4):
                        last = pe.transpose(bank[5 + b][:, q * P:(q + 1) * P], act[:, b, q * P:(q + 1) * P], ident)
                    last.then_inc(bank_full[5 + b], 1)
                bank_free(5, 1)
                bank_free(6, 1)
                bank_free(7, 1)
                for j in range(8):
                    w = arrived(2 * KT + j).rearrange("p (i n) -> p i n", i=2)
                    for i in range(2):
                        kt = 2 * j + i
                        at = 64 * (kt // 4 % 2)
                        for n in range(2):
                            last = pe.matmul(bank[7][64 * n:64 * n + 64, :], actT[:, kt // 8 * 4 + kt % 4, at:at + 64],
                                             w[:, i, n * 512:n * 512 + 512], start=(kt == 0), stop=(kt == 15))
                    last.then_inc(unit_used, 1)
                for o, b in enumerate((0, 7, 1, 2, 3, 4, 5, 6)):
                    t, n = o // 2, o % 2
                    if o == 0:
                        bank_free(7, 2)
                    bank_free(b, EU[b] - 1)
                    pe.matmul(bank[b][:, :], gselT[64 * n:64 * n + 64, t, :], eo[64 * n:64 * n + 64, :],
                              start=True, stop=True).then_inc(bank_full[b], 1)

            expert(0, True)
            with pe.Fori(1, NE) as e:
                expert(e, False)

            transposes("yT", 2 * TT)
            h_both = (hT_hi, hT_lo)
            for n in range(12):
                unit = M + n // 2
                if n % 2 == 0:
                    split(unit)
                project(f"proj{n}", both(unit, 256), (n % 2) * P, h_both, KT, None if n else "yT")
            for u in range(2):
                split(M + 6 + u)
                w = both(M + 6 + u, 256)
                for t in range(TT):
                    b = start(f"v{u}_{t}")
                    for k in range(KT):
                        last = product(b[:, 0:256], [v[:, k, t * P:(t + 1) * P] for v in h_both],
                                       [v[:, k, :] for v in w], k == 0, k == KT - 1)
                    finish(f"v{u}_{t}", last)
            for n in range(4, 12):
                was_read(pe, f"proj{n}")
            for u in range(2):
                for t in range(TT):
                    was_read(pe, f"v{u}_{t}")

            def head_scores(h):
                r = 64 * (h % 2)
                for q in range(TT):
                    b = start(f"score{h}_{q}")
                    nk = (q + 1) * P
                    finish(f"score{h}_{q}", pe.matmul(b[:, 0:nk], qT[r:r + 64, h // 2, q * P:(q + 1) * P],
                                                      kT[r:r + 64, h // 2, 0:nk], start=True, stop=True))

            def head_values(h):
                pe.wait_ge(prob_ready, h + 1)
                for piece, kts in enumerate(((0,), (1,), (2, 3))):
                    b = start(f"probT{h}_{piece}")
                    c = 0
                    for kt in kts:
                        for q in range(kt, TT):
                            last = pe.transpose(b[:, c:c + P], att[:, q, kt * P:(kt + 1) * P], ident)
                            c += P
                    finish(f"probT{h}_{piece}", last)
                r = 64 * (h % 2)
                b = start(f"pv{h}")
                for piece in range(3):
                    was_read(pe, f"probT{h}_{piece}")
                for q in range(TT):
                    for kt in range(q + 1):
                        at = ((0, 4, 7, 9)[kt] + q - kt) * P
                        last = pe.matmul(b[r:r + 64, q * P:(q + 1) * P], v_s[:, kt, h * DH:(h + 1) * DH],
                                         pT[:, at:at + P], start=(kt == 0), stop=(kt == q))
                finish(f"pv{h}", last)

            def ssm_tables(c):
                pe.wait_ge(wext_ready, c + 1)
                for i, name in enumerate(("st_re", "st_im")):
                    b = start(f"{name}_{c}")
                    for g in range(CGP):
                        last = pe.transpose(b[:, g * P:(g + 1) * P], wext[:, i, g, 0:P], ident)
                    finish(f"{name}_{c}", last)

            def ssm_lags(c):
                pe.wait_ge(bbd_ready, 1)
                pe.wait_ge(wc_ready, c + 1)
                b = start(f"lags_{c}")
                for ri in range(2):
                    for g in range(CGP):
                        last = pe.matmul(b[32 * g:32 * g + 32, 0:P], bbd[:, ri, c * CGP + g, :], wc[:, ri, g, 0:P],
                                         start=(ri == 0), stop=(ri == 1))
                finish(f"lags_{c}", last)

            def ssm_states(c):
                pe.wait_ge(u_in, 16 * T8 * (c + 1))
                was_read(pe, f"st_re_{c}")
                was_read(pe, f"st_im_{c}")
                b = start(f"state{c}")
                for ri in range(2):
                    for g in range(CG):
                        r = 64 * (g % 2)
                        at = ri * 256 + (g // 2) * NCH
                        last = pe.matmul(b[r:r + 64, at:at + NCH], st[:, ri, g // 2, r:r + 64], ubuf[:, g, :],
                                         start=True, stop=True)
                finish(f"state{c}", last)
                was_read(pe, f"lags_{c}")
                b = start(f"near{c}")
                for lag in range(T8 + 1):
                    n = (T8 - lag % T8) * NCH
                    last = pe.matmul(b[:, S - n:S], kbd[:, lag, :],
                                     uT[:, c, :, :].rearrange("p t j -> p (t j)")[:, 0:n],
                                     start=(lag == 0), stop=(lag == T8))
                finish(f"near{c}", last)

            def ssm_out(c):
                pe.wait_ge(states_ready, c + 1)
                b = start(f"ssm{c}")
                for g in range(CGP):
                    for ri in range(2):
                        last = pe.matmul(b[:, g * P:(g + 1) * P], wc[:, ri, g, SG:SG + P],
                                         hbd[:, ri, g, :, :].rearrange("p a b -> p (a b)"),
                                         start=(ri == 0), stop=(ri == 1))
                finish(f"ssm{c}", last)

            for i in range(STEPS):
                if i < HEADS:
                    head_scores(i)
                unit = M + 8 + i
                split(unit)
                for n in range(2):
                    project(f"gate{2 * i + n}", both(unit, 256), n * P, h_both, KT)
                if i % 2 == 1 and i < 2 * CT:
                    ssm_lags(i // 2)
                if i < HEADS:
                    head_values(i)
                if i % 2 == 0 and 2 <= i <= 2 * CT:
                    ssm_out(i // 2 - 1)
                if i % 2 == 0 and i < 2 * CT:
                    ssm_tables(i // 2)
                if i % 2 == 1 and i < 2 * CT:
                    ssm_states(i // 2)
            operands = {"ao": ("za", (za_hi, za_lo)), "glu": ("y", (y_hi, y_lo)), "so": ("ys", (ys_hi, ys_lo))}
            for u, (what, n0) in enumerate(last_units):
                tile, rows = operands[what]
                split(M + 20 + u)
                for n in range(n0, n0 + 4):
                    project(f"{what}{n}", both(M + 20 + u, 512), (n - n0) * P, rows, CT, None if n else tile)
            out_project("fin", (ga_hi, ga_lo), M + 26, (0, 2, 4, 6), lambda m: f"ga{m}")

        @block.scalar
        def _(act_e):
            steps = [0]

            def link(ins):
                steps[0] += 1
                ins.then_inc(act_step, 1)
                act_e.wait_ge(act_step, steps[0])

            act_e.dma_start(cst, cst_d).then_inc(cst_in, 16)
            act_e.dma_start(cols, cols_d).then_inc(cols_in, 16)

            def squares(n0, first=None):
                for t in range(TT):
                    if first is not None:
                        first(t)
                    act_e.activation(nrm[:, t, :], xres[:, t, :], ACT.Square,
                                     accum_out=stat[:, n0 + t:n0 + t + 1]).then_inc(square_sum, 1)

            def scaled(prefix, gain):
                for k in range(KT):
                    full(act_e, f"{prefix}{k}")
                    read(f"{prefix}{k}", act_e.activation(hT[:, k, :], bank[k][:, :], ACT.Copy, scale=col(gain, k)))

            def scaled_hi(prefix, gain):
                for k in range(KT):
                    full(act_e, f"{prefix}{k}")
                    tile_hi(hT_hi[:, k, :], bank[k][:, :], scale=col(gain, k))

            def copy_out(name, dst, src=None):
                full(act_e, name)
                read(name, act_e.activation(dst, bank[jobs.bank(name)][:, :] if src is None else src, ACT.Copy))

            def weights_hi(unit):
                loaded(act_e, unit)
                if unit == 9:
                    act_e.wait_ge(gt_free, CT)
                elif unit == 8:
                    act_e.wait_ge(unit_used, 6)
                elif unit in (M, M + 1):
                    s = RING2 + 1 + unit - M
                    act_e.wait_ge(unit_used, last_of[s] + 1)
                elif unit > 1 and unit not in (7, 10):
                    act_e.wait_ge(unit_used, unit - 1)
                act_e.activation(hi_of(unit), ring[slot_of(unit)], ACT.Copy).then_inc(w_hi, 1)

            def tile_hi(dst, src, **kw):
                act_e.activation(dst, src, ACT.Copy, **kw).then_inc(hi_ready, 1)

            squares(0, lambda t: act_e.wait_ge(x_in[t], 16))
            weights_hi(0)
            act_e.wait_ge(cols_in, 16)
            act_e.wait_ge(halves, 1)
            link(act_e.activation(kneg, kneg, ACT.Exp, scale=-1.0))
            act_e.activation(kneg, kneg, ACT.Ln, bias=1.0).then_inc(lam_ln, 1)
            scaled_hi("xT", "g1")
            weights_hi(1)
            act_e.wait_ge(pad_zero, 1)

            def project_out(n):
                copy_out(f"in{n}", lrux[:, n, CONV_LEFT:CONV_LEFT + S] if n < CT else mixT[:, n if n < 8 else n - 8, :])

            def gates(c):
                for d in range(2):
                    tile = gt[:, d, :, :]
                    if c:
                        act_e.wait_ge(gt_free, c)
                    for j in range(2):
                        name = f"lru{c}_{2 * d + j}"
                        full(act_e, name)
                        read(name, act_e.activation(tile[:, j, :], bank[jobs.bank(name)][:, :], ACT.Tanh, scale=0.5,
                                                    bias=hbias[:, (2 * d + j) * CT + c:(2 * d + j) * CT + c + 1]))
                    was_read(act_e, f"lru{c}_{2 * d}")
                    k = CT * d + c
                    act_e.activation(tile[:, 2, :], tile[:, 0, :], ACT.Exp, scale=kpos[:, k:k + 1], bias=kpos[:, k:k + 1])
                    act_e.activation(tile[:, 3, :], tile[:, 0, :], ACT.Tanh, scale=kneg[:, k:k + 1],
                                     bias=kneg[:, k:k + 1]).then_inc(acts_ready, 1)
                for d in range(2):
                    act_e.wait_ge(m2_ready, 2 * c + d + 1)
                    act_e.activation(gt[:, d, 3, :], gt[:, d, 3, :], ACT.Sqrt).then_inc(root_ready, 1)

            def mix_out(g):
                full(act_e, f"mix{g}")
                tile_hi(mix_hi[:, CT + g, :], bank[jobs.bank(f"mix{g}")][:, :])

            for n in range(9):
                if n % 2 == 0 and n:
                    weights_hi(n // 2 + 1)
                project_out(n)
            for c in range(CT):
                for half in range(2):
                    name = f"four{c}_{half}"
                    full(act_e, name)
                    tile_hi(four_hi[:, c, 2 * half:2 * half + 2, :].rearrange("p a b -> p (a b)"),
                            bank[jobs.bank(name)][:, :])
            weights_hi(7)
            act_e.wait_ge(k_ready, 1)
            gates(0)
            project_out(9)
            project_out(10)
            gates(1)
            project_out(11)
            weights_hi(8)
            gates(2)
            mix_out(0)
            mix_out(1)
            gates(3)
            mix_out(2)
            weights_hi(9)
            mix_out(3)
            for c in range(CT):
                act_e.wait_ge(gelu_in, c + 1)
                act_e.activation(lrux[:, c, 0:S], lrux[:, c, 0:S], ACT.Tanh, scale=GELU_C).then_inc(gelu_tanh, 1)
            weights_hi(10)
            for c in range(CT):
                act_e.wait_ge(lru_done, c + 1)
                tile_hi(mix_hi[:, c, :], mixT[:, c, :])
            weights_hi(11)
            weights_hi(12)

            for t in range(TT):
                was_read(act_e, f"out{2 * t + 1}")
                act_e.activation(nrm[:, t, :], xres[:, t, :], ACT.Square,
                                 accum_out=stat[:, 8 + t:9 + t]).then_inc(square_sum, 1)
            scaled("h2T", "g2")
            copy_out("logitT", logT, bank[jobs.bank("logitT")][:, 0:P])
            act_e.wait_ge(soft_in, 1)
            b = bank[jobs.bank("logits")]
            for t in range(TT):
                last = act_e.activation(aff[:, t, 0:NE], b[:, 32 * t:32 * t + NE], ACT.Exp, bias=stat[:, 16 + t:17 + t],
                                        accum_out=stat[:, 20 + t:21 + t])
                if t < TT - 1:
                    last.then_inc(soft_exp, 1)
            read("logits", last)
            copy_out("scoreT", score, bank[jobs.bank("scoreT")][0:NE, :])
            full(act_e, "posT")
            read("posT", act_e.activation(posT[:, :, 0:NE], bank[jobs.bank("posT")][:, 0:TT * NE].rearrange("p (t e) -> p t e", t=TT),
                                          ACT.Copy))

            with act_e.Fori(0, NE) as e:
                def filled(b, n):
                    act_e.wait_ge(bank_full[b], e * EF[b] + (moe_told[b] + n + 1))

                filled(0, 0)
                act_e.activation(xg, bank[0][:, :], ACT.Copy).then_inc(bank_read[0], 1)
                filled(7, 0)
                act_e.activation(flat(gselT), bank[7][:, :], ACT.Copy).then_inc(bank_read[7], 1)
                act_e.wait_ge(unit_used, e * E_UNITS + (B1_UNITS + 2 * KT - 1))
                for b in range(2):
                    act_e.activation(th[:, b, :], bank[1 + b][:, :], ACT.Tanh, scale=0.5).then_inc(tanh_ready, 1)
                for b in range(2):
                    filled(5 + b, 0)
                    act_e.activation(actT[:, 4 * b:4 * b + 4, :].rearrange("p a b -> p (a b)"), bank[5 + b][:, :],
                                     ACT.Copy).then_inc(bank_read[5 + b], 1)
                act_e.wait_ge(unit_used, e * E_UNITS + (B1_UNITS + E_UNITS))
                act_e.activation(eo, bank[7][:, :], ACT.Copy).then_inc(bank_read[7], 1)

            weights_hi(M)
            weights_hi(M + 1)
            for t in range(TT):
                act_e.wait_ge(bank_read[(7, 2, 4, 6)[t]], jobs.before(f"yT{(7, 2, 4, 6)[t]}"))
                act_e.activation(nrm[:, t, :], xres[:, t, :], ACT.Square,
                                 accum_out=stat[:, 24 + t:25 + t]).then_inc(square_sum, 1)
            for t in range(TT):
                act_e.wait_ge(between, t + 1)
                act_e.activation(nrm[:, t, :], xres[:, t, :], ACT.Square,
                                 accum_out=stat[:, 32 + t:33 + t]).then_inc(square_sum, 1)
            scaled_hi("yT", "gb2")
            act_e.wait_ge(prep_in, 1)
            act_e.activation(prep[:, 0, :], col("log_dt", 0, GP), ACT.Exp).then_inc(prep_exp, 1)
            act_e.wait_ge(prep_in, 2)
            act_e.activation(prep[:, 3, :], prep[:, 1, :], ACT.Exp).then_inc(prep_exp, 1)
            act_e.activation(prep[:, 4, :], prep[:, 1, :], ACT.Exp, scale=float(T8)).then_inc(prep_exp, 1)
            act_e.wait_ge(sin_arg, 1)
            act_e.activation(prep[:, 7, :], prep[:, 5, :], ACT.Sin, scale=0.5).then_inc(prep_sin, 1)
            act_e.activation(prep[:, 6, :], prep[:, 5, :], ACT.Sin).then_inc(prep_sin, 1)

            def staged(c):
                name = f"proj{c}"
                full(act_e, name)
                read(name, act_e.activation(uT[:, c, :, :],
                                            bank[jobs.bank(name)][:, :].rearrange("p (j t) -> p t j", t=T8), ACT.Copy))

            for n in range(12):
                if n % 2 == 0 and n:
                    weights_hi(M + n // 2 + 1)
                if n < 4:
                    staged(n)
                else:
                    copy_out(f"proj{n}", (qT if n < 8 else kT)[:, n % 4, :])
            for u in range(2):
                weights_hi(M + u + 7)
                for t in range(TT):
                    name = f"v{u}_{t}"
                    copy_out(name, v_s[:, t, 256 * u:256 * u + 256], bank[jobs.bank(name)][:, 0:256])

            for i in range(STEPS):
                if i < HEADS:
                    for q in range(TT):
                        nk = (q + 1) * P
                        act_e.wait_ge(max_ready, TT * i + q + 1)
                        act_e.activation(att[:, q, 0:nk], att[:, q, 0:nk], ACT.Exp, bias=stat[:, 40 + q:41 + q],
                                         accum_out=stat[:, 44 + q:45 + q]).then_inc(exp_ready, 1)
                weights_hi(M + 9 + i)
                for n in range(2):
                    name, g = f"gate{2 * i + n}", 2 * i + n
                    full(act_e, name)
                    src = bank[jobs.bank(name)][:, :]
                    if g < 2 * CT:
                        dst = (zaT if g < CT else zsT)[:, g % CT, :]
                        act_e.activation(dst, src, ACT.Tanh, scale=0.5).then_inc(th_ready, 1)
                    else:
                        j = g - 2 * CT
                        dst = (gaT if j < KT else gsT)[:, j % KT, :]
                        if j == KT:
                            full(act_e, f"ssm{CT - 1}")
                        read(name, act_e.activation(dst, src, ACT.Tanh, scale=0.5, bias=hbias[:, 24 + j:25 + j]))
                if i < HEADS:
                    for b in range(3):
                        w = (4, 3, 3)[b] * P
                        name = f"probT{i}_{b}"
                        copy_out(name, pT[:, (0, 4, 7)[b] * P:(0, 4, 7)[b] * P + w], bank[jobs.bank(name)][:, 0:w])
                if i % 2 == 0 and i < 2 * CT:
                    for ri, name in enumerate(("st_re", "st_im")):
                        copy_out(f"{name}_{i // 2}", flat(st[:, ri, :, :]))
                if i % 2 == 0 and 2 <= i <= 2 * CT:
                    c = i // 2 - 1
                    if c:
                        act_e.wait_ge(y_out, 16 * T8 * c)
                    copy_out(f"ssm{c}", flat(ybuf))
                if i % 2 == 1 and i < 2 * CT:
                    copy_out(f"near{i // 2}", uT[:, i // 2, :, :].rearrange("p t j -> p (t j)"))
                if i == HEADS:
                    act_e.wait_ge(states_ready, CT)
                    for c in range(CT):
                        was_read(act_e, f"pv{2 * c + 1}")
                        tile_hi(za_hi[:, c, :], zaT[:, c, :])
                if i in (GELU_STEP, GELU_STEP + 1):
                    cs = range(2 * (i - GELU_STEP), 2 * (i - GELU_STEP) + 2)
                    for c in cs:
                        act_e.wait_ge(ygelu_in, c + 1)
                        act_e.activation(tmp[:, c % 2, :], tmp[:, c % 2, :], ACT.Tanh, scale=GELU_C).then_inc(ytanh, 1)
                    for c in cs:
                        act_e.wait_ge(y_ready, c + 1)
                        tile_hi(y_hi[:, c, :], yT[:, c, :])
            weights_hi(M + 21)
            weights_hi(M + 22)
            for n in range(CT):
                name = f"glu{n}"
                if n == 0:
                    full(act_e, f"score{HEADS - 1}_{TT - 1}")
                full(act_e, name)
                read(name, act_e.activation(ysT[:, n, :], bank[jobs.bank(name)][:, :], ACT.Tanh, scale=0.25,
                                            bias=hbias[:, 16 + CT + n:17 + CT + n]))
            weights_hi(M + 23)
            for c in range(CT):
                act_e.wait_ge(glu_ready, c + 1)
                tile_hi(ys_hi[:, c, :], ysT[:, c, :])
            for u in range(24, 27):
                weights_hi(M + u)
            for d in range(KT):
                act_e.wait_ge(merged, d + 1)
                tile_hi(ga_hi[:, d, :], gaT[:, d, :])
            for u in range(27, 30):
                weights_hi(M + u)
            for t in range(TT):
                was_read(act_e, f"fin{2 * t + 1}")
                act_e.activation(nrm[:, t, :], xres[:, t, :], ACT.Square,
                                 accum_out=stat[:, 48 + t:49 + t]).then_inc(square_sum, 1)

        @block.gpsimd
        def _(pool):
            steps = [0]

            def link(ins):
                steps[0] += 1
                ins.then_inc(pool_step, 1)
                pool.wait_ge(pool_step, steps[0])

            def roots(n0, count0):
                for t in range(TT):
                    pool.wait_ge(square_sum, count0 + t + 1)
                    c = stat[:, n0 + t:n0 + t + 1]
                    link(pool.tensor_scalar(c, c, 1.0 / D, EPS, ALU.mult, ALU.add))
                    pool.tensor_tensor(stat[:, n0 + 4 + t:n0 + 5 + t], c, stat[:, 62:63], ALU.pow).then_inc(root_mean, 1)

            pool.memset(lrux, 0.0).then_inc(pad_zero, 1)
            link(pool.memset(stat[:, 62:63], -0.5))
            roots(0, 0)
            for c in range(CT):
                was_read(pool, f"in{8 + c}")
                pool.wait_ge(conv_ready, c + 1)
                g, xg = lrux[:, c, 0:S], mixT[:, c, :]
                link(pool.tensor_tensor(g, xg, xg, ALU.mult))
                link(pool.tensor_scalar(g, g, GELU_A, 1.0, ALU.mult, ALU.add))
                pool.tensor_tensor(g, g, xg, ALU.mult).then_inc(gelu_in, 1)
            roots(8, TT)
            pool.wait_ge(unit_used, B1_UNITS + RING + EARLY)
            pool.dma_start(gfb, gf_d.partition_broadcast(P)).then_inc(gf_in, 16)
            roots(24, 2 * TT)
            pool.wait_ge(bank_full[6], moe_told[6] + NE * EF[6])
            pool.dma_start(bc.rearrange("p a g c -> p (a g c)"), bc_d).then_inc(bc_in, 16)
            roots(32, 3 * TT)
            pool.wait_ge(x_saved, 16 * TT)
            pool.wait_ge(normed, 3 * TT)
            for h in range(HEADS):
                pool.dma_start(relb[:, h, :], bass.AP(tensor=relp.tensor, offset=h * (REL + P), ap=[[1, P], [1, REL]])
                               ).then_inc(rel_in, 16)
            for c in range(CT):
                was_read(pool, f"proj{c}")
            pool.dma_start(u_dram.rearrange("(c p) t j -> p c t j", p=P), uT).then_inc(u_out, 16)
            pool.wait_ge(u_out, 16)

            def inputs(c):
                for t in range(T8):
                    pool.dma_start(ubuf[t * SG:(t + 1) * SG, :, :],
                                   u_dram[c * P:(c + 1) * P, t, :].rearrange("(g c) j -> c g j", c=SG)).then_inc(u_in, 16)

            def output_table(c):
                if c:
                    was_read(pool, f"score1_{TT - 1}")
                    scratch = flat(relb[:, 0:2, :])
                else:
                    scratch = flat(ybuf)
                cs = slice(c * CGP, (c + 1) * CGP)

                def steps_of(pw):
                    return pw[:, cs, ts].unsqueeze(3).to_broadcast([P, CGP, ts.stop - ts.start, SG])

                def chans_of(v):
                    return v[:, cs, :].unsqueeze(2).to_broadcast([P, CGP, ts.stop - ts.start, SG])

                for ts in (slice(0, T8), slice(T8, T8 + 1)):
                    wr, wi = (wc[:, k, :, ts.start * SG:ts.stop * SG].rearrange("p g (t c) -> p g t c", c=SG)
                              for k in range(2))
                    sc = scratch[:, 0:CGP * (ts.stop - ts.start) * SG].rearrange("p (g t c) -> p g t c", g=CGP, c=SG)
                    pool.tensor_tensor(wr, steps_of(pw_re), chans_of(bc[:, 2, :, :]), ALU.mult)
                    link(pool.tensor_tensor(sc, steps_of(pw_in), chans_of(bc[:, 3, :, :]), ALU.mult))
                    link(pool.tensor_tensor(wr, wr, sc, ALU.add))
                    pool.tensor_tensor(wi, steps_of(pw_in), chans_of(bc[:, 2, :, :]), ALU.mult)
                    link(pool.tensor_tensor(sc, steps_of(pw_re), chans_of(bc[:, 3, :, :]), ALU.mult))
                    last = pool.tensor_tensor(wi, wi, sc, ALU.subtract)
                    if ts.stop == T8:
                        link(last)
                last.then_inc(wc_ready, 1)

            inputs(0)
            pool.wait_ge(pw_ready, 1)
            output_table(0)
            for c in range(CT):
                if c + 1 < CT:
                    full(pool, f"state{c}")
                    inputs(c + 1)
                    full(pool, f"ssm{c}")
                    output_table(c + 1)
                was_read(pool, f"ssm{c}")
                for t in range(T8):
                    pool.dma_start(y_dram[c * P:(c + 1) * P, t, :].rearrange("(g c) j -> c g j", c=SG),
                                   ybuf[t * SG:(t + 1) * SG, :, :]).then_inc(y_out, 16)
            pool.wait_ge(y_out, 16 * T8 * CT)
            full(pool, f"score{HEADS - 1}_{TT - 1}")
            pool.dma_start(yT, y_dram.rearrange("(c p) t j -> p c (t j)", p=P)).then_inc(y_in, 16)
            full(pool, f"pv{HEADS - 1}")
            pool.dma_start(gfin, gfin_d.partition_broadcast(P)).then_inc(gfin_in, 16)
            roots(48, 4 * TT)

        @block.vector
        def _(dve):
            steps = [0]

            def link(ins):
                steps[0] += 1
                ins.then_inc(dve_step, 1)
                dve.wait_ge(dve_step, steps[0])

            def tt(out_, a, b, op):
                return dve.tensor_tensor(out_, a, b, op)

            def stt(out_, a, s, b, op0, op1):
                return dve.scalar_tensor_tensor(out_, a, s, b, op0, op1)

            def normalise(n0, count0):
                for t in range(TT):
                    dve.wait_ge(root_mean, count0 + t + 1)
                    dve.tensor_scalar(nrm[:, t, :], xres[:, t, :], stat[:, n0 + 4 + t:n0 + 5 + t], None,
                                      ALU.mult).then_inc(normed, 1)

            def weights_lo(unit):
                dve.wait_ge(w_hi, split_units.index(unit) + 1)
                tt(ring_r[slot_of(unit)], ring[slot_of(unit)], hi_of(unit), ALU.subtract).then_inc(w_lo, 1)

            def tile_lo(tile, dst, src, hi):
                high_stands(dve, tile)
                tt(dst, src, hi, ALU.subtract).then_inc(lo_ready, 1)

            def scaled_lo(prefix, gain):
                for k in range(KT):
                    if k >= 3 * KT // 4:
                        full(dve, f"{prefix}{KT - 1}")
                    high_stands(dve, f"{prefix}{k}")
                    read(f"{prefix}{k}", stt(hT_lo[:, k, :], bank[k][:, :], col(gain, k), hT_hi[:, k, :], ALU.mult,
                                             ALU.subtract))

            dve.wait_ge(cols_in, 16)
            link(dve.tensor_scalar(kneg, col("lam", 0, 2 * CT), -1.0, None, ALU.mult))
            tt(kneg, kneg, col("lam", 0, 2 * CT), ALU.max).then_inc(halves, 1)
            dve.tensor_scalar(hbias[:, 0:4 * CT], col("bias_lru", 0, 4 * CT), 0.5, None, ALU.mult)
            dve.tensor_scalar(hbias[:, 4 * CT:4 * CT + 3 * KT], col("b_glu", 0, 3 * KT), 0.5, None, ALU.mult)
            normalise(0, 0)
            weights_lo(0)
            scaled_lo("xT", "g1")
            weights_lo(1)
            dve.wait_ge(lam_ln, 1)
            link(dve.tensor_scalar(kpos, col("lam", 0, 2 * CT), 0.0, None, ALU.min))
            link(tt(kpos, kpos, kneg, ALU.subtract))
            link(dve.tensor_scalar(kpos, kpos, LRU_C / 2, None, ALU.mult))
            dve.tensor_scalar(kneg, kpos, -1.0, None, ALU.mult).then_inc(k_ready, 1)
            for c in range(CT):
                was_read(dve, f"in{c}")
                o = conv[:, c, :]
                link(dve.tensor_scalar(o, lrux[:, c, 0:S], col("conv_w", c), col("conv_b", c), ALU.mult, ALU.add))
                for k in range(1, CONV):
                    last = stt(o, lrux[:, c, k:k + S], col("conv_w", k * CT + c), o, ALU.mult, ALU.add)
                    if k < CONV - 1:
                        link(last)
                last.then_inc(conv_ready, 1)
                if c in (1, 3):
                    weights_lo(2 if c == 1 else 3)
            weights_lo(4)
            weights_lo(5)
            for c in range(CT):
                for half in range(2):
                    name = f"four{c}_{half}"
                    g = slice(2 * half, 2 * half + 2)
                    high_stands(dve, name)
                    read(name, tt(four_lo[:, c, g, :].rearrange("p a b -> p (a b)"), bank[jobs.bank(name)][:, :],
                                  four_hi[:, c, g, :].rearrange("p a b -> p (a b)"), ALU.subtract))

            def recurrences(c):
                for d in range(2):
                    dve.wait_ge(acts_ready, 2 * c + d + 1)
                    link(tt(gt[:, d, 0, :], gt[:, d, 2, :], gt[:, d, 2, :], ALU.mult))
                    stt(gt[:, d, 3, :], gt[:, d, 0, :], 1.0, gt[:, d, 3, :], ALU.add, ALU.mult).then_inc(m2_ready, 1)
                for d in range(2):
                    last = stt(gt[:, d, 1, :], gt[:, d, 1, :], 1.0, conv[:, c, :], ALU.add, ALU.mult)
                link(last)
                for d in range(2):
                    dve.wait_ge(root_ready, 2 * c + d + 1)
                    link(stt(gt[:, d, 1, :], gt[:, d, 3, :], 0.5, gt[:, d, 1, :], ALU.mult, ALU.mult))
                    a, b, h = gt[:, d, 2, :], gt[:, d, 1, :], gt[:, d, 0, :]
                    if d:
                        a, b, h = a[:, ::-1], b[:, ::-1], h[:, ::-1]
                    link(dve.tensor_tensor_scan(h, a, b, 0.0, ALU.mult, ALU.add))
                tt(conv[:, c, :], gt[:, 0, 0, :], gt[:, 1, 0, :], ALU.add).then_inc(gt_free, 1)

            def mix_low(g):
                high_stands(dve, f"mix{g}")
                read(f"mix{g}", tt(mix_lo[:, CT + g, :], bank[jobs.bank(f"mix{g}")][:, :], mix_hi[:, CT + g, :],
                                   ALU.subtract))

            weights_lo(7)
            recurrences(0)
            recurrences(1)
            weights_lo(8)
            recurrences(2)
            mix_low(0)
            mix_low(1)
            recurrences(3)
            mix_low(2)
            weights_lo(9)
            mix_low(3)
            for c in range(CT):
                dve.wait_ge(gelu_tanh, c + 1)
                dve.wait_ge(gt_free, c + 1)
                link(stt(mixT[:, c, :], lrux[:, c, 0:S], 1.0, mixT[:, c, :], ALU.add, ALU.mult))
                stt(mixT[:, c, :], mixT[:, c, :], 0.5, conv[:, c, :], ALU.mult, ALU.mult).then_inc(lru_done, 1)
            weights_lo(10)
            for c in range(CT):
                tile_lo(f"lru{c}", mix_lo[:, c, :], mixT[:, c, :], mix_hi[:, c, :])
            weights_lo(11)
            weights_lo(12)

            def residual(prefix, scale):
                for o in range(8):
                    name = f"{prefix}{o}"
                    r = xres[:, o // 2, o % 2 * 512:o % 2 * 512 + 512]
                    full(dve, name)
                    read(name, stt(r, bank[jobs.bank(name)][:, :], scale, r, ALU.mult, ALU.add))

            residual("out", 1.0)

            normalise(8, TT)
            full(dve, "logits")
            b = bank[jobs.bank("logits")]
            for t in range(TT):
                last = dve.tensor_reduce(stat[:, 16 + t:17 + t], b[:, 32 * t:32 * t + NE], AX, ALU.max, negate=True)
            last.then_inc(soft_in, 1)
            full(dve, f"mix{CT - 1}")
            dve.memset(aff[:, :, NE:NE + 1], 0.0)
            dve.memset(posT[:, :, NE:NE + 1], -1.0)
            dve.memset(ones, 1.0)
            for t in range(TT):
                if t < TT - 1:
                    dve.wait_ge(soft_exp, t + 1)
                else:
                    was_read(dve, "logits")
                last = dve.reciprocal(stat[:, 20 + t:21 + t], stat[:, 20 + t:21 + t])
            link(last)
            for t in range(TT):
                last = dve.tensor_scalar(aff[:, t, 0:NE], aff[:, t, 0:NE], stat[:, 20 + t:21 + t], None, ALU.mult)
            last.then_inc(aff_ready, 1)
            was_read(dve, "scoreT")
            for _ in range(CAP // 8):
                link(dve.max(top, score))
                link(dve.match_replace(score, top, score, -1.0))
            link(dve.tensor_scalar(taken, score, -0.5, None, ALU.is_lt))
            link(dve.tensor_tensor_scan(rank, ones, taken, 0.0, ALU.mult, ALU.add))
            link(tt(rank, rank, taken, ALU.mult))
            dve.tensor_scalar(rank, rank, -1.0, None, ALU.add).then_inc(pos_ready, 1)
            was_read(dve, "posT")

            def select(e):
                return tt(sel, posT[:, :, bass.ds(e, 1)].to_broadcast([P, TT, CAP]),
                          slotrow.unsqueeze(1).to_broadcast([P, TT, CAP]), ALU.is_equal)

            def gated(e):
                return tt(gsel, sel.unsqueeze(2).to_broadcast([P, TT, 2, CAP]),
                          aff[:, :, bass.ds(e, 1)].unsqueeze(3).to_broadcast([P, TT, 2, CAP]), ALU.mult)

            select(0).then_inc(sel_ready, 1)
            dve.wait_ge(sel_ready, 1)
            gated(0).then_inc(sel_ready, 1)

            with dve.Fori(0, NE) as e:
                def filled(b, n):
                    dve.wait_ge(bank_full[b], e * EF[b] + (moe_told[b] + n + 1))

                filled(0, 1)
                tt(xinT.rearrange("p (q j) c -> p j q c", j=4),
                   bank[0][:, :].rearrange("p (j q c) -> p j q c", j=4, q=2),
                   col("g2", 0, KT).rearrange("p (q j) -> p j q", j=4).unsqueeze(3).to_broadcast([P, 4, 2, CAP]),
                   ALU.mult).then_inc(bank_read[0], 1)
                for b in range(2):
                    dve.wait_ge(tanh_ready, 2 * e + (b + 1))
                    stt(th[:, b, :], th[:, b, :], 1.0, bank[1 + b][:, :], ALU.add, ALU.mult).then_inc(bank_read[1 + b], 1)
                dve.wait_ge(unit_used, e * E_UNITS + (B1_UNITS + 2 * KT))
                for b in range(2):
                    dve.wait_ge(bank_read[1 + b], e * EU[1 + b] + (moe_uses[1 + b] + 1))
                    stt(act[:, b, :], th[:, b, :], 0.5, bank[3 + b][:, :], ALU.mult, ALU.mult).then_inc(act_ready, 1)
                select(e + 1).then_inc(sel_ready, 1)
                filled(7, 0)
                dve.wait_ge(sel_ready, 2 * e + 3)
                gated(e + 1).then_inc(sel_ready, 1)
                for o, b in enumerate((0, 7, 1, 2, 3, 4, 5, 6)):
                    r = xres[:, o // 2, o % 2 * 512:o % 2 * 512 + 512]
                    filled(b, EF[b] - 1)
                    tt(r, r, bank[b][:, :], ALU.add).then_inc(bank_read[b], 1)

            dve.wait_ge(gf_in, 16)
            for t in range(TT):
                dve.wait_ge(root_mean, 2 * TT + t + 1)
                stt(xres[:, t, :], xres[:, t, :], stat[:, 28 + t:29 + t], gfb, ALU.mult, ALU.mult).then_inc(between, 1)
            normalise(32, 3 * TT)
            weights_lo(M)
            weights_lo(M + 1)
            scaled_lo("yT", "gb2")

            def p(n):
                return prep[:, n, :]

            def cmul(dst, a, b, s):
                tt(s[0], a[0], b[0], ALU.mult)
                tt(s[1], a[1], b[1], ALU.mult)
                tt(s[2], a[0], b[1], ALU.mult)
                link(tt(s[3], a[1], b[0], ALU.mult))
                tt(dst[0], s[0], s[1], ALU.subtract)
                link(tt(dst[1], s[2], s[3], ALU.add))

            dve.wait_ge(between, TT)
            dve.memset(flat(prep), 0.0).then_inc(prep_in, 1)
            dve.wait_ge(prep_exp, 1)
            tt(p(1), col("a_re", 0, GP), p(0), ALU.mult)
            link(tt(p(2), col("a_im", 0, GP), p(0), ALU.mult))
            link(dve.tensor_scalar(p(5), p(2), 1 / TWO_PI, ROUND, ALU.mult, ALU.add))
            dve.tensor_scalar(p(5), p(5), -ROUND, None, ALU.add).then_inc(prep_in, 1)
            dve.wait_ge(prep_in, 2)
            link(stt(p(8), p(5), -PI_HI, p(2), ALU.mult, ALU.add))
            link(stt(p(8), p(5), -PI_MID, p(8), ALU.mult, ALU.add))
            link(stt(p(5), p(5), -PI_LO, p(8), ALU.mult, ALU.add))
            dve.tensor_scalar(p(5), p(5), -3.1415925, 3.1415925, ALU.max, ALU.min).then_inc(sin_arg, 1)
            dve.wait_ge(prep_exp, 3)
            dve.wait_ge(prep_sin, 2)
            link(tt(p(9), p(7), p(7), ALU.mult))
            link(dve.tensor_scalar(p(9), p(9), -2.0, 1.0, ALU.mult, ALU.add))
            dve.memset(pw_re[:, :, 0], 1.0)
            dve.memset(pw_im[:, :, 0], 0.0)
            tt(pw_re[:, :, 1], p(3), p(9), ALU.mult)
            link(tt(pw_im[:, :, 1], p(3), p(6), ALU.mult))
            link(dve.tensor_scalar(p(10), pw_re[:, :, 1], -1.0, None, ALU.add))
            are, aim, nim = col("a_re", 0, GP), col("a_im", 0, GP), pw_im[:, :, 1]
            tt(p(11), are, are, ALU.mult)
            tt(p(12), aim, aim, ALU.mult)
            tt(p(13), p(10), are, ALU.mult)
            tt(p(14), nim, aim, ALU.mult)
            tt(p(15), nim, are, ALU.mult)
            link(tt(p(16), p(10), aim, ALU.mult))
            tt(p(11), p(11), p(12), ALU.add)
            tt(p(13), p(13), p(14), ALU.add)
            link(tt(p(15), p(15), p(16), ALU.subtract))
            link(dve.reciprocal(p(11), p(11)))
            tt(p(13), p(13), p(11), ALU.mult)
            link(tt(p(15), p(15), p(11), ALU.mult))

            weights_lo(M + 2)

            def per_chan(v):
                return v.unsqueeze(2).to_broadcast([P, GP, SG])

            dve.wait_ge(bc_in, 16)
            sc = [prot[:, i, :, 0:SG] for i in range(2)] + [prot[:, i, :, SG:2 * SG] for i in range(2)]
            cmul((bc[:, 0, :, :], bc[:, 1, :, :]), (bc[:, 0, :, :], bc[:, 1, :, :]),
                 (per_chan(p(13)), per_chan(p(15))), sc)
            link(dve.memset(bbd.rearrange("p a g c -> p (a g c)"), 0.0))
            for a in range(2):
                q = slice(64 * a, 64 * a + 64)
                for ri in range(2):
                    last = dve.tensor_copy(bbd[q, ri, :, a * SG:(a + 1) * SG], bc[q, ri, :, :])
            last.then_inc(bbd_ready, 1)
            weights_lo(M + 3)
            for k in range(2, T8 + 1):
                cmul((pw_re[:, :, k], pw_im[:, :, k]), (pw_re[:, :, k - 1], pw_im[:, :, k - 1]),
                     (pw_re[:, :, 1], pw_im[:, :, 1]), [p(17), p(18), p(19), p(20)])
            dve.tensor_scalar(pw_in, pw_im, -1.0, None, ALU.mult)
            weights_lo(M + 4)
            for _ in range(3):
                cmul((p(9), p(6)), (p(9), p(6)), (p(9), p(6)), [p(17), p(18), p(19), p(20)])
            dve.memset(rotc[:, :, 0:1], 1.0)
            link(dve.memset(rots[:, :, 0:1], 0.0))
            n = 1
            while n < NCH:
                ec = p(9).unsqueeze(2).to_broadcast([P, GP, n])
                es = p(6).unsqueeze(2).to_broadcast([P, GP, n])
                lo, hi = slice(0, n), slice(n, 2 * n)
                s0, s1 = prot[:, 0, :, 0:n], prot[:, 1, :, 0:n]
                tt(s0, rotc[:, :, lo], ec, ALU.mult)
                link(tt(s1, rots[:, :, lo], es, ALU.mult))
                link(tt(rotc[:, :, hi], s0, s1, ALU.subtract))
                tt(s0, rotc[:, :, lo], es, ALU.mult)
                link(tt(s1, rots[:, :, lo], ec, ALU.mult))
                link(tt(rots[:, :, hi], s0, s1, ALU.add))
                n *= 2
                if n == NCH // 2:
                    weights_lo(M + 5)
                if n < NCH:
                    cmul((p(9), p(6)), (p(9), p(6)), (p(9), p(6)), [p(17), p(18), p(19), p(20)])
            dve.tensor_copy(mag8, p(4))
            dve.memset(hbd.rearrange("p a b c d -> p (a b c d)"), 0.0).then_inc(pw_ready, 1)
            dve.wait_ge(pw_ready, 1)

            def input_table(c):
                cs = slice(c * CGP, (c + 1) * CGP)

                def steps_of(pw):
                    return pw[:, cs, T8 - 1::-1].unsqueeze(3).to_broadcast([P, CGP, T8, SG])

                def chans_of(v):
                    return v[:, cs, :].unsqueeze(2).to_broadcast([P, CGP, T8, SG])

                wr, wi = (wext[:, i, :, :].rearrange("p g (t c) -> p g t c", t=T8) for i in range(2))
                s = tmp[:, 1, :].rearrange("p (g t c) -> p g t c", g=CGP, t=T8)
                tt(wr, steps_of(pw_re), chans_of(bc[:, 0, :, :]), ALU.mult)
                link(tt(s, steps_of(pw_im), chans_of(bc[:, 1, :, :]), ALU.mult))
                link(tt(wr, wr, s, ALU.subtract))
                tt(wi, steps_of(pw_re), chans_of(bc[:, 1, :, :]), ALU.mult)
                link(tt(s, steps_of(pw_im), chans_of(bc[:, 0, :, :]), ALU.mult))
                tt(wi, wi, s, ALU.add).then_inc(wext_ready, 1)

            def states(c):
                cs = slice(c * CGP, (c + 1) * CGP)
                name = f"state{c}"
                full(dve, name)
                b = bank[jobs.bank(name)]
                vr, vi = (b[:, i * 256:(i + 1) * 256].rearrange("p (g j) -> p g j", g=CGP) for i in range(2))
                t0, t1, t2, t3 = (tmp[:, i // 2, i % 2 * 256:i % 2 * 256 + 256].rearrange("p (g j) -> p g j", g=CGP)
                                  for i in range(4))
                rc, rs = rotc[:, cs, :], rots[:, cs, :]
                tt(t0, vr, rc, ALU.mult)
                tt(t1, vi, rs, ALU.mult)
                tt(t2, vi, rc, ALU.mult)
                tt(t3, vr, rs, ALU.mult).then_inc(bank_read[jobs.bank(name)], 1)
                was_read(dve, name)
                tt(t0, t0, t1, ALU.add)
                link(tt(t2, t2, t3, ALU.subtract))
                for g in range(CGP):
                    dc = mag8[:, c * CGP + g:c * CGP + g + 1].to_broadcast([P, NCH])
                    dve.tensor_tensor_scan(t1[:, g, :], dc, t0[:, g, :], 0.0, ALU.mult, ALU.add)
                    last = dve.tensor_tensor_scan(t3[:, g, :], dc, t2[:, g, :], 0.0, ALU.mult, ALU.add)
                link(last)
                tt(t0, t1, rc, ALU.mult)
                link(tt(t2, t3, rs, ALU.mult))
                for a in range(2):
                    q = slice(64 * a, 64 * a + 64)
                    last = tt(hbd[q, 0, :, a, 1:NCH], t0[q, :, 0:NCH - 1], t2[q, :, 0:NCH - 1], ALU.subtract)
                link(last)
                tt(t0, t1, rs, ALU.mult)
                link(tt(t2, t3, rc, ALU.mult))
                for a in range(2):
                    q = slice(64 * a, 64 * a + 64)
                    last = tt(hbd[q, 1, :, a, 1:NCH], t0[q, :, 0:NCH - 1], t2[q, :, 0:NCH - 1], ALU.add)
                last.then_inc(states_ready, 1)
                dve.wait_ge(states_ready, c + 1)

            weights_lo(M + 6)
            input_table(0)
            weights_lo(M + 7)
            weights_lo(M + 8)
            dve.wait_ge(rel_in, 16 * HEADS)
            link(dve.memset(relb[0:CHUNK, :, 0:CHUNK], -1e30))

            def gelu_end(c):
                dve.wait_ge(ytanh, c + 1)
                stt(yT[:, c, :], tmp[:, c % 2, :], 1.0, yT[:, c, :], ALU.add, ALU.mult).then_inc(y_ready, 1)
                dve.wait_ge(y_ready, c + 1)

            for i in range(STEPS):
                if i < HEADS:
                    if i:
                        full(dve, f"probT{i - 1}_2")
                    for q in range(TT):
                        name, nk = f"score{i}_{q}", (q + 1) * P
                        full(dve, name)
                        b = bank[jobs.bank(name)]
                        near = min(nk, REL)
                        if nk > near:
                            dve.tensor_scalar(att[:, q, 0:nk - near], b[:, 0:nk - near], SCALE, col("rb_far", i),
                                              ALU.mult, ALU.add)
                        read(name, stt(att[:, q, nk - near:nk], b[:, nk - near:nk], SCALE, relb[:, i, 0:near][:, ::-1],
                                       ALU.mult, ALU.add))
                        was_read(dve, name)
                        dve.tensor_reduce(stat[:, 40 + q:41 + q], att[:, q, 0:nk], AX, ALU.max,
                                          negate=True).then_inc(max_ready, 1)
                    for q in range(TT):
                        nk = (q + 1) * P
                        dve.wait_ge(exp_ready, TT * i + q + 1)
                        link(dve.reciprocal(stat[:, 56 + q:57 + q], stat[:, 44 + q:45 + q]))
                        last = dve.tensor_scalar(att[:, q, 0:nk], att[:, q, 0:nk], stat[:, 56 + q:57 + q], None, ALU.mult)
                    last.then_inc(prob_ready, 1)
                weights_lo(M + 9 + i)
                if i == HEADS:
                    for c in range(CT):
                        tile_lo(f"za{c}", za_lo[:, c, :], zaT[:, c, :], za_hi[:, c, :])
                for n in range(2):
                    g = 2 * i + n
                    if g < 2 * CT:
                        name = f"gate{g}"
                        dst = (zaT if g < CT else zsT)[:, g % CT, :]
                        dve.wait_ge(th_ready, g + 1)
                        read(name, stt(dst, dst, 1.0, bank[jobs.bank(name)][:, :], ALU.add, ALU.mult))
                if i % 2 == 1 and i < 2 * CT:
                    c, name = i // 2, f"lags_{i // 2}"
                    full(dve, name)
                    if c:
                        full(dve, f"near{c - 1}")
                    dve.tensor_scalar(kbd[:, T8, :], ident, col("skip", c), None, ALU.mult)
                    read(name, tt(kbd[:, 0:T8, :].rearrange("p d (g c) -> p d g c", g=CG),
                                  bank[jobs.bank(name)][:, 0:P].rearrange("p (d c) -> p d c", d=T8).unsqueeze(2)
                                  .to_broadcast([P, T8, CG, SG]),
                                  group_of.unsqueeze(1).unsqueeze(3).to_broadcast([P, T8, CG, SG]), ALU.mult))
                if i < HEADS:
                    name, r = f"pv{i}", slice(64 * (i % 2), 64 * (i % 2) + 64)
                    full(dve, name)
                    was_read(dve, f"gate{i // 2}")
                    z = zaT[r, i // 2, :]
                    read(name, stt(z, bank[jobs.bank(name)][r, :], 0.5, z, ALU.mult, ALU.mult))
                if i in (GELU_STEP, GELU_STEP + 1):
                    cs = range(2 * (i - GELU_STEP), 2 * (i - GELU_STEP) + 2)
                    for c in cs:
                        y, near, s = yT[:, c, :], uT[:, c, :, :].rearrange("p t j -> p (t j)"), tmp[:, c % 2, :]
                        dve.wait_ge(y_in, 16)
                        was_read(dve, f"near{c}")
                        link(tt(y, y, near, ALU.add))
                        link(tt(s, y, y, ALU.mult))
                        link(dve.tensor_scalar(s, s, GELU_A, 1.0, ALU.mult, ALU.add))
                        tt(s, s, y, ALU.mult).then_inc(ygelu_in, 1)
                    for c in cs:
                        gelu_end(c)
                    for c in cs:
                        tile_lo(f"y{c}", y_lo[:, c, :], yT[:, c, :], y_hi[:, c, :])
                if i % 2 == 1 and i < 2 * CT:
                    states(i // 2)
                    if i // 2 + 1 < CT:
                        input_table(i // 2 + 1)
            def attention_out(d):
                name = f"ao{d}"
                full(dve, name)
                was_read(dve, f"gate{2 * CT + d}")
                read(name, stt(gaT[:, d, :], gaT[:, d, :], 1.0, bank[jobs.bank(name)][:, :], ALU.add, ALU.mult))

            weights_lo(M + 21)
            for d in range(4):
                attention_out(d)
            weights_lo(M + 22)
            weights_lo(M + 23)
            for c in range(CT):
                name = f"glu{CT + c}"
                full(dve, name)
                read(name, dve.tensor_scalar(tmp[:, 0, :], bank[jobs.bank(name)][:, :], 0.5, col("b_glu", c),
                                             ALU.mult, ALU.add))
                was_read(dve, name)
                was_read(dve, f"glu{c}")
                link(stt(tmp[:, 1, :], ysT[:, c, :], 1.0, tmp[:, 0, :], ALU.add, ALU.mult))
                stt(ysT[:, c, :].rearrange("p (j t) -> p t j", t=T8), tmp[:, 1, :].rearrange("p (t j) -> p t j", t=T8),
                    0.25, zsT[:, c, :].rearrange("p (j t) -> p t j", t=T8), ALU.mult, ALU.mult).then_inc(glu_ready, 1)
                dve.wait_ge(glu_ready, c + 1)
            for c in range(CT):
                tile_lo(f"ys{c}", ys_lo[:, c, :], ysT[:, c, :], ys_hi[:, c, :])
            weights_lo(M + 24)
            for d in range(4, KT):
                attention_out(d)
            weights_lo(M + 25)
            for d in range(KT):
                if d == 4:
                    weights_lo(M + 26)
                name = f"so{d}"
                full(dve, name)
                was_read(dve, f"gate{2 * CT + KT + d}")
                read(name, stt(gsT[:, d, :], gsT[:, d, :], 1.0, bank[jobs.bank(name)][:, :], ALU.add, ALU.mult))
                if d:
                    tile_lo(f"ga{d - 1}", ga_lo[:, d - 1, :], gaT[:, d - 1, :], ga_hi[:, d - 1, :])
                was_read(dve, name)
                was_read(dve, f"ao{d}")
                tt(gaT[:, d, :], gaT[:, d, :], gsT[:, d, :], ALU.add).then_inc(merged, 1)
            tile_lo(f"ga{KT - 1}", ga_lo[:, KT - 1, :], gaT[:, KT - 1, :], ga_hi[:, KT - 1, :])
            for u in range(27, 30):
                weights_lo(M + u)
            dve.wait_ge(x_back, 16)
            residual("fin", 0.5)
            dve.wait_ge(gfin_in, 16)
            for t in range(TT):
                dve.wait_ge(root_mean, 4 * TT + t + 1)
                stt(xres[:, t, :], xres[:, t, :], stat[:, 52 + t:53 + t], gfin, ALU.mult, ALU.mult).then_inc(final_ready, 1)


def lay_out(i):
    f = {k: np.ascontiguousarray(np.asarray(v)) for k, v in i.items()}

    def tiles(v):
        return v.reshape(-1, P).T

    def pairs(v):
        return v.reshape(GP, 2, NS, -1).transpose(1, 2, 0, 3).reshape(P, GP, -1)

    bd = np.zeros((P, 4, CT, P), np.float32)
    for j, name in enumerate(("lru_wa_f", "lru_wx_f", "lru_wa_b", "lru_wx_b")):
        w = f[name].reshape(CT, 2, 64, 64)
        for a in range(2):
            bd[64 * a:64 * a + 64, j, :, 64 * a:64 * a + 64] = w[:, a].transpose(1, 0, 2)
    parts = {
        "g1": tiles(f["norm1_g"]), "g2": tiles(f["norm2_g"]), "gb2": tiles(f["norm_gain_2"][0]),
        "conv_w": tiles(f["conv_w"].reshape(-1)), "conv_b": tiles(f["conv_b"]),
        "bias_lru": np.concatenate([tiles(f[n]) for n in ("lru_ba_f", "lru_bx_f", "lru_ba_b", "lru_bx_b")], 1),
        "lam": np.concatenate([tiles(f["lru_lam_f"]), tiles(f["lru_lam_b"])], 1),
        "b_glu": tiles(f["b_glu_2"][0]), "gate_b": tiles(f["gate_bias_2"][0]),
        "a_re": pairs(f["ssm_a_re_2"][0])[:, :, 0], "a_im": pairs(f["ssm_a_im_2"][0])[:, :, 0],
        "log_dt": pairs(np.repeat(f["ssm_log_dt_2"][0][:, None], NS, 1))[:, :, 0],
        "skip": tiles(f["ssm_d_2"][0]),
        "rb_far": np.repeat(f["rel_bias_2"][0][:, NREL - 1][None], P, 0),
        "w_router": np.pad(f["w_router"].reshape(KT, P, NE).transpose(1, 0, 2), ((0, 0), (0, 0), (0, NE))).reshape(P, -1),
    }
    cols = np.concatenate([parts[n] for n, _ in COLS], 1)
    c_re, c_im = (f[n][0].transpose(0, 2, 1) for n in ("ssm_c_re_2", "ssm_c_im_2"))
    bc = np.stack([pairs(f["ssm_b_re_2"][0]), pairs(f["ssm_b_im_2"][0]), pairs(c_re), pairs(c_im)], 1)
    n = np.arange(P)
    ang = 2 * np.pi * (np.outer(n, n) % P) / P
    cst = np.concatenate([np.eye(P), np.cos(ang), np.sin(ang), np.tile(np.arange(CAP), (P, 1)),
                          np.arange(P)[:, None] // SG == np.arange(CG)[None]], 1).astype(np.float32)
    n = np.arange(S)
    ang = 2 * np.pi * (np.outer(n, n) % S) / S
    dft_s = (np.stack([np.cos(ang), -np.sin(ang)]) / np.sqrt(S * P)).astype(np.float32)
    return {
        "x": f["x"][0], "cols": cols, "cst": cst, "wbd": bd.reshape(P, -1), "w_in": f["w_in"], "dft_s": dft_s,
        "w_out": f["w_out"], "w_gate": f["w_gate"], "w_up": f["w_up"], "w_down": f["w_down"],
        "gf": f["normf_g"], "w_in2": f["w_in_2"][0],
        "relp": np.pad(f["rel_bias_2"][0], ((0, 0), (CHUNK, REL + P - CHUNK - NREL)), mode="edge"),
        "bc": bc.reshape(P, -1), "w_glu": f["w_glu_2"][0], "w_ao": f["w_attn_out_2"][0],
        "w_so": f["w_ssm_out_2"][0], "w_out2": f["w_out_2"][0], "gfin": f["final_gain_2"],
    }


def kernel(**inputs):
    import concourse.bacc as bacc
    from concourse.bass_utils import run_bass_kernel_spmd

    nc = bacc.Bacc("TRN2", target_bir_lowering=False, num_devices=1)
    arrays, args = {}, []
    for name, a in lay_out(inputs).items():
        a = np.ascontiguousarray(a)
        arrays[f"in_{name}"] = a
        args.append(nc.dram_tensor(f"in_{name}", a.shape, mybir.dt.from_np(a.dtype), kind="ExternalInput").ap())
    args.append(nc.dram_tensor("out", (S, D), f32, kind="ExternalOutput").ap())
    args.append(nc.dram_tensor("u_scratch", (LRU, T8, NCH), f32, kind="Internal").ap())
    args.append(nc.dram_tensor("y_scratch", (LRU, T8, NCH), f32, kind="Internal").ap())
    args.append(nc.dram_tensor("x_scratch", (S, D), f32, kind="Internal").ap())
    build(nc, *args)
    r = run_bass_kernel_spmd(nc, [arrays], core_ids=[0])
    return r.results[0]["out"].reshape(1, S, D)
```
